# Optimizing a Trainium2 kernel written in Bass

```python
import math
import jax, jax.numpy as jnp
from jax import lax
import numpy as np

D_MODEL = 1024
BATCH = 1
SEQ = 128
DEPTH = 2
DEC_BATCH = 1
DEC_SEQ = 512
PAST_LEN = 256

GRID_W = 64
POS_BASE = 10000.0
HEAD_DIM = 64
MIX_W = D_MODEL
GLA_HEADS = D_MODEL // 4 // HEAD_DIM
MLSTM_HEADS = D_MODEL // 4 // HEAD_DIM
SSD_HEADS = D_MODEL // 2 // HEAD_DIM
N_MIX_HEADS = GLA_HEADS + MLSTM_HEADS + SSD_HEADS
GLA_W = GLA_HEADS * HEAD_DIM
MLSTM_W = MLSTM_HEADS * HEAD_DIM
SSD_W = SSD_HEADS * HEAD_DIM
GLA_DK = HEAD_DIM // 2
GLA_QK = GLA_HEADS * GLA_DK
GLA_RANK = 16
GLA_GATE_TEMP = 16.0
SSD_GROUPS = 2
SSD_HPG = SSD_HEADS // SSD_GROUPS
SSD_N = 64
SSD_GN = SSD_GROUPS * SSD_N
CONV_K = 3
CONV_CH = SSD_W + 2 * SSD_GN
CHUNK = 64
PEER_HEADS = 8
PEER_DK = 128
N_KEYS = 128
N_EXPERTS = N_KEYS * N_KEYS
PEER_TOPK = 16
PEER_BLOCK = 128
DEEPNORM_ALPHA = (2 * DEPTH) ** 0.25
DEEPNORM_BETA = (8 * DEPTH) ** -0.25
IN_SPLITS = (GLA_QK, GLA_QK, GLA_W, GLA_W, 2 * GLA_RANK,
             MLSTM_W, MLSTM_W, MLSTM_W, MLSTM_W, 2 * MLSTM_HEADS, 2 * MLSTM_HEADS,
             SSD_W, SSD_W, SSD_GN, SSD_GN, 2 * SSD_HEADS)
IN_W = (2 * GLA_QK + 2 * GLA_W + 2 * GLA_RANK + 4 * MLSTM_W + 4 * MLSTM_HEADS
        + 2 * SSD_W + 2 * SSD_GN + 2 * SSD_HEADS)

kernel_name = "hybrid_gla_mlstm_ssd_peer_flow_step"

def _ln(x, eps=1e-6):
    xf = x.astype(jnp.float32)
    mu = jnp.mean(xf, axis=-1, keepdims=True)
    var = jnp.mean(jnp.square(xf - mu), axis=-1, keepdims=True)
    return ((xf - mu) * lax.rsqrt(var + eps)).astype(x.dtype)

def _rms_norm(x, eps=1e-6):
    xf = x.astype(jnp.float32)
    return (xf * lax.rsqrt(jnp.mean(jnp.square(xf), axis=-1, keepdims=True) + eps)).astype(x.dtype)

def _flip(t):
    return jnp.flip(t, axis=1)

def _chunks(t):
    b, l = t.shape[:2]
    return jnp.moveaxis(t.reshape((b, l // CHUNK, CHUNK) + t.shape[2:]), 1, 0)

def _unchunk(t):
    n, b, c = t.shape[:3]
    return jnp.moveaxis(t, 0, 1).reshape((b, n * c) + t.shape[3:])

def _lower_mask():
    return jnp.tril(jnp.ones((CHUNK, CHUNK), dtype=bool))

def _grid_pos_embed(n_tokens, dim):
    rows = n_tokens // GRID_W
    r = jnp.repeat(jnp.arange(rows, dtype=jnp.float32), GRID_W)
    col = jnp.tile(jnp.arange(GRID_W, dtype=jnp.float32), rows)
    quarter = dim // 4
    inv_freq = 1.0 / (POS_BASE ** (jnp.arange(quarter, dtype=jnp.float32) / quarter))
    ang_r = r[:, None] * inv_freq
    ang_c = col[:, None] * inv_freq
    return jnp.concatenate([jnp.sin(ang_r), jnp.cos(ang_r), jnp.sin(ang_c), jnp.cos(ang_c)], axis=-1)

def _centered_dwconv(x, w, b):
    y = lax.conv_general_dilated(x, w[:, None, :], window_strides=(1,),
                                 padding=[(CONV_K // 2, CONV_K // 2)],
                                 dimension_numbers=('NWC', 'WIO', 'NWC'),
                                 feature_group_count=x.shape[-1])
    return y + b

def _gla_scan(q, k, v, log_a, s0):
    out_dtype = v.dtype
    mask = _lower_mask()[None, :, :, None, None]

    def step(s, inp):
        qc, kc, vc, lac = inp
        b = jnp.cumsum(lac, axis=1)
        rel = jnp.exp(jnp.where(mask, b[:, :, None] - b[:, None], -jnp.inf))
        att = jnp.einsum('bthd,bshd,btshd->bhts', qc, kc, rel)
        o = (jnp.einsum('bhts,bshv->bthv', att, vc)
             + jnp.einsum('bthd,bhdv->bthv', qc * jnp.exp(b), s))
        b_last = b[:, -1]
        s = (jnp.exp(b_last)[..., None] * s
             + jnp.einsum('bshd,bshv->bhdv', kc * jnp.exp(b_last[:, None] - b), vc))
        return s, o

    xs = tuple(_chunks(t.astype(jnp.float32)) for t in (q, k, v, log_a))
    s_fin, o = lax.scan(step, s0.astype(jnp.float32), xs)
    return _unchunk(o).astype(out_dtype), s_fin.astype(out_dtype)

def _mlstm_scan(q, k, v, i_pre, log_f, c0, n0, m0):
    out_dtype = v.dtype
    mask = _lower_mask()[None, :, :, None]

    def step(carry, inp):
        c, n, m = carry
        qc, kc, vc, ic, fc = inp
        fcum = jnp.cumsum(fc, axis=1)
        dmat = jnp.where(mask, fcum[:, :, None] - fcum[:, None] + ic[:, None], -jnp.inf)
        m_t = jnp.maximum(fcum + m[:, None], jnp.max(dmat, axis=2))
        w_state = jnp.exp(fcum + m[:, None] - m_t)
        w = jnp.exp(dmat - m_t[:, :, None]) * jnp.einsum('bthd,bshd->btsh', qc, kc)
        num = (w_state[..., None] * jnp.einsum('bhvd,bthd->bthv', c, qc)
               + jnp.einsum('btsh,bshv->bthv', w, vc))
        den = w_state * jnp.einsum('bhd,bthd->bth', n, qc) + jnp.sum(w, axis=2)
        h = num / jnp.maximum(jnp.abs(den), jnp.exp(-m_t))[..., None]
        f_tot = fcum[:, -1]
        d_last = f_tot[:, None] - fcum + ic
        m_new = jnp.maximum(f_tot + m, jnp.max(d_last, axis=1))
        w_s = jnp.exp(d_last - m_new[:, None])
        keep = jnp.exp(f_tot + m - m_new)
        c = keep[..., None, None] * c + jnp.einsum('bsh,bshv,bshd->bhvd', w_s, vc, kc)
        n = keep[..., None] * n + jnp.einsum('bsh,bshd->bhd', w_s, kc)
        return (c, n, m_new), h

    xs = tuple(_chunks(t.astype(jnp.float32)) for t in (q, k, v, i_pre, log_f))
    init = (c0.astype(jnp.float32), n0.astype(jnp.float32), m0.astype(jnp.float32))
    (c_f, n_f, m_f), h = lax.scan(step, init, xs)
    return (_unchunk(h).astype(out_dtype), c_f.astype(out_dtype),
            n_f.astype(out_dtype), m_f.astype(out_dtype))

def _ssd_scan(x, dt, a, bm, cm, s0):
    out_dtype = x.dtype
    b_, l = x.shape[:2]
    f32 = jnp.float32
    xg = x.astype(f32).reshape(b_, l, SSD_GROUPS, SSD_HPG, HEAD_DIM)
    dtg = dt.astype(f32).reshape(b_, l, SSD_GROUPS, SSD_HPG)
    lag = dtg * a.astype(f32).reshape(SSD_GROUPS, SSD_HPG)
    mask = _lower_mask()[None, :, :, None, None]

    def step(s, inp):
        xc, dtc, lac, bc, cc = inp
        acum = jnp.cumsum(lac, axis=1)
        decay = jnp.exp(jnp.where(mask, acum[:, :, None] - acum[:, None], -jnp.inf))
        cb = jnp.einsum('btgn,bsgn->btsg', cc, bc)
        y = (jnp.einsum('btsg,btsgr,bsgrp->btgrp', cb, decay, xc * dtc[..., None])
             + jnp.exp(acum)[..., None] * jnp.einsum('bgrpn,btgn->btgrp', s, cc))
        a_last = acum[:, -1]
        s = (jnp.exp(a_last)[..., None, None] * s
             + jnp.einsum('bsgr,bsgrp,bsgn->bgrpn', jnp.exp(a_last[:, None] - acum) * dtc, xc, bc))
        return s, y

    xs = (_chunks(xg), _chunks(dtg), _chunks(lag), _chunks(bm.astype(f32)), _chunks(cm.astype(f32)))
    s_init = s0.astype(f32).reshape(b_, SSD_GROUPS, SSD_HPG, HEAD_DIM, SSD_N)
    s_fin, y = lax.scan(step, s_init, xs)
    y = _unchunk(y).reshape(b_, l, SSD_HEADS, HEAD_DIM)
    return y.astype(out_dtype), s_fin.reshape(b_, SSD_HEADS, HEAD_DIM, SSD_N).astype(out_dtype)

def _mixer(u, st, w_in, conv_w, conv_b, gla_wa2, gla_ba, mlstm_bi, mlstm_bf,
           ssd_dt_bias, ssd_a_log, ssd_d, gnorm_w, w_out):
    st_gla, st_mc, st_mn, st_mm, st_ssd = st
    b_, l, _ = u.shape
    offs = [sum(IN_SPLITS[:i]) for i in range(1, len(IN_SPLITS))]
    (gq, gk, gv, gg, ga, mq, mk, mv, mo, mi, mfg,
     sx, sz, sb, sc, sdt) = jnp.split(u @ w_in, offs, axis=-1)

    q = gq.reshape(b_, l, GLA_HEADS, GLA_DK) * GLA_DK ** -0.5
    k = gk.reshape(b_, l, GLA_HEADS, GLA_DK)
    v = gv.reshape(b_, l, GLA_HEADS, HEAD_DIM)
    la = jax.nn.log_sigmoid(jnp.einsum('bljr,jrk->bljk', ga.reshape(b_, l, 2, GLA_RANK), gla_wa2)
                            + gla_ba) / GLA_GATE_TEMP
    la = la.reshape(b_, l, 2, GLA_HEADS, GLA_DK)
    o_f, s_f = _gla_scan(q, k, v, la[:, :, 0], st_gla[:, 0])
    o_b, s_b = _gla_scan(_flip(q), _flip(k), _flip(v), _flip(la[:, :, 1]), st_gla[:, 1])
    o_gla = (o_f + _flip(o_b)) * jax.nn.silu(gg).reshape(b_, l, GLA_HEADS, HEAD_DIM)
    new_gla = jnp.stack([s_f, s_b], axis=1)

    q = mq.reshape(b_, l, MLSTM_HEADS, HEAD_DIM)
    k = mk.reshape(b_, l, MLSTM_HEADS, HEAD_DIM) * HEAD_DIM ** -0.5
    v = mv.reshape(b_, l, MLSTM_HEADS, HEAD_DIM)
    ig = mi.reshape(b_, l, 2, MLSTM_HEADS) + mlstm_bi
    lf = jax.nn.log_sigmoid(mfg.reshape(b_, l, 2, MLSTM_HEADS) + mlstm_bf)
    h_f, c_f, n_f, m_f = _mlstm_scan(q, k, v, ig[:, :, 0], lf[:, :, 0],
                                     st_mc[:, 0], st_mn[:, 0], st_mm[:, 0])
    h_b, c_b, n_b, m_b = _mlstm_scan(_flip(q), _flip(k), _flip(v), _flip(ig[:, :, 1]), _flip(lf[:, :, 1]),
                                     st_mc[:, 1], st_mn[:, 1], st_mm[:, 1])
    o_ml = jax.nn.sigmoid(mo).reshape(b_, l, MLSTM_HEADS, HEAD_DIM) * (h_f + _flip(h_b))
    new_mc = jnp.stack([c_f, c_b], axis=1)
    new_mn = jnp.stack([n_f, n_b], axis=1)
    new_mm = jnp.stack([m_f, m_b], axis=1)

    xbc = jax.nn.silu(_centered_dwconv(jnp.concatenate([sx, sb, sc], axis=-1), conv_w, conv_b))
    sx, sb, sc = jnp.split(xbc, [SSD_W, SSD_W + SSD_GN], axis=-1)
    x = sx.reshape(b_, l, SSD_HEADS, HEAD_DIM)
    bm = sb.reshape(b_, l, SSD_GROUPS, SSD_N)
    cm = sc.reshape(b_, l, SSD_GROUPS, SSD_N)
    dt = jax.nn.softplus(sdt.reshape(b_, l, 2, SSD_HEADS) + ssd_dt_bias)
    a = -jnp.exp(ssd_a_log)
    y_f, z_f = _ssd_scan(x, dt[:, :, 0], a[0], bm, cm, st_ssd[:, 0])
    y_b, z_b = _ssd_scan(_flip(x), _flip(dt[:, :, 1]), a[1], _flip(bm), _flip(cm), st_ssd[:, 1])
    y_ssd = (y_f + _flip(y_b) + ssd_d[:, None] * x) * jax.nn.silu(sz).reshape(b_, l, SSD_HEADS, HEAD_DIM)
    new_ssd = jnp.stack([z_f, z_b], axis=1)

    heads = jnp.concatenate([o_gla, o_ml, y_ssd], axis=2)
    heads = _rms_norm(heads) * gnorm_w.reshape(N_MIX_HEADS, HEAD_DIM)
    out = heads.reshape(b_, l, MIX_W) @ w_out
    return out, (new_gla, new_mc, new_mn, new_mm, new_ssd)

def _peer(u, wq, keys, pu, pv):
    b_, l, d = u.shape
    t = b_ * l
    xt = u.reshape(t, d)
    q = (xt @ wq).reshape(t, PEER_HEADS, 2, PEER_DK // 2)
    s = jnp.einsum('thpk,pnk->thpn', q, keys).astype(jnp.float32)
    top_s, top_i = lax.top_k(s, PEER_TOPK)
    cand_s = (top_s[:, :, 0, :, None] + top_s[:, :, 1, None, :]).reshape(t, PEER_HEADS, PEER_TOPK * PEER_TOPK)
    cand_i = (top_i[:, :, 0, :, None] * N_KEYS + top_i[:, :, 1, None, :]).reshape(t, PEER_HEADS, PEER_TOPK * PEER_TOPK)
    best_s, best_j = lax.top_k(cand_s, PEER_TOPK)
    idx = jnp.take_along_axis(cand_i, best_j, axis=-1)
    g = jax.nn.softmax(best_s, axis=-1).astype(u.dtype)
    nblk = t // PEER_BLOCK

    def block(args):
        xb, ib, gb = args
        act = jax.nn.gelu(jnp.einsum('thkd,td->thk', jnp.take(pu, ib, axis=0), xb), approximate=False) * gb
        return jnp.einsum('thk,thkd->td', act, jnp.take(pv, ib, axis=0))

    out = lax.map(block, (xt.reshape(nblk, PEER_BLOCK, d),
                          idx.reshape(nblk, PEER_BLOCK, PEER_HEADS, PEER_TOPK),
                          g.reshape(nblk, PEER_BLOCK, PEER_HEADS, PEER_TOPK)))
    return out.reshape(b_, l, d)

def _layer(x, cond, st, w_ada, b_ada, w_in, conv_w, conv_b, gla_wa2, gla_ba, mlstm_bi, mlstm_bf,
           ssd_dt_bias, ssd_a_log, ssd_d, gnorm_w, w_out, ln1_w, ln1_b,
           peer_wq, peer_keys, peer_u, peer_v, ln2_w, ln2_b):
    mod = jax.nn.silu(cond) @ w_ada + b_ada
    sh1, sc1, g1, sh2, sc2, g2 = jnp.split(mod[:, None, :], 6, axis=-1)
    u = _ln(x) * (1 + sc1) + sh1
    mix, new_st = _mixer(u, st, w_in, conv_w, conv_b, gla_wa2, gla_ba, mlstm_bi, mlstm_bf,
                         ssd_dt_bias, ssd_a_log, ssd_d, gnorm_w, w_out)
    x = _ln(DEEPNORM_ALPHA * x + g1 * mix) * ln1_w + ln1_b
    u = _ln(x) * (1 + sc2) + sh2
    x = _ln(DEEPNORM_ALPHA * x + g2 * _peer(u, peer_wq, peer_keys, peer_u, peer_v)) * ln2_w + ln2_b
    return x, new_st

def setup_inputs(seed: int = 0) -> dict:
    key = jax.random.key(seed)
    ks = jax.random.split(key, 32)
    D = D_MODEL
    f32 = jnp.float32

    def nrm(i, shape):
        return jax.random.normal(ks[i], shape, f32)

    dt0 = jnp.exp(jax.random.uniform(ks[18], (DEPTH, 2, SSD_HEADS), f32,
                                     minval=math.log(1e-3), maxval=math.log(1e-1)))
    return {
        'x_prompt': nrm(0, (BATCH, SEQ, D)),
        'x_sample': nrm(1, (DEC_BATCH, DEC_SEQ, D)),
        'c': nrm(2, (DEC_BATCH, D)),
        'state_gla': 0.5 * nrm(3, (DEC_BATCH, DEPTH, 2, GLA_HEADS, GLA_DK, HEAD_DIM)),
        'state_mlstm_c': 0.3 * nrm(4, (DEC_BATCH, DEPTH, 2, MLSTM_HEADS, HEAD_DIM, HEAD_DIM)),
        'state_mlstm_n': 0.3 * nrm(5, (DEC_BATCH, DEPTH, 2, MLSTM_HEADS, HEAD_DIM)),
        'state_mlstm_m': nrm(6, (DEC_BATCH, DEPTH, 2, MLSTM_HEADS)),
        'state_ssd': 0.5 * nrm(7, (DEC_BATCH, DEPTH, 2, SSD_HEADS, HEAD_DIM, SSD_N)),
        'c_ctx': nrm(8, (D,)),
        'w_ada': nrm(9, (DEPTH, D, 6 * D)) * D ** -0.5,
        'b_ada': 0.02 * nrm(10, (DEPTH, 6 * D)),
        'w_in': nrm(11, (DEPTH, D, IN_W)) * D ** -0.5,
        'conv_w': nrm(12, (DEPTH, CONV_K, CONV_CH)) * CONV_K ** -0.5,
        'conv_b': 0.02 * nrm(13, (DEPTH, CONV_CH)),
        'gla_wa2': nrm(14, (DEPTH, 2, GLA_RANK, GLA_QK)) * GLA_RANK ** -0.5,
        'gla_ba': 0.1 * nrm(15, (DEPTH, 2, GLA_QK)),
        'mlstm_bi': 0.1 * nrm(16, (DEPTH, 2, MLSTM_HEADS)),
        'mlstm_bf': jnp.linspace(3.0, 6.0, MLSTM_HEADS) + 0.1 * nrm(17, (DEPTH, 2, MLSTM_HEADS)),
        'ssd_dt_bias': dt0 + jnp.log(-jnp.expm1(-dt0)),
        'ssd_a_log': jnp.log(jax.random.uniform(ks[19], (DEPTH, 2, SSD_HEADS), f32, minval=1.0, maxval=16.0)),
        'ssd_d': 1.0 + 0.1 * nrm(20, (DEPTH, SSD_HEADS)),
        'gnorm_w': 1.0 + 0.05 * nrm(21, (DEPTH, MIX_W)),
        'w_out': nrm(22, (DEPTH, MIX_W, D)) * (MIX_W ** -0.5 * DEEPNORM_BETA),
        'ln1_w': 1.0 + 0.05 * nrm(23, (DEPTH, D)),
        'ln1_b': 0.02 * nrm(24, (DEPTH, D)),
        'peer_wq': nrm(25, (DEPTH, D, PEER_HEADS * PEER_DK)) * D ** -0.5,
        'peer_keys': nrm(26, (DEPTH, 2, N_KEYS, PEER_DK // 2)) * (PEER_DK // 2) ** -0.5,
        'peer_u': nrm(27, (DEPTH, N_EXPERTS, D)) * D ** -0.5,
        'peer_v': nrm(28, (DEPTH, N_EXPERTS, D)) * DEEPNORM_BETA,
        'ln2_w': 1.0 + 0.05 * nrm(29, (DEPTH, D)),
        'ln2_b': 0.02 * nrm(30, (DEPTH, D)),
    }

def reference(x_prompt, x_sample, c, state_gla, state_mlstm_c, state_mlstm_n, state_mlstm_m, state_ssd,
              c_ctx, w_ada, b_ada, w_in, conv_w, conv_b, gla_wa2, gla_ba, mlstm_bi, mlstm_bf,
              ssd_dt_bias, ssd_a_log, ssd_d, gnorm_w, w_out, ln1_w, ln1_b,
              peer_wq, peer_keys, peer_u, peer_v, ln2_w, ln2_b):
    def layer(h, cond, st, l):
        return _layer(h, cond, st, w_ada[l], b_ada[l], w_in[l], conv_w[l], conv_b[l], gla_wa2[l], gla_ba[l],
                      mlstm_bi[l], mlstm_bf[l], ssd_dt_bias[l], ssd_a_log[l], ssd_d[l], gnorm_w[l], w_out[l],
                      ln1_w[l], ln1_b[l], peer_wq[l], peer_keys[l], peer_u[l], peer_v[l], ln2_w[l], ln2_b[l])

    bp = x_prompt.shape[0]
    dtype = x_prompt.dtype
    zero_st = (jnp.zeros((bp, 2, GLA_HEADS, GLA_DK, HEAD_DIM), dtype),
               jnp.zeros((bp, 2, MLSTM_HEADS, HEAD_DIM, HEAD_DIM), dtype),
               jnp.zeros((bp, 2, MLSTM_HEADS, HEAD_DIM), dtype),
               jnp.zeros((bp, 2, MLSTM_HEADS), dtype),
               jnp.zeros((bp, 2, SSD_HEADS, HEAD_DIM, SSD_N), dtype))
    h = x_prompt
    ctx_states = []
    for l in range(DEPTH):
        h, st = layer(h, c_ctx[None, :], zero_st, l)
        ctx_states.append(st)
    y_prompt = h
    new_state_gla = jnp.stack([s[0] for s in ctx_states], axis=1)
    new_state_mlstm_c = jnp.stack([s[1] for s in ctx_states], axis=1)
    new_state_mlstm_n = jnp.stack([s[2] for s in ctx_states], axis=1)
    new_state_mlstm_m = jnp.stack([s[3] for s in ctx_states], axis=1)
    new_state_ssd = jnp.stack([s[4] for s in ctx_states], axis=1)

    h = x_sample + _grid_pos_embed(x_sample.shape[1], x_sample.shape[2]).astype(x_sample.dtype)
    for l in range(DEPTH):
        st = (state_gla[:, l], state_mlstm_c[:, l], state_mlstm_n[:, l], state_mlstm_m[:, l], state_ssd[:, l])
        h, _ = layer(h, c, st, l)
    y_sample = h

    return (y_prompt, y_sample, new_state_gla, new_state_mlstm_c, new_state_mlstm_n, new_state_mlstm_m, new_state_ssd)


_drawn_inputs = setup_inputs


def setup_inputs(seed=0):
    import zlib

    import numpy as np

    out = dict(_drawn_inputs(seed))
    spreads = {}
    factors = {'state_gla': 8.0, 'state_mlstm_n': 3.502, 'state_mlstm_m': 3.167, 'ssd_d': 3.189}
    for name, (base, spread) in spreads.items():
        noise = np.random.default_rng([zlib.crc32(name.encode()), seed]).standard_normal(out[name].shape)
        drawn = base * np.exp(spread * noise) if base else spread * noise
        out[name] = __import__('jax').numpy.asarray(drawn.astype(out[name].dtype))
    for name, factor in factors.items():
        out[name] = (out[name] * factor).astype(out[name].dtype)
    return out
```

```python
import math
from contextlib import ExitStack

import numpy as np

import concourse.bass as bass
from concourse import mybir

F32 = mybir.dt.float32
U32 = mybir.dt.uint32
ALU = mybir.AluOpType
ACT = mybir.ActivationFunctionType
AX = mybir.AxisListType.X

P = 128
D = 1024
KC = D // P
DEPTH = 2
TILES = 5
NPOS = 6
SEQ_TILES = 1
DEC_TILES = 4
GRID_W = 64
POS_BASE = 10000.0
HD = 64
GH, MH, SH = 4, 4, 8
GDK = 32
RANK = 16
IN_W = 3136
O_GQ, O_GK, O_GV, O_GG, O_GA = 0, 128, 256, 512, 768
O_MQ, O_MK, O_MV, O_MO, O_MI = 800, 1056, 1312, 1568, 1824
O_SX, O_SZ, O_SB, O_SDT = 1840, 2352, 2864, 3120
NDIR = 140
DB = NDIR + 4 + 8
VA = MH * (HD + 1)
TOK_W = 256 + VA + 2 * DB
S_SSD, S_ML, S_GLA, S_W = 0, 512, 512 + VA, 512 + VA + 256
NE = 16384
HEADS = 8
TOPK = 16
SLOTS = HEADS * TOPK
ALPHA = (2 * DEPTH) ** 0.25
EPS = 1e-6
BL = 16
NB = P // BL
CLAMP = 40.0
PHASES = 5


EVENTS = {
    "m_pe": ["mod0", "mod1"],
    "m_dve": ["mod0", "mod1"],
    "i_dve": ["add"],
    "p_dve": [
        "st0", "st1", "mv", "rs", "xn", "xs", "xsh", "ut0", "gat", "c4", "z0", "z1", "z2", "ig", "zs",
        "za", "vg", "vm", "sp", "la", "dt",
    ],
    "p_act": ["sd", "ut1", "a1", "a2", "b1", "b2", "ze", "ln", "silug", "siluz", "sigmo"],
    "p_pe": ["tr0", "tr1", "A", "B", "C", "D", "E1", "E", "gate", "last"],
    "pl_dve": ["coef", "vone"],
    "pl_act": ["ea"],
    "c_dve": [
        "a0", "b0", "c0", "a1", "b1", "c1", "a2", "b2", "c2", "a3", "b3", "c3", "a4", "b4", "c4", "a5",
        "b5", "c5", "tok0", "tok1",
    ],
    "c_act": ["silu0", "silu1", "silu2", "silu3", "silu4", "silu"],
    "c_pe": ["t0", "t1"],
    "s_dve0": [
        "cs", "f4", "dec", "g4", "ex0", "ex1", "ex2", "ex3", "ex4", "ex5", "ex6", "ex7", "cbm", "g4r",
        "r4", "kta", "ktb", "qba", "qbb", "gg8", "qh", "kdm", "qp0", "qp1", "qp2", "qp3", "ktm", "gt",
        "kmd", "em0", "em1", "em2", "em3", "w8", "xw", "qkm", "me0", "me1", "me2", "me3", "ys0", "ys1",
        "wm", "at", "t1", "hm0", "hm1", "dn0", "dn1", "rc", "ym", "yg", "t3", "sng", "t2", "last",
    ],
    "s_dve1": [
        "cs", "f4", "dec", "g4", "ex0", "ex1", "ex2", "ex3", "ex4", "ex5", "ex6", "ex7", "cbm", "g4r",
        "r4", "kta", "ktb", "qba", "qbb", "gg8", "qh", "kdm", "qp0", "qp1", "qp2", "qp3", "ktm", "gt",
        "kmd", "em0", "em1", "em2", "em3", "w8", "xw", "qkm", "me0", "me1", "me2", "me3", "ys0", "ys1",
        "wm", "at", "t1", "hm0", "hm1", "dn0", "dn1", "rc", "ym", "yg", "t3", "sng", "t2", "last",
    ],
    "s_act0": ["ea", "eb", "kd", "ex0", "ex1", "kt", "qb", "em", "me"],
    "s_act1": ["ea", "eb", "kd", "ex0", "ex1", "kt", "qb", "em", "me"],
    "s_pe0": ["cum", "g4r", "km", "qk", "kdt", "gb", "ssd", "att", "ups", "mli", "upg", "upm"],
    "s_pe1": ["cum", "g4r", "km", "qk", "kdt", "gb", "ssd", "att", "ups", "mli", "upg", "upm"],
    "s_pool0": ["ct0", "qm0", "ct1", "qm1", "xd", "vw", "sns", "snm", "sna1", "sna"],
    "s_pool1": ["ct0", "qm0", "ct1", "qm1", "xd", "vw", "sns", "snm", "sna1", "sna"],
    "o_dve": [
        "y0", "y1", "y2", "y3", "sq", "hr", "hrm", "hrr", "yn1", "yn2", "yt0", "g0", "g1", "r1", "st0a",
        "st1a", "mva", "rsa", "x1a", "x1b", "x1c", "st0b", "st1b", "mvb", "rsb", "u2a", "u2b", "u2c",
        "ut0", "qt0", "ma0", "mb0", "mc0", "md0", "mf0", "ma1", "mb1", "mc1", "md1", "mf1", "ma2",
        "mb2", "mc2", "md2", "mf2", "ma3", "mb3", "mc3", "md3", "mf3", "ma4", "mb4", "mc4", "md4",
        "mf4", "ma5", "mb5", "mc5", "md5", "mf5", "ma6", "mb6", "mc6", "md6", "mf6", "ma7", "mb7",
        "mc7", "md7", "mf7", "ma8", "mb8", "mc8", "md8", "mf8", "ma9", "mb9", "mc9", "md9", "mf9",
        "ma10", "mb10", "mc10", "md10", "mf10", "ma11", "mb11", "mc11", "md11", "mf11", "ma12", "mb12",
        "mc12", "md12", "mf12", "ma13", "mb13", "mc13", "md13", "mf13", "ma14", "mb14", "mc14", "md14",
        "mf14", "ma15", "mb15", "mc15", "md15", "mf15", "tf", "can", "na0", "nb0", "nc0", "nd0", "ne0",
        "na1", "nb1", "nc1", "nd1", "ne1", "na2", "nb2", "nc2", "nd2", "ne2", "na3", "nb3", "nc3",
        "nd3", "ne3", "na4", "nb4", "nc4", "nd4", "ne4", "na5", "nb5", "nc5", "nd5", "ne5", "na6",
        "nb6", "nc6", "nd6", "ne6", "na7", "nb7", "nc7", "nd7", "ne7", "ba", "bb", "baf", "bbf", "oh0",
        "oi0", "oj0", "oh1", "oi1", "oj1", "ixa", "ixb", "sma", "smb", "smc", "smd",
    ],
    "o_act": ["hsd", "yt1", "sda", "sdb", "ut1", "qt1", "sc0", "sc1", "sc2", "sc3", "sme"],
    "o_pe": ["yt0", "yt1", "out", "ut0", "ut1", "q0", "q1", "s0", "s1", "s2", "s3"],
    "e_pool": ["ix0", "gw0", "ix1", "gw1"],
    "e_dve": [
        "dot0", "dot1", "dot2", "dot3", "dot4", "dot5", "dot6", "dot7", "aw0", "dot8", "dot9", "dot10",
        "dot11", "aw1", "dot12", "dot13", "dot14", "dot15", "aw2", "dot16", "dot17", "dot18", "dot19",
        "aw3", "dot20", "dot21", "dot22", "dot23", "aw4", "dot24", "dot25", "dot26", "dot27", "aw5",
        "acc00", "acc01", "dot28", "dot29", "dot30", "dot31", "aw6", "aw7", "acc10", "acc11",
    ],
    "e_act": [
        "ge0", "ge1", "dg0", "dg1", "dg2", "dg3", "ge2", "dg4", "dg5", "dg6", "dg7", "ge3", "dg8",
        "dg9", "dg10", "dg11", "ge4", "dg12", "dg13", "dg14", "dg15", "ge5", "dg16", "dg17", "dg18",
        "dg19", "ge6", "dg20", "dg21", "dg22", "dg23", "ge7", "dg24", "dg25", "dg26", "dg27", "dg28",
        "dg29", "dg30", "dg31",
    ],
    "e_pe": [
        "v0", "v1", "v2", "v3", "v4", "v5", "v6", "v7", "v8", "v9", "v10", "v11", "v12", "v13", "v14",
        "v15", "v16", "v17", "v18", "v19", "v20", "v21", "v22", "v23", "v24", "v25", "v26", "v27",
        "v28", "v29", "v30", "v31",
    ],
    "et_dve": ["zero", "r0", "r1", "st0", "st1", "mv", "r2", "xa", "xw", "xb"],
    "et_act": ["sd"],
}


class Steps:

    def __init__(self, sem, names, unit=1, ahead=1):
        self.sem, self.names, self.unit, self.ahead, self.seen = sem, names, unit, ahead, 0

    def take(self, name):
        assert self.names[self.seen % len(self.names)] == name, (name, self.names, self.seen)
        self.seen += 1

    @property
    def round(self):
        return len(self.names) * self.unit

    def at(self, it, name, back=0):
        i = self.names.index(name)
        return it * self.round + ((self.ahead - back) * self.round + (i + 1) * self.unit)


def build(nc, io):
    x_in, pos_in, c2t, w_ada, b_ada = io["x_in"], io["pos_in"], io["c2t"], io["w_ada"], io["b_ada"]
    xres, state, mstate = io["xres"], io["state"], io["mstate"]

    ctx = ExitStack()
    with ctx:
        def sem(name):
            return ctx.enter_context(nc.semaphore(name))


        def dram(name, shape, dt=F32):
            return io["scratch"](name, shape, dt)

        modd = dram("modd", [DEPTH, 2, 6 * D])
        tok_d = dram("tok_d", [NPOS, P, TOK_W])
        feat_d = dram("feat_d", [NPOS, P, 6 * P])
        gate_d = dram("gate_d", [NPOS, P, D])
        conv_d = dram("conv_d", [P, 6, NPOS * P + 2])
        ctok_d = dram("ctok_d", [NPOS, P, 640])
        cfeat_d = dram("cfeat_d", [NPOS, P, 2 * P])
        y_d = dram("y_d", [2, NPOS, P, D])
        u2_d = dram("u2_d", [NPOS, P, D])
        x1_d = dram("x1_d", [NPOS, P, D])

        big = ctx.enter_context(nc.sbuf_tensor("big", [P, 53200], F32))
        ps = [ctx.enter_context(nc.psum_tensor(f"bank{b}", [P, 512], F32)) for b in range(8)]

        class Area:
            def __init__(self, base):
                self.top = base

            def __call__(self, cols, parts=P):
                a = self.top
                self.top += cols
                assert self.top <= 53200, self.top
                return big[0:parts, a:a + cols]

        keep = Area(0)
        ident = keep(P)
        ones = keep(P)
        eps = keep(1)
        idx_all = keep(NPOS * SLOTS)
        gw_all = keep(NPOS * SLOTS)
        base = keep.top

        met = sem("met")
        credit = sem("credit")
        passed = sem("passed")
        start_ld = sem("start_ld")
        sem_ones = sem("sem_ones")
        sem_silu = sem("sem_silu")
        fill_st = sem("fill_st")

        def apart(eng, s, value):
            eng.wait_ge(s, value)
            eng.sem_inc(passed, 1)

        def meet(eng, n):
            eng.sem_inc(passed, 1)
            eng.drain().then_inc(met, 1)
            apart(eng, met, n * 5 + 5)

        def linker(eng, s, it, alone=False):
            s.seen = 0

            def link(name, ins):
                s.take(name)
                ins.then_inc(s.sem, 1)
                eng.wait_ge(s.sem, s.at(it, name))
                if alone:
                    eng.sem_inc(passed, 1)
            return link

        def marker(s):
            s.seen = 0

            def mark(name, ins):
                s.take(name)
                ins.then_inc(s.sem, 1)
            return mark

        def pos(s):
            return nc.s_assert_within(s + ((s + 3) >> 2), 0, NPOS - 1,
                                      skip_runtime_bounds_check_because="s is 0..4: 0, 2, 3, 4, 5")

        def bwd_pos(s):
            return nc.s_assert_within(((s + 3) >> 2) * 6 - s, 0, NPOS - 1,
                                      skip_runtime_bounds_check_because="s is 0..4: 0, 5, 4, 3, 2")

        def group(s):
            return nc.s_assert_within((s + 3) >> 2, 0, 1,
                                      skip_runtime_bounds_check_because="s is 0..4: 0, 1, 1, 1, 1")

        def at1(t, i):
            v = t[bass.ds(i, 1)]
            return v.rearrange("a " + " ".join("bcde"[:len(v.shape) - 1]) + " -> (a b) "
                               + " ".join("cde"[:len(v.shape) - 2]))

        def grp(ap, **k):
            return ap.rearrange("p (a b) -> p a b", **k)

        def rows(ap):
            return ap.partition_broadcast(P)

        sp_own, act_own, pe_own, dve_own, pool_own = [], [], [], [], []

        def mk(owner, name, unit=1, events=None, ahead=1):
            s = Steps(sem(name), EVENTS[name] if events is None else events, unit, ahead)
            if ahead:
                owner.append(s)
            return s

        m_w = [mk(sp_own, f"m_w{u}", 32, ["w"]) for u in (0, 1)]
        m_pe, m_dve = mk(pe_own, "m_pe"), mk(dve_own, "m_dve")
        m_out = [mk(sp_own, f"m_out{u}", 16, ["out"]) for u in (0, 1)]
        i_ld, i_dve, i_st = mk(sp_own, "i_ld", 32, ["ld"]), mk(dve_own, "i_dve"), mk(sp_own, "i_st", 16, ["st"])
        p_w, p_par = sem("p_w"), sem("p_par")
        p_x, p_mod = mk(sp_own, "p_x", 16, ["x"]), mk(sp_own, "p_mod", 32, ["mod"])
        p_dve, p_act, p_pe = mk(dve_own, "p_dve"), mk(act_own, "p_act"), mk(pe_own, "p_pe")
        p_st = mk(sp_own, "p_st", 64, ["st"])
        pl_dve, pl_act = mk(dve_own, "pl_dve"), mk(act_own, "pl_act")
        c_par = sem("c_par")
        c_ld, c_st = mk(sp_own, "c_ld", 16, ["ld"]), mk(sp_own, "c_st", 32, ["st"])
        c_dve, c_act, c_pe = mk(dve_own, "c_dve"), mk(act_own, "c_act"), mk(pe_own, "c_pe")
        s_con = sem("s_con")
        s_pad = sem("s_pad")
        s_ld = [mk(sp_own, f"s_ld{d}", 64, ["ld"]) for d in (0, 1)]
        s_ls = [mk(sp_own, f"s_ls{d}", 64, ["ls"]) for d in (0, 1)]
        s_st = [mk(sp_own, f"s_st{d}", 48, ["st"]) for d in (0, 1)]
        s_dve = [mk(dve_own, f"s_dve{d}") for d in (0, 1)]
        s_act = [mk(act_own, f"s_act{d}") for d in (0, 1)]
        s_pe = [mk(pe_own, f"s_pe{d}") for d in (0, 1)]
        s_pool = [mk(pool_own, f"s_pool{d}") for d in (0, 1)]
        o_par = sem("o_par")
        o_ld, o_ldx, o_st = mk(sp_own, "o_ld", 64, ["ld"]), mk(sp_own, "o_ldx", 64, ["ld"]), mk(sp_own, "o_st", 32, ["st"])
        o_dve, o_act, o_pe = mk(dve_own, "o_dve"), mk(act_own, "o_act"), mk(pe_own, "o_pe")
        e_par = sem("e_par")
        e_u, e_x, e_st = mk(sp_own, "e_u", 16, ["u"]), mk(sp_own, "e_x", 32, ["x"]), mk(sp_own, "e_st", 16, ["st"])
        e_gat = [mk(pool_own, f"e_gat{j}", 16, ["g0", "g1"], ahead=0) for j in range(TOPK)]
        e_pool = mk(pool_own, "e_pool")
        e_dve, e_act, e_pe = mk(dve_own, "e_dve"), mk(act_own, "e_act"), mk(pe_own, "e_pe")
        et_dve, et_act = mk(dve_own, "et_dve"), mk(act_own, "et_act")

        def give_credit(eng, own):
            for s in own:
                if s.names:
                    eng.sem_inc(s.sem, s.round)
            eng.sem_inc(credit, 1)
            eng.wait_ge(credit, 5)

        a = Area(base)
        WA = [a(KC * 512) for _ in (0, 1)]
        BA = [a(512, 2) for _ in (0, 1)]
        MO = [a(512, 2) for _ in (0, 1)]
        CT, CS2 = a(2 * KC), a(2 * KC)
        XI, PI_ = a(D), a(D)

        a = Area(base)
        WIN = a(KC * IN_W)
        win = WIN.rearrange("p (k n) -> p k n", k=KC)
        X, SC, SHF, U = a(D), a(D), a(D), a(D)
        UT = a(D)
        FA, CP, GG, TB = a(6 * P), a(6 * P), a(D), a(TOK_W)
        GAT = a(P, 32)
        WA2 = a(256, 32)
        BROW, COEF, SGN = a(2 * NDIR), a(2 * NDIR), a(2 * NDIR)
        BIG_, ALOG = a(8), a(16)
        Z, ZA, ZL = a(2 * NDIR), a(2 * NDIR), a(2 * NDIR)
        ST6, MV, SD, RS = a(12), a(2), a(1), a(1)
        dirs = TB[:, 256 + VA:].rearrange("p (d w) -> p d w", d=2)

        a = Area(base)
        CI, CW, CB_ = a(6 * 130), a(18), a(6)
        CV, CV2, CO = a(6 * P), a(6 * P), a(6 * P)
        CTK = a(640)

        a = Area(base)
        TRI, PERM = [a(P) for _ in (0, 1)], [a(P) for _ in (0, 1)]
        GM = a(S_W)
        sc = []
        for d in (0, 1):
            v = dict(TK=a(256 + VA + DB), FT=a(6 * P), TX=a(640), FX=a(2 * P), ST=a(S_W), MB=a(4), MC=a(1, 4),
                     CS=a(162), F4=a(1, 4), EX=a(8 * P), CTP=a(2 * P), CBM=a(2 * P), XD=a(512), XW=a(512),
                     EA=a(29), KT=a(NB * P), QB=a(P), QP=a(NB * 4 * BL), QH=a(P), EB=a(P), AT=a(4 * P),
                     KD=a(P), KMD=a(3 * P), G4=a(4), G4R=a(P, 4), R4=a(P, 4), GG8=a(8), GT=a(4), EMA=a(16),
                     EM=a(16), ME=a(4 * P), QMP=a(4 * P), T1=a(512), T2=a(VA), T3=a(256), VW=a(VA), HM=a(VA),
                     DN=a(4), RC=a(4), Y=a(D), SN=a(S_W), MN=a(1, 4))
            sc.append(v)

        a = Area(base)
        WO, WQ = a(KC * D), a(KC * D)
        wo, wq = (w.rearrange("p (k n) -> p k n", k=KC) for w in (WO, WQ))
        KEYS = a(256)
        GNW, L1W, L1B = a(D), a(D), a(D)
        DROW = a(8)
        IOTA, LOFS = a(16), a(1)
        YF, YB, GO, TX3, XO, G1, SC2, SH2 = a(D), a(D), a(D), a(512), a(D), a(D), a(D), a(D)
        YT, U2T, QT = a(D), a(D), a(D)
        SQ, HR, HR2, HR3 = a(D), a(16), a(16), a(16)
        SCO = a(2048)
        TV, TI, TF = a(256), a(256), a(256)
        CAN = a(2048)
        BV, BI, BA1, BB1, BAF, BBF = a(P), a(P), a(P), a(P), a(P), a(P)
        OH = a(2048)
        IFR, JFR = a(P), a(P)
        SM, SR = a(8), a(8)
        oST6, oMV, oSD, oRS = a(12), a(2), a(1), a(1)

        a = Area(base)
        RING = a(TOPK * 2 * D)
        ring = RING.rearrange("p (j n) -> p j n", j=TOPK)
        EU, EX1, EG2, ACC = a(D), a(D), a(D), a(D)
        L2W, L2B = a(D), a(D)
        IXH, GWH = a(2 * TOPK), a(2 * TOPK)
        DOT, AG, AW = a(2 * TOPK), a(2 * TOPK), a(2 * TOPK)
        DG = a(8 * P)
        eST6, eMV, eSD, eRS = a(12), a(2), a(1), a(1)

        block = ctx.enter_context(nc.Block())

        @block.sync
        def _(sp):
            give_credit(sp, sp_own)
            sp.dma_start(ident, io["ident"]).then_inc(start_ld, 16)
            sp.dma_start(CT, c2t).then_inc(start_ld, 16)
            for d, slots in ((0, (0, 2)), (1, (1, 6))):
                for w, slot in enumerate(slots):
                    sp.dma_start(state[:, d, slot], io["state0"][:, d, w]).then_inc(fill_st, 16)
                    sp.dma_start(mstate[:, d, slot], io["m0"][:, d, w]).then_inc(fill_st, 16)
            for c0, c1 in ((0, 1), (P + 1, 2 * P + 1), (NPOS * P + 1, NPOS * P + 2)):
                with nc.allow_non_contiguous_dma(reason="one column at either edge"):
                    sp.dma_start(conv_d[:, :, c0:c1], io["zeros"][:, :, 0:c1 - c0]).then_inc(fill_st, 16)

            with sp.Fori(0, DEPTH) as l:
                with sp.Fori(0, 6) as jj:
                    it = l * 6 + jj
                    for u in (0, 1):
                        cols = bass.ds(jj * 1024 + u * 512, 512)
                        apart(sp, m_pe.sem, m_pe.at(it, f"mod{u}", 1))
                        apart(sp, m_dve.sem, m_dve.at(it, f"mod{u}", 1))
                        sp.dma_start(WA[u].rearrange("p (k n) -> p k n", k=KC),
                                     at1(w_ada, l)[:, cols].rearrange("(k p) n -> p k n", p=P)
                                     ).then_inc(m_w[u].sem, 16)
                        sp.dma_start(BA[u], at1(b_ada, l)[cols].partition_broadcast(2)
                                     ).then_inc(m_w[u].sem, 16)
                    for u in (0, 1):
                        cols = bass.ds(jj * 1024 + u * 512, 512)
                        apart(sp, m_dve.sem, m_dve.at(it, f"mod{u}"))
                        sp.dma_start(at1(modd, l)[:, cols], MO[u]).then_inc(m_out[u].sem, 16)
            with sp.Fori(0, TILES) as s:
                p = pos(s)
                apart(sp, i_dve.sem, i_dve.at(s, "add", 1))
                apart(sp, i_st.sem, i_st.at(s, "st", 1))
                sp.dma_start(XI, at1(x_in, p)).then_inc(i_ld.sem, 16)
                sp.dma_start(PI_, at1(pos_in, p)).then_inc(i_ld.sem, 16)
                apart(sp, i_dve.sem, i_dve.at(s, "add"))
                sp.dma_start(at1(xres, p), XI).then_inc(i_st.sem, 16)
            apart(sp, i_st.sem, i_st.at(TILES - 1, "st"))
            for u in (0, 1):
                apart(sp, m_out[u].sem, m_out[u].at(DEPTH * 6 - 1, "out"))
            apart(sp, fill_st, 16 * 11)
            meet(sp, 0)

            with sp.Fori(0, DEPTH) as l:
                for k in range(KC):
                    sp.dma_start(win[:, k, :], at1(io["w_in"], l)[k * P:(k + 1) * P, :]).then_inc(p_w, 16)
                sp.dma_start(BROW, rows(at1(io["gbias"], l))).then_inc(p_par, 16)
                sp.dma_start(BIG_, rows(at1(io["mlstm_bi"], l))).then_inc(p_par, 16)
                sp.dma_start(ALOG, rows(at1(io["ssd_a_log"], l))).then_inc(p_par, 16)
                sp.dma_start(WA2, at1(io["wa2"], l)).then_inc(p_par, 16)
                sp.dma_start(SGN, rows(io["sgn"])).then_inc(p_par, 16)
                sp.dma_start(COEF, rows(io["coef"])).then_inc(p_par, 16)
                with sp.Fori(0, TILES) as s:
                    it, p = l * TILES + s, pos(s)
                    mrow = modd[bass.ds(l, 1), bass.ds(group(s), 1), :].rearrange("a b n -> (a b n)")
                    apart(sp, p_dve.sem, p_dve.at(it, "xn", 1))
                    sp.dma_start(X, at1(xres, p)).then_inc(p_x.sem, 16)
                    apart(sp, p_dve.sem, p_dve.at(it, "xsh", 1))
                    sp.dma_start(SC, rows(mrow[D:2 * D])).then_inc(p_mod.sem, 16)
                    sp.dma_start(SHF, rows(mrow[0:D])).then_inc(p_mod.sem, 16)
                    apart(sp, p_act.sem, p_act.at(it, "b2"))
                    sp.dma_start(at1(feat_d, p), FA).then_inc(p_st.sem, 16)
                    apart(sp, p_dve.sem, p_dve.at(it, "dt"))
                    sp.dma_start(conv_d[:, :, bass.ds(p * P + 1, P)],
                                 CP.rearrange("p (c n) -> p c n", c=6)).then_inc(p_st.sem, 16)
                    sp.dma_start(at1(tok_d, p), TB).then_inc(p_st.sem, 16)
                    apart(sp, p_act.sem, p_act.at(it, "sigmo"))
                    sp.dma_start(at1(gate_d, p), GG).then_inc(p_st.sem, 16)
                apart(sp, p_st.sem, p_st.at(l * TILES + TILES - 1, "st"))
                meet(sp, l * PHASES + 1)

                sp.dma_start(CW, at1(io["conv_w"], l)).then_inc(c_par, 16)
                sp.dma_start(CB_, at1(io["conv_b"], l)).then_inc(c_par, 16)
                with sp.Fori(0, TILES) as s:
                    it, p = l * TILES + s, pos(s)
                    apart(sp, c_dve.sem, c_dve.at(it, "c5", 1))
                    sp.dma_start(CI.rearrange("p (c n) -> p c n", c=6),
                                 conv_d[:, :, bass.ds(p * P, P + 2)]).then_inc(c_ld.sem, 16)
                    apart(sp, c_act.sem, c_act.at(it, "silu"))
                    sp.dma_start(at1(cfeat_d, p), CO[:, 4 * P:6 * P]).then_inc(c_st.sem, 16)
                    apart(sp, c_dve.sem, c_dve.at(it, "tok1"))
                    sp.dma_start(at1(ctok_d, p), CTK).then_inc(c_st.sem, 16)
                apart(sp, c_st.sem, c_st.at(l * TILES + TILES - 1, "st"))
                meet(sp, l * PHASES + 2)

                for d in (0, 1):
                    sp.dma_start(TRI[d], io["tri"][d]).then_inc(s_con, 16)
                    sp.dma_start(PERM[d], io["perm"][d]).then_inc(s_con, 16)
                sp.dma_start(GM, io["gmask"]).then_inc(s_con, 16)
                with sp.Fori(0, TILES) as s:
                    it = l * TILES + s
                    for d in (0, 1):
                        v = sc[d]
                        p = pos(s) if d == 0 else bwd_pos(s)
                        src = p if d == 0 else p + 1
                        apart(sp, s_pe[d].sem, s_pe[d].at(it, "upm", 1))
                        apart(sp, s_dve[d].sem, s_dve[d].at(it, "last", 1))
                        apart(sp, s_pool[d].sem, s_pool[d].at(it, "sna", 1))
                        sp.dma_start(v["TK"][:, 0:256 + VA], at1(tok_d, p)[:, 0:256 + VA]).then_inc(s_ld[d].sem, 16)
                        sp.dma_start(v["TK"][:, 256 + VA:],
                                     at1(tok_d, p)[:, 256 + VA + d * DB:256 + VA + (d + 1) * DB]
                                     ).then_inc(s_ld[d].sem, 16)
                        sp.dma_start(v["FT"], at1(feat_d, p)).then_inc(s_ld[d].sem, 16)
                        sp.dma_start(v["TX"], at1(ctok_d, p)).then_inc(s_ld[d].sem, 16)
                        sp.dma_start(v["FX"], at1(cfeat_d, p)).then_inc(s_ls[d].sem, 16)
                        apart(sp, s_st[d].sem, s_st[d].at(it, "st", 1))
                        stl, msl = (t[bass.ds(l, 1), d, bass.ds(src, 1)] for t in (state, mstate))
                        sp.dma_start(v["ST"], stl.rearrange("a b p n -> (a b p) n")).then_inc(s_ls[d].sem, 16)
                        sp.dma_start(v["MB"], rows(msl.rearrange("a b n -> (a b n)"))).then_inc(s_ls[d].sem, 16)
                        sp.dma_start(v["MC"], msl.rearrange("a b (n c) -> (a b n) c", c=1)).then_inc(s_ls[d].sem, 16)
                    for d in (0, 1):
                        v = sc[d]
                        p = pos(s) if d == 0 else bwd_pos(s)
                        dst = p + 1 if d == 0 else p
                        apart(sp, s_dve[d].sem, s_dve[d].at(it, "last"))
                        apart(sp, s_pool[d].sem, s_pool[d].at(it, "sna"))
                        ydst = y_d[d, bass.ds(p, 1)].rearrange("a p n -> (a p) n")
                        sp.dma_start(ydst, v["Y"]).then_inc(s_st[d].sem, 16)
                        stl, msl = (t[bass.ds(l, 1), d, bass.ds(dst, 1)] for t in (state, mstate))
                        sp.dma_start(stl.rearrange("a b p n -> (a b p) n"), v["SN"]).then_inc(s_st[d].sem, 16)
                        sp.dma_start(msl.rearrange("a b (n c) -> (a b n) c", c=1), v["MN"]).then_inc(s_st[d].sem, 16)
                for d in (0, 1):
                    apart(sp, s_st[d].sem, s_st[d].at(l * TILES + TILES - 1, "st"))
                meet(sp, l * PHASES + 3)

                sp.dma_start(wo, at1(io["w_out"], l).rearrange("(k p) n -> p k n", p=P)).then_inc(o_par, 16)
                sp.dma_start(wq, at1(io["peer_wq"], l).rearrange("(k p) n -> p k n", p=P)).then_inc(o_par, 16)
                sp.dma_start(KEYS, at1(io["keys"], l)).then_inc(o_par, 16)
                sp.dma_start(GNW, rows(at1(io["gnorm_w"], l))).then_inc(o_par, 16)
                sp.dma_start(L1W, rows(at1(io["ln1_w"], l))).then_inc(o_par, 16)
                sp.dma_start(L1B, rows(at1(io["ln1_b"], l))).then_inc(o_par, 16)
                sp.dma_start(DROW, rows(at1(io["ssd_d"], l))).then_inc(o_par, 16)
                sp.dma_start(IOTA, rows(io["iota"])).then_inc(o_par, 16)
                sp.dma_start(LOFS, rows(at1(io["lofs"], l))).then_inc(o_par, 16)
                with sp.Fori(0, TILES) as s:
                    it, p = l * TILES + s, pos(s)
                    mrow = modd[bass.ds(l, 1), bass.ds(group(s), 1), :].rearrange("a b n -> (a b n)")
                    apart(sp, o_dve.sem, o_dve.at(it, "yn2", 1))
                    apart(sp, o_pe.sem, o_pe.at(it, "yt1", 1))
                    for dst, src in ((YF, y_d[0, bass.ds(p, 1)].rearrange("a p n -> (a p) n")),
                                     (YB, y_d[1, bass.ds(p, 1)].rearrange("a p n -> (a p) n")),
                                     (GO, at1(gate_d, p)), (TX3, at1(ctok_d, p)[:, 0:512])):
                        sp.dma_start(dst, src).then_inc(o_ld.sem, 16)
                    apart(sp, o_dve.sem, o_dve.at(it, "u2c", 1))
                    apart(sp, o_pe.sem, o_pe.at(it, "ut1", 1))
                    apart(sp, o_st.sem, o_st.at(it, "st", 1))
                    for dst, src in ((XO, at1(xres, p)), (G1, rows(mrow[2 * D:3 * D])),
                                     (SC2, rows(mrow[4 * D:5 * D])), (SH2, rows(mrow[3 * D:4 * D]))):
                        sp.dma_start(dst, src).then_inc(o_ldx.sem, 16)
                    apart(sp, o_dve.sem, o_dve.at(it, "u2c"))
                    sp.dma_start(at1(x1_d, p), XO).then_inc(o_st.sem, 16)
                    sp.dma_start(at1(u2_d, p), SC2).then_inc(o_st.sem, 16)
                apart(sp, o_st.sem, o_st.at(l * TILES + TILES - 1, "st"))
                meet(sp, l * PHASES + 4)

                sp.dma_start(L2W, rows(at1(io["ln2_w"], l))).then_inc(e_par, 16)
                sp.dma_start(L2B, rows(at1(io["ln2_b"], l))).then_inc(e_par, 16)
                with sp.Fori(0, TILES) as s:
                    it, p = l * TILES + s, pos(s)
                    mrow = modd[bass.ds(l, 1), bass.ds(group(s), 1), :].rearrange("a b n -> (a b n)")
                    apart(sp, et_dve.sem, et_dve.at(it, "r2", 1))
                    sp.dma_start(EU, at1(u2_d, p)).then_inc(e_u.sem, 16)
                    apart(sp, e_st.sem, e_st.at(it, "st", 1))
                    sp.dma_start(EX1, at1(x1_d, p)).then_inc(e_x.sem, 16)
                    sp.dma_start(EG2, rows(mrow[5 * D:6 * D])).then_inc(e_x.sem, 16)
                    apart(sp, et_dve.sem, et_dve.at(it, "xb"))
                    sp.dma_start(at1(xres, p), EX1).then_inc(e_st.sem, 16)
                apart(sp, e_st.sem, e_st.at(l * TILES + TILES - 1, "st"))
                meet(sp, l * PHASES + 5)

        @block.vector
        def _(ve):
            give_credit(ve, dve_own)
            v_ = nc.vector

            def norm_stats(link, x, st6, mv):
                for h in (0, 1):
                    link(f"st{h}" + norm_stats.tag, v_.bn_stats(st6[:, 6 * h:6 * h + 6], x[:, 512 * h:512 * h + 512]))
                ve.sem_inc(passed, 1)
                link("mv" + norm_stats.tag, v_.bn_aggr(mv, st6))
            norm_stats.tag = ""

            v_.memset(ones, 1.0).then_inc(sem_ones, 1)
            v_.memset(eps, EPS).then_inc(sem_ones, 1)
            ve.wait_ge(sem_ones, 2)

            ve.sem_inc(passed, 1)
            with ve.Fori(0, DEPTH) as l:
                ve.sem_inc(passed, 1)
                with ve.Fori(0, 6) as jj:
                    it = l * 6 + jj
                    link = linker(ve, m_dve, it)
                    for u in (0, 1):
                        ve.wait_ge(m_pe.sem, m_pe.at(it, f"mod{u}"))
                        ve.wait_ge(m_w[u].sem, m_w[u].at(it, "w"))
                        ve.wait_ge(m_out[u].sem, m_out[u].at(it, "out", 1))
                        link(f"mod{u}", v_.tensor_tensor(MO[u], ps[u][0:2, :], BA[u], ALU.add))
            ve.sem_inc(passed, 1)
            with ve.Fori(0, TILES) as s:
                link = linker(ve, i_dve, s)
                ve.wait_ge(i_ld.sem, i_ld.at(s, "ld"))
                link("add", v_.tensor_tensor(XI, XI, PI_, ALU.add))
            meet(ve, 0)

            ve.sem_inc(passed, 1)
            with ve.Fori(0, DEPTH) as l:
                ve.wait_ge(p_par, (l + 1) * 96)
                link = linker(ve, pl_dve, l)
                ve.wait_ge(pl_act.sem, pl_act.at(l, "ea"))
                cf = grp(COEF, a=2)
                link("coef", v_.tensor_scalar(cf[:, :, 132:140], grp(ALOG, a=2), -1.0, None, ALU.mult))
                link("vone", v_.memset(TB[:, 256:256 + VA].rearrange("p (h e) -> p h e", h=MH)[:, :, HD:HD + 1], 1.0))
                ve.sem_inc(passed, 1)
                with ve.Fori(0, TILES) as s:
                    it = l * TILES + s
                    link = linker(ve, p_dve, it)
                    ve.wait_ge(p_x.sem, p_x.at(it, "x"))
                    norm_stats(link, X, ST6, MV)
                    ve.wait_ge(p_act.sem, p_act.at(it, "sd"))
                    link("rs", v_.reciprocal(RS, SD))
                    ve.wait_ge(p_pe.sem, p_pe.at(it, "tr1", 1))
                    link("xn", v_.tensor_scalar(U, X, MV[:, 0:1], RS, ALU.subtract, ALU.mult))
                    ve.wait_ge(p_mod.sem, p_mod.at(it, "mod"))
                    link("xs", v_.scalar_tensor_tensor(U, SC, 1.0, U, ALU.add, ALU.mult))
                    link("xsh", v_.tensor_tensor(U, U, SHF, ALU.add))
                    ve.wait_ge(p_pe.sem, p_pe.at(it, "tr0"))
                    ve.wait_ge(p_pe.sem, p_pe.at(it, "last", 1))
                    link("ut0", v_.tensor_copy(UT[:, 0:512], ps[0][:, :]))
                    ve.wait_ge(p_st.sem, p_st.at(it, "st", 1))
                    ve.wait_ge(p_pe.sem, p_pe.at(it, "D"))
                    link("gat", v_.tensor_copy(GAT, ps[5][0:32, 0:P]))
                    link("c4", v_.tensor_copy(CP[:, 2 * P:6 * P], ps[4][:, :]))
                    ve.wait_ge(p_pe.sem, p_pe.at(it, "gate"))
                    z, br = grp(Z, a=2), grp(BROW, a=2)
                    link("z0", v_.tensor_tensor(z[:, :, 0:128], grp(ps[1][:, 32:288], a=2), br[:, :, 0:128], ALU.add))
                    link("z1", v_.tensor_tensor(z[:, :, 128:132], grp(ps[1][:, 8:16], a=2), br[:, :, 128:132], ALU.add))
                    link("z2", v_.tensor_tensor(z[:, :, 132:140], grp(ps[1][:, 16:32], a=2), br[:, :, 132:140], ALU.add))
                    link("ig", v_.tensor_tensor(dirs[:, :, NDIR:NDIR + 4], grp(ps[1][:, 0:8], a=2),
                                                grp(BIG_, a=2), ALU.add))
                    link("zs", v_.tensor_tensor(Z, Z, SGN, ALU.mult))
                    link("za", v_.scalar_tensor_tensor(ZA, Z, -1.0, Z, ALU.mult, ALU.max))
                    ve.wait_ge(p_pe.sem, p_pe.at(it, "E"))
                    link("vg", v_.tensor_copy(TB[:, 0:256], ps[6][:, 0:256]))
                    link("vm", v_.tensor_copy(TB[:, 256:256 + VA].rearrange("p (h e) -> p h e", h=MH)[:, :, 0:HD],
                                              ps[6][:, 256:512].rearrange("p (h e) -> p h e", h=MH)))
                    ve.wait_ge(p_act.sem, p_act.at(it, "ln"))
                    link("sp", v_.scalar_tensor_tensor(Z, Z, 0.0, ZL, ALU.max, ALU.add))
                    link("la", v_.tensor_tensor(dirs[:, :, 0:NDIR], grp(Z, a=2), cf, ALU.mult))
                    link("dt", v_.tensor_copy(dirs[:, :, NDIR + 4:DB], grp(Z, a=2)[:, :, 132:140]))
                meet(ve, l * PHASES + 1)

                ve.wait_ge(c_par, (l + 1) * 32)
                ci, cv, cv2 = (t.rearrange("p (c n) -> p c n", c=6) for t in (CI, CV, CV2))
                ve.sem_inc(passed, 1)
                with ve.Fori(0, TILES) as s:
                    it = l * TILES + s
                    link = linker(ve, c_dve, it)
                    ve.wait_ge(c_ld.sem, c_ld.at(it, "ld"))
                    ve.wait_ge(c_act.sem, c_act.at(it, "silu", 1))
                    for c in range(6):
                        link(f"a{c}", v_.tensor_scalar(cv[:, c, :], ci[:, c, 0:P], CW[:, 3 * c:3 * c + 1], None, ALU.mult))
                        link(f"b{c}", v_.scalar_tensor_tensor(cv[:, c, :], ci[:, c, 1:P + 1], CW[:, 3 * c + 1:3 * c + 2],
                                                              cv[:, c, :], ALU.mult, ALU.add))
                        link(f"c{c}", v_.scalar_tensor_tensor(cv2[:, c, :], ci[:, c, 2:P + 2], CW[:, 3 * c + 2:3 * c + 3],
                                                              cv[:, c, :], ALU.mult, ALU.add))
                    ve.wait_ge(c_pe.sem, c_pe.at(it, "t1"))
                    ve.wait_ge(c_st.sem, c_st.at(it, "st", 1))
                    link("tok0", v_.tensor_copy(CTK[:, 0:512], ps[0][:, :]))
                    link("tok1", v_.tensor_copy(CTK[:, 512:640], ps[1][:, 0:P]))
                meet(ve, l * PHASES + 2)

                ve.wait_ge(s_con, (l + 1) * 80)
                ve.wait_ge(s_pad, (l + 1) * 6)
                ve.sem_inc(passed, 1)
                with ve.Fori(0, TILES) as s:
                    it = l * TILES + s
                    links = [linker(ve, s_dve[d], it) for d in (0, 1)]
                    V = [{k: x for k, x in sc[d].items()} for d in (0, 1)]

                    def hb(ap, h, n):
                        return ap.unsqueeze(2).broadcast_to([P, h, n])

                    for d in (0, 1):
                        b, L = V[d], links[d]
                        cs = b["CS"]
                        ve.wait_ge(s_pe[d].sem, s_pe[d].at(it, "cum"))
                        L("cs", v_.tensor_copy(cs[:, 0:153], ps[4 * d][:, 0:153]))
                        L("f4", v_.tensor_copy(b["F4"], ps[4 * d][0:4, 153:154]))
                        L("dec", v_.tensor_tensor(cs[:, 153:161], cs[:, 144:152], cs[:, 132:140], ALU.subtract))
                        L("g4", v_.tensor_tensor(b["G4"], b["TK"][:, 256 + VA + NDIR:256 + VA + NDIR + 4],
                                                 cs[:, 128:132], ALU.subtract))
                        for h in range(SH):
                            L(f"ex{h}", v_.tensor_scalar(b["EX"][:, h * P:(h + 1) * P],
                                                         ps[4 * d + 1 + h // 4][:, h % 4 * P:(h % 4 + 1) * P],
                                                         cs[:, 132 + h:133 + h], 0.0, ALU.subtract, ALU.min))
                    for d in (0, 1):
                        b, L = V[d], links[d]
                        cs = b["CS"]
                        ve.wait_ge(s_pe[d].sem, s_pe[d].at(it, "g4r"))
                        L("cbm", v_.tensor_tensor(grp(b["CBM"], a=2), grp(ps[4 * d + 3][:, 0:256], a=2),
                                                  TRI[d].unsqueeze(1).broadcast_to([P, 2, P]), ALU.mult))
                        L("g4r", v_.tensor_copy(b["G4R"], ps[4 * d][0:4, 0:P]))
                        L("r4", v_.tensor_tensor_scan(b["R4"], b["G4R"], b["G4R"], b["MC"], ALU.max, ALU.max))
                        mid = cs[:, BL // 2:P:BL]
                        kt = grp(b["KT"], a=NB)
                        L("kta", v_.tensor_tensor(kt, cs[:, 0:P].unsqueeze(1).broadcast_to([P, NB, P]),
                                                  hb(mid, NB, P), ALU.subtract))
                        L("ktb", v_.tensor_scalar(b["KT"], b["KT"], -CLAMP, None, ALU.max))
                        L("qba", v_.tensor_tensor(grp(b["QB"], a=NB), grp(cs[:, 0:P], a=NB), hb(mid, NB, BL),
                                                  ALU.subtract))
                        L("qbb", v_.tensor_scalar(b["QB"], b["QB"], CLAMP, None, ALU.min))
                    for d in (0, 1):
                        b, L = V[d], links[d]
                        gqT, gkT = b["FT"][:, 0:P], b["FT"][:, P:2 * P]
                        ve.wait_ge(s_pe[d].sem, s_pe[d].at(it, "km"))
                        L("gg8", v_.tensor_copy(b["GG8"], ps[4 * d][:, 128:136]))
                        ve.wait_ge(s_act[d].sem, s_act[d].at(it, "kd"))
                        L("qh", v_.tensor_tensor(b["QH"], b["EB"], gqT, ALU.mult))
                        L("kdm", v_.tensor_tensor(b["KD"], b["KD"], gkT, ALU.mult))
                        ve.wait_ge(s_act[d].sem, s_act[d].at(it, "qb"))
                        for h in range(GH):
                            r = slice(GDK * h, GDK * h + GDK)
                            L(f"qp{h}", v_.tensor_tensor(
                                b["QP"][r, :].rearrange("p (b h i) -> p b h i", b=NB, h=GH)[:, :, h, :],
                                b["QB"][r, :].rearrange("p (b i) -> p b i", b=NB),
                                b["FT"][r, 0:P].rearrange("p (b i) -> p b i", b=NB), ALU.mult))
                        L("ktm", v_.tensor_tensor(grp(b["KT"], a=NB), grp(b["KT"], a=NB),
                                                  gkT.unsqueeze(1).broadcast_to([P, NB, P]), ALU.mult))
                    for d in (0, 1):
                        b, L = V[d], links[d]
                        cs, ema = b["CS"], b["EMA"]
                        ve.wait_ge(s_pe[d].sem, s_pe[d].at(it, "kdt"))
                        L("gt", v_.tensor_copy(b["GT"], ps[4 * d][:, 136:140]))
                        L("kmd", v_.tensor_copy(b["KMD"], ps[4 * d + 2][:, 0:3 * P]))
                        L("em0", v_.tensor_tensor(ema[:, 0:4], b["MB"], b["GT"], ALU.subtract))
                        L("em1", v_.scalar_tensor_tensor(ema[:, 4:8], cs[:, 128:132], -1.0, b["GT"],
                                                         ALU.mult, ALU.subtract))
                        L("em2", v_.tensor_tensor(ema[:, 8:12], b["G4"], b["GG8"][:, 4:8], ALU.subtract))
                        L("em3", v_.tensor_tensor(ema[:, 12:16], b["MB"], b["GG8"][:, 4:8], ALU.subtract))
                        ve.wait_ge(s_act[d].sem, s_act[d].at(it, "ex1"))
                        ex = b["EX"].rearrange("p (g r s) -> p g r s", g=2, r=4)
                        L("w8", v_.tensor_tensor(ex, ex, grp(b["CBM"], a=2).unsqueeze(2).broadcast_to([P, 2, 4, P]),
                                                 ALU.mult))
                        ve.wait_ge(s_act[d].sem, s_act[d].at(it, "ea"))
                        ve.wait_ge(s_pool[d].sem, s_pool[d].at(it, "xd"))
                        L("xw", v_.tensor_tensor(grp(b["XW"], a=SH), grp(b["XD"], a=SH),
                                                 hb(b["EA"][:, 21:29], SH, HD), ALU.mult))
                        ve.wait_ge(s_pe[d].sem, s_pe[d].at(it, "qk"))
                        L("qkm", v_.tensor_tensor(grp(b["T1"], a=4), grp(ps[4 * d + 3][:, :], a=4),
                                                  TRI[d].unsqueeze(1).broadcast_to([P, 4, P]), ALU.mult))
                    for d in (0, 1):
                        b, L = V[d], links[d]
                        ve.wait_ge(s_pe[d].sem, s_pe[d].at(it, "gb"))
                        for h in range(MH):
                            L(f"me{h}", v_.tensor_scalar(b["ME"][:, h * P:(h + 1) * P], ps[4 * d][:, h * P:(h + 1) * P],
                                                         b["G4"][:, h:h + 1], 0.0, ALU.subtract, ALU.max))
                        ve.wait_ge(s_pe[d].sem, s_pe[d].at(it, "ssd"))
                        ve.wait_ge(s_st[d].sem, s_st[d].at(it, "st", 1))
                        L("ys0", v_.tensor_tensor(grp(b["Y"][:, 512:], a=SH), grp(ps[4 * d + 2][:, :], a=SH),
                                                  hb(b["EA"][:, 0:8], SH, HD), ALU.mult))
                        L("ys1", v_.tensor_tensor(b["Y"][:, 512:], b["Y"][:, 512:], ps[4 * d + 1][:, :], ALU.add))
                    for d in (0, 1):
                        b, L = V[d], links[d]
                        ve.wait_ge(s_act[d].sem, s_act[d].at(it, "me"))
                        L("wm", v_.tensor_tensor(b["ME"], b["ME"], b["T1"], ALU.mult))
                        ve.wait_ge(s_pe[d].sem, s_pe[d].at(it, "att"))
                        L("at", v_.tensor_tensor(
                            b["AT"].rearrange("p (h b i) -> p h b i", h=GH, b=NB),
                            ps[4 * d][:, :].rearrange("p (b h i) -> p h b i", b=NB, h=GH),
                            TRI[d].rearrange("p (b i) -> p b i", b=NB).unsqueeze(1).broadcast_to([P, GH, NB, BL]),
                            ALU.mult))
                        ve.wait_ge(s_pe[d].sem, s_pe[d].at(it, "ups"))
                        L("t1", v_.tensor_tensor(b["T1"], ps[4 * d + 3][:, :], GM[:, S_SSD:S_ML], ALU.mult))
                    for d in (0, 1):
                        b, L = V[d], links[d]
                        sn, st, em = b["SN"], b["ST"], b["EM"]
                        ve.wait_ge(s_pe[d].sem, s_pe[d].at(it, "mli"))
                        L("hm0", v_.tensor_tensor(grp(b["HM"], a=MH), grp(ps[4 * d + 2][:, 0:VA], a=MH),
                                                  hb(em[:, 0:4], MH, HD + 1), ALU.mult))
                        L("hm1", v_.tensor_tensor(b["HM"], b["HM"], ps[4 * d + 1][:, 0:VA], ALU.add))
                        hm = grp(b["HM"], a=MH)
                        L("dn0", v_.scalar_tensor_tensor(b["DN"].unsqueeze(2), hm[:, :, HD:HD + 1], -1.0,
                                                         hm[:, :, HD:HD + 1], ALU.mult, ALU.max))
                        L("dn1", v_.tensor_tensor(b["DN"], b["DN"], em[:, 4:8], ALU.max))
                        L("rc", v_.reciprocal(b["RC"], b["DN"]))
                        L("ym", v_.tensor_tensor(grp(b["Y"][:, 256:512], a=MH), hm[:, :, 0:HD], hb(b["RC"], MH, HD), ALU.mult))
                        ve.wait_ge(s_pe[d].sem, s_pe[d].at(it, "upg"))
                        L("yg", v_.tensor_copy(b["Y"][:, 0:256], ps[4 * d][:, 0:256]))
                        L("t3", v_.tensor_tensor(b["T3"], ps[4 * d][:, 256:512], GM[:, S_GLA:S_W], ALU.mult))
                        L("sng", v_.scalar_tensor_tensor(sn[:, S_GLA:S_W], st[:, S_GLA:S_W], b["EA"][:, 20:21], b["T3"],
                                                         ALU.mult, ALU.add))
                        ve.wait_ge(s_pe[d].sem, s_pe[d].at(it, "upm"))
                        L("t2", v_.tensor_tensor(b["T2"], ps[4 * d + 3][:, 0:VA], GM[:, S_ML:S_GLA], ALU.mult))
                        L("last", v_.tensor_tensor(b["MN"], b["F4"], b["R4"][:, P - 1:P], ALU.add))
                meet(ve, l * PHASES + 3)

                ve.wait_ge(o_par, (l + 1) * 144)
                ve.sem_inc(passed, 1)
                with ve.Fori(0, TILES) as s:
                    it, p = l * TILES + s, pos(s)
                    link = linker(ve, o_dve, it)
                    ve.wait_ge(o_ld.sem, o_ld.at(it, "ld"))
                    yf = YF
                    link("y0", v_.tensor_tensor(yf, YF, YB, ALU.add))
                    tx = grp(TX3, a=SH)
                    link("y1", v_.tensor_tensor(tx, tx, DROW.unsqueeze(2).broadcast_to([P, SH, HD]), ALU.mult))
                    link("y2", v_.tensor_tensor(yf[:, 512:], yf[:, 512:], TX3, ALU.add))
                    link("y3", v_.tensor_tensor(yf, yf, GO, ALU.mult))
                    link("sq", v_.tensor_tensor(SQ, yf, yf, ALU.mult))
                    link("hr", v_.tensor_reduce(HR, grp(SQ, a=16), AX, ALU.add))
                    link("hrm", v_.tensor_scalar(HR2, HR, 1.0 / HD, EPS, ALU.mult, ALU.add))
                    ve.wait_ge(o_act.sem, o_act.at(it, "hsd"))
                    link("hrr", v_.reciprocal(HR3, HR3))
                    link("yn1", v_.tensor_tensor(grp(yf, a=16), grp(yf, a=16),
                                                 HR3.unsqueeze(2).broadcast_to([P, 16, HD]), ALU.mult))
                    link("yn2", v_.tensor_tensor(yf, yf, GNW, ALU.mult))
                    ve.wait_ge(o_pe.sem, o_pe.at(it, "yt0"))
                    link("yt0", v_.tensor_copy(YT[:, 0:512], ps[0][:, :]))
                    ve.wait_ge(o_pe.sem, o_pe.at(it, "out"))
                    ve.wait_ge(o_ldx.sem, o_ldx.at(it, "ld"))
                    for h in (0, 1):
                        c = slice(512 * h, 512 * h + 512)
                        link(f"g{h}", v_.tensor_tensor(G1[:, c], ps[2 + h][:, :], G1[:, c], ALU.mult))
                    link("r1", v_.scalar_tensor_tensor(XO, XO, ALPHA, G1, ALU.mult, ALU.add))
                    norm_stats.tag = "a"
                    norm_stats(link, XO, oST6, oMV)
                    ve.wait_ge(o_act.sem, o_act.at(it, "sda"))
                    link("rsa", v_.reciprocal(oRS, oSD))
                    link("x1a", v_.tensor_scalar(XO, XO, oMV[:, 0:1], oRS, ALU.subtract, ALU.mult))
                    link("x1b", v_.tensor_tensor(XO, XO, L1W, ALU.mult))
                    link("x1c", v_.tensor_tensor(XO, XO, L1B, ALU.add))
                    norm_stats.tag = "b"
                    norm_stats(link, XO, oST6, oMV)
                    norm_stats.tag = ""
                    ve.wait_ge(o_act.sem, o_act.at(it, "sdb"))
                    link("rsb", v_.reciprocal(oRS, oSD))
                    link("u2a", v_.tensor_scalar(G1, XO, oMV[:, 0:1], oRS, ALU.subtract, ALU.mult))
                    link("u2b", v_.scalar_tensor_tensor(SC2, SC2, 1.0, G1, ALU.add, ALU.mult))
                    link("u2c", v_.tensor_tensor(SC2, SC2, SH2, ALU.add))
                    ve.wait_ge(o_pe.sem, o_pe.at(it, "ut0"))
                    link("ut0", v_.tensor_copy(U2T[:, 0:512], ps[4][:, :]))
                    ve.wait_ge(o_pe.sem, o_pe.at(it, "q0"))
                    link("qt0", v_.tensor_copy(QT[:, 0:512], ps[0][:, :]))
                    ve.wait_ge(o_act.sem, o_act.at(it, "sc3"))
                    NEG = -3.0e38
                    for i in range(16):
                        sco, tv, ti = SCO[:, i * P:(i + 1) * P], TV[:, 16 * i:16 * i + 16], \
                            TI[:, 16 * i:16 * i + 16].bitcast(U32)
                        ve.sem_inc(passed, 1)
                        link(f"ma{i}", v_.max(tv[:, 0:8], sco))
                        ve.sem_inc(passed, 1)
                        link(f"mb{i}", v_.max_index(ti[:, 0:8], tv[:, 0:8], sco))
                        ve.sem_inc(passed, 1)
                        link(f"mc{i}", v_.match_replace(sco, tv[:, 0:8], sco, NEG))
                        ve.sem_inc(passed, 1)
                        link(f"md{i}", v_.max(tv[:, 8:16], sco))
                        ve.sem_inc(passed, 1)
                        link(f"mf{i}", v_.max_index(ti[:, 8:16], tv[:, 8:16], sco))
                    link("tf", v_.tensor_copy(TF, TI.bitcast(U32)))
                    tv4 = TV.rearrange("p (h q a) -> p h q a", h=HEADS, q=2)
                    tf4 = TF.rearrange("p (h q a) -> p h q a", h=HEADS, q=2)
                    can4 = CAN.rearrange("p (h a b) -> p h a b", h=HEADS, a=TOPK)
                    oh4 = OH.rearrange("p (h a b) -> p h a b", h=HEADS, a=TOPK)
                    full = [P, HEADS, TOPK, TOPK]
                    link("can", v_.tensor_tensor(can4, tv4[:, :, 0, :].unsqueeze(3).broadcast_to(full),
                                                 tv4[:, :, 1, :].unsqueeze(2).broadcast_to(full), ALU.add))
                    for h in range(HEADS):
                        can, bv, bi = CAN[:, h * 256:(h + 1) * 256], BV[:, 16 * h:16 * h + 16], \
                            BI[:, 16 * h:16 * h + 16].bitcast(U32)
                        ve.sem_inc(passed, 1)
                        link(f"na{h}", v_.max(bv[:, 0:8], can))
                        ve.sem_inc(passed, 1)
                        link(f"nb{h}", v_.max_index(bi[:, 0:8], bv[:, 0:8], can))
                        ve.sem_inc(passed, 1)
                        link(f"nc{h}", v_.match_replace(can, bv[:, 0:8], can, NEG))
                        ve.sem_inc(passed, 1)
                        link(f"nd{h}", v_.max(bv[:, 8:16], can))
                        ve.sem_inc(passed, 1)
                        link(f"ne{h}", v_.max_index(bi[:, 8:16], bv[:, 8:16], can))
                    link("ba", v_.tensor_scalar(BA1.bitcast(U32), BI.bitcast(U32), 4, None, ALU.logical_shift_right))
                    link("bb", v_.tensor_scalar(BB1.bitcast(U32), BI.bitcast(U32), 15, None, ALU.bitwise_and))
                    link("baf", v_.tensor_copy(BAF, BA1.bitcast(U32)))
                    link("bbf", v_.tensor_copy(BBF, BB1.bitcast(U32)))
                    for q, (src, dst) in enumerate(((BAF, IFR), (BBF, JFR))):
                        link(f"oh{q}", v_.tensor_tensor(grp(OH, a=P), src.unsqueeze(2).broadcast_to([P, P, TOPK]),
                                                        IOTA.unsqueeze(1).broadcast_to([P, P, TOPK]), ALU.is_equal))
                        link(f"oi{q}", v_.tensor_tensor(oh4, oh4, tf4[:, :, q, :].unsqueeze(2).broadcast_to(full), ALU.mult))
                        link(f"oj{q}", v_.tensor_reduce(dst, grp(OH, a=P), AX, ALU.add))
                    link("ixa", v_.scalar_tensor_tensor(IFR, IFR, 128.0, JFR, ALU.mult, ALU.add))
                    link("ixb", v_.tensor_scalar(idx_all.bitcast(U32)[:, bass.ds(p * SLOTS, SLOTS)], IFR, LOFS, None, ALU.add))
                    bv3 = grp(BV, a=HEADS)
                    link("sma", v_.tensor_tensor(grp(JFR, a=HEADS), bv3, bv3[:, :, 0:1].broadcast_to([P, HEADS, TOPK]),
                                                 ALU.subtract))
                    ve.wait_ge(o_act.sem, o_act.at(it, "sme"))
                    link("smb", v_.tensor_reduce(SM, grp(IFR, a=HEADS), AX, ALU.add))
                    link("smc", v_.reciprocal(SR, SM))
                    link("smd", v_.tensor_tensor(grp(gw_all[:, bass.ds(p * SLOTS, SLOTS)], a=HEADS), grp(IFR, a=HEADS),
                                                 SR.unsqueeze(2).broadcast_to([P, HEADS, TOPK]), ALU.mult))
                meet(ve, l * PHASES + 4)

                ve.wait_ge(e_par, (l + 1) * 32)
                ve.sem_inc(passed, 1)
                with ve.Fori(0, TILES) as s:
                    it = l * TILES + s
                    tl = linker(ve, et_dve, it)
                    tl("zero", v_.memset(ACC, 0.0))
                    ve.wait_ge(e_u.sem, e_u.at(it, "u"))
                    ve.sem_inc(passed, 1)
                    with ve.Fori(0, HEADS // 2) as hh:
                        jt = it * (HEADS // 2) + hh
                        link = linker(ve, e_dve, jt)

                        def dots(g):
                            for i in range(4):
                                n = 4 * g + i
                                u, j = divmod(n, TOPK)
                                ve.wait_ge(e_gat[j].sem, e_gat[j].at(jt, f"g{u}"))
                                link(f"dot{n}", v_.tensor_tensor_reduce(
                                    ring[:, j, 0:D], ring[:, j, 0:D], EU, 1.0, 0.0, ALU.mult, ALU.add, DOT[:, n:n + 1]))

                        def weigh(g):
                            ve.wait_ge(e_act.sem, e_act.at(jt, f"ge{g}"))
                            ve.wait_ge(e_pool.sem, e_pool.at(jt, f"gw{g // 4}"))
                            link(f"aw{g}", v_.tensor_tensor(AW[:, 4 * g:4 * g + 4], AG[:, 4 * g:4 * g + 4],
                                                            GWH[:, 4 * g:4 * g + 4], ALU.mult))

                        def gather_sum(u):
                            ve.wait_ge(e_pe.sem, e_pe.at(jt, f"v{TOPK * u + TOPK - 1}"))
                            for h in (0, 1):
                                c = slice(512 * h, 512 * h + 512)
                                link(f"acc{u}{h}", v_.tensor_tensor(ACC[:, c], ACC[:, c], ps[2 * u + h][:, :], ALU.add))

                        dots(0)
                        for g in range(1, 8):
                            dots(g)
                            weigh(g - 1)
                            if g == 6:
                                gather_sum(0)
                        weigh(7)
                        gather_sum(1)
                    ve.wait_ge(e_x.sem, e_x.at(it, "x"))
                    tl("r0", v_.tensor_tensor(ACC, ACC, EG2, ALU.mult))
                    tl("r1", v_.scalar_tensor_tensor(EX1, EX1, ALPHA, ACC, ALU.mult, ALU.add))
                    norm_stats(tl, EX1, eST6, eMV)
                    ve.wait_ge(et_act.sem, et_act.at(it, "sd"))
                    tl("r2", v_.reciprocal(eRS, eSD))
                    tl("xa", v_.tensor_scalar(EX1, EX1, eMV[:, 0:1], eRS, ALU.subtract, ALU.mult))
                    tl("xw", v_.tensor_tensor(EX1, EX1, L2W, ALU.mult))
                    tl("xb", v_.tensor_tensor(EX1, EX1, L2B, ALU.add))
                meet(ve, l * PHASES + 5)

        @block.scalar
        def _(ae):
            give_credit(ae, act_own)
            a_ = nc.scalar

            ae.wait_ge(start_ld, 32)
            ae.activation(CS2, CT, ACT.Silu).then_inc(sem_silu, 1)
            ae.wait_ge(sem_ones, 2)
            meet(ae, 0)
            ae.sem_inc(passed, 1)
            with ae.Fori(0, DEPTH) as l:
                link = linker(ae, pl_act, l)
                ae.wait_ge(p_par, (l + 1) * 96)
                link("ea", a_.activation(ALOG, ALOG, ACT.Exp))
                ae.sem_inc(passed, 1)
                with ae.Fori(0, TILES) as s:
                    it = l * TILES + s
                    link = linker(ae, p_act, it)
                    ae.wait_ge(p_dve.sem, p_dve.at(it, "mv"))
                    link("sd", a_.activation(SD, MV[:, 1:2], ACT.Sqrt, bias=eps))
                    ae.wait_ge(p_pe.sem, p_pe.at(it, "tr1"))
                    ae.wait_ge(p_pe.sem, p_pe.at(it, "last", 1))
                    link("ut1", a_.activation(UT[:, 512:1024], ps[1][:, :], ACT.Copy))
                    ae.wait_ge(p_pe.sem, p_pe.at(it, "A"))
                    ae.wait_ge(p_st.sem, p_st.at(it, "st", 1))
                    link("a1", a_.activation(FA[:, 0:P], ps[2][:, 0:P], ACT.Copy, scale=GDK ** -0.5))
                    link("a2", a_.activation(FA[:, P:4 * P], ps[2][:, P:4 * P], ACT.Copy))
                    ae.wait_ge(p_pe.sem, p_pe.at(it, "B"))
                    link("b1", a_.activation(CP[:, 0:2 * P], ps[3][:, 2 * P:4 * P], ACT.Copy))
                    link("b2", a_.activation(FA[:, 4 * P:6 * P], ps[3][:, 0:2 * P], ACT.Copy, scale=HD ** -0.5))
                    ae.wait_ge(p_dve.sem, p_dve.at(it, "za"))
                    link("ze", a_.activation(ZA, ZA, ACT.Exp, scale=-1.0))
                    link("ln", a_.activation(ZL, ZA, ACT.Ln, bias=ones[:, 0:1]))
                    ae.wait_ge(p_pe.sem, p_pe.at(it, "last"))
                    link("silug", a_.activation(GG[:, 0:256], ps[7][:, 0:256], ACT.Silu))
                    link("siluz", a_.activation(GG[:, 512:1024], ps[0][:, :], ACT.Silu))
                    link("sigmo", a_.activation(GG[:, 256:512], ps[7][:, 256:512], ACT.Sigmoid))
                meet(ae, l * PHASES + 1)

                ae.wait_ge(c_par, (l + 1) * 32)
                ae.sem_inc(passed, 1)
                with ae.Fori(0, TILES) as s:
                    it = l * TILES + s
                    link = linker(ae, c_act, it)
                    ae.wait_ge(c_pe.sem, c_pe.at(it, "t1", 1))
                    ae.wait_ge(c_st.sem, c_st.at(it, "st", 1))
                    for c in range(6):
                        ae.wait_ge(c_dve.sem, c_dve.at(it, f"c{c}"))
                        link(f"silu{c}" if c < 5 else "silu",
                             a_.activation(CO[:, c * P:(c + 1) * P], CV2[:, c * P:(c + 1) * P], ACT.Silu,
                                           bias=CB_[:, c:c + 1]))
                meet(ae, l * PHASES + 2)

                ae.sem_inc(passed, 1)
                with ae.Fori(0, TILES) as s:
                    it = l * TILES + s
                    links = [linker(ae, s_act[d], it) for d in (0, 1)]
                    for d in (0, 1):
                        b, L = sc[d], links[d]
                        cs = b["CS"]
                        ae.wait_ge(s_dve[d].sem, s_dve[d].at(it, "dec"))
                        L("ea", a_.activation(b["EA"], cs[:, 132:161], ACT.Exp))
                        L("eb", a_.activation(b["EB"], cs[:, 0:P], ACT.Exp))
                        L("kd", a_.activation(b["KD"], cs[:, 0:P], ACT.Exp, bias=cs[:, 152:153], scale=-1.0))
                        for q in (0, 1):
                            ae.wait_ge(s_dve[d].sem, s_dve[d].at(it, f"ex{4 * q + 3}"))
                            L(f"ex{q}", a_.activation(b["EX"][:, 512 * q:512 * q + 512],
                                                      b["EX"][:, 512 * q:512 * q + 512], ACT.Exp))
                    for d in (0, 1):
                        b, L = sc[d], links[d]
                        ae.wait_ge(s_dve[d].sem, s_dve[d].at(it, "qbb"))
                        L("kt", a_.activation(b["KT"], b["KT"], ACT.Exp, scale=-1.0))
                        L("qb", a_.activation(b["QB"], b["QB"], ACT.Exp))
                    for d in (0, 1):
                        b, L = sc[d], links[d]
                        ae.wait_ge(s_dve[d].sem, s_dve[d].at(it, "em3"))
                        L("em", a_.activation(b["EM"], b["EMA"], ACT.Exp))
                    for d in (0, 1):
                        b, L = sc[d], links[d]
                        ae.wait_ge(s_dve[d].sem, s_dve[d].at(it, "me3"))
                        L("me", a_.activation(b["ME"], b["ME"], ACT.Exp, scale=-1.0))
                meet(ae, l * PHASES + 3)

                ae.sem_inc(passed, 1)
                with ae.Fori(0, TILES) as s:
                    it = l * TILES + s
                    link = linker(ae, o_act, it)
                    ae.wait_ge(o_dve.sem, o_dve.at(it, "hrm"))
                    link("hsd", a_.activation(HR3, HR2, ACT.Sqrt))
                    ae.wait_ge(o_pe.sem, o_pe.at(it, "yt1"))
                    link("yt1", a_.activation(YT[:, 512:1024], ps[1][:, :], ACT.Copy))
                    ae.wait_ge(o_dve.sem, o_dve.at(it, "mva"))
                    link("sda", a_.activation(oSD, oMV[:, 1:2], ACT.Sqrt, bias=eps))
                    ae.wait_ge(o_dve.sem, o_dve.at(it, "mvb"))
                    link("sdb", a_.activation(oSD, oMV[:, 1:2], ACT.Sqrt, bias=eps))
                    ae.wait_ge(o_pe.sem, o_pe.at(it, "ut1"))
                    link("ut1", a_.activation(U2T[:, 512:1024], ps[5][:, :], ACT.Copy))
                    ae.wait_ge(o_pe.sem, o_pe.at(it, "q1"))
                    link("qt1", a_.activation(QT[:, 512:1024], ps[1][:, :], ACT.Copy))
                    for b in range(4):
                        ae.wait_ge(o_pe.sem, o_pe.at(it, f"s{b}"))
                        link(f"sc{b}", a_.activation(SCO[:, 512 * b:512 * b + 512], ps[(2, 3, 4, 5)[b]][:, :], ACT.Copy))
                    ae.wait_ge(o_dve.sem, o_dve.at(it, "sma"))
                    link("sme", a_.activation(IFR, JFR, ACT.Exp))
                meet(ae, l * PHASES + 4)

                ae.sem_inc(passed, 1)
                with ae.Fori(0, TILES) as s:
                    it = l * TILES + s
                    ae.sem_inc(passed, 1)
                    with ae.Fori(0, HEADS // 2) as hh:
                        jt = it * (HEADS // 2) + hh
                        link = linker(ae, e_act, jt)

                        def gelu(g):
                            ae.wait_ge(e_dve.sem, e_dve.at(jt, f"dot{4 * g + 3}"))
                            link(f"ge{g}", a_.activation(AG[:, 4 * g:4 * g + 4], DOT[:, 4 * g:4 * g + 4], ACT.Gelu))

                        def diag(g):
                            ae.wait_ge(e_dve.sem, e_dve.at(jt, f"aw{g}"))
                            for i in range(4):
                                n = 4 * g + i
                                if n < 8:
                                    ae.wait_ge(e_pe.sem, e_pe.at(jt, f"v{n + 24}", 1))
                                else:
                                    ae.wait_ge(e_pe.sem, e_pe.at(jt, f"v{n - 8}"))
                                link(f"dg{n}", a_.activation(DG[:, n % 8 * P:(n % 8 + 1) * P], ident, ACT.Copy,
                                                             scale=AW[:, n:n + 1]))
                        gelu(0)
                        for g in range(1, 8):
                            gelu(g)
                            diag(g - 1)
                        diag(7)
                    tl = linker(ae, et_act, it)
                    ae.wait_ge(et_dve.sem, et_dve.at(it, "mv"))
                    tl("sd", a_.activation(eSD, eMV[:, 1:2], ACT.Sqrt, bias=eps))
                meet(ae, l * PHASES + 5)

        @block.tensor
        def _(pe):
            give_credit(pe, pe_own)
            mm = nc.tensor.matmul

            pe.wait_ge(sem_silu, 1)
            pe.wait_ge(sem_ones, 2)
            pe.sem_inc(passed, 1)
            with pe.Fori(0, DEPTH) as l:
                pe.sem_inc(passed, 1)
                with pe.Fori(0, 6) as jj:
                    it = l * 6 + jj
                    mark = marker(m_pe)
                    for u in (0, 1):
                        pe.wait_ge(m_w[u].sem, m_w[u].at(it, "w"))
                        pe.wait_ge(m_dve.sem, m_dve.at(it, f"mod{u}", 1))
                        for k in range(KC):
                            i = mm(ps[u][0:2, :], CS2[:, 2 * k:2 * k + 2], WA[u][:, 512 * k:512 * k + 512],
                                   start=(k == 0), stop=(k == KC - 1))
                        mark(f"mod{u}", i)
            meet(pe, 0)

            def turn(bank, src, first):
                for c in range(4):
                    i = nc.tensor.transpose(bank[:, c * P:(c + 1) * P], src[:, (first + c) * P:(first + c + 1) * P], ident)
                return i

            pe.sem_inc(passed, 1)
            with pe.Fori(0, DEPTH) as l:
                pe.wait_ge(p_w, (l + 1) * 16 * KC)
                pe.wait_ge(p_par, (l + 1) * 96)
                pe.sem_inc(passed, 1)
                with pe.Fori(0, TILES) as s:
                    it = l * TILES + s
                    mark = marker(p_pe)
                    pe.wait_ge(p_dve.sem, p_dve.at(it, "xsh"))
                    pe.wait_ge(p_act.sem, p_act.at(it, "sigmo", 1))
                    pe.wait_ge(p_dve.sem, p_dve.at(it, "dt", 1))
                    mark("tr0", turn(ps[0], U, 0))
                    mark("tr1", turn(ps[1], U, 4))
                    pe.wait_ge(p_dve.sem, p_dve.at(it, "ut0"))
                    pe.wait_ge(p_act.sem, p_act.at(it, "ut1"))

                    def feature_major(bank, blocks):
                        for q, (c0, m) in enumerate(blocks):
                            for k in range(KC):
                                i = mm(bank[0:m, q * P:(q + 1) * P], win[:, k, c0:c0 + m], UT[:, k * P:(k + 1) * P],
                                       start=(k == 0), stop=(k == KC - 1))
                        return i

                    def token_major(out, c0, n):
                        for k in range(KC):
                            i = mm(out, UT[:, k * P:(k + 1) * P], win[:, k, c0:c0 + n], start=(k == 0), stop=(k == KC - 1))
                        return i

                    mark("A", feature_major(ps[2], [(O_GQ, P), (O_GK, P), (O_MQ, P), (O_MQ + P, P)]))
                    mark("B", feature_major(ps[3], [(O_MK, P), (O_MK + P, P), (O_SX, P), (O_SX + P, P)]))
                    mark("C", feature_major(ps[4], [(O_SX + 2 * P, P), (O_SX + 3 * P, P), (O_SB, P), (O_SB + P, P)]))
                    mark("D", feature_major(ps[5], [(O_GA, 32)]))
                    token_major(ps[1][:, 0:16], O_MI, 16)
                    token_major(ps[1][:, 16:32], O_SDT, 16)
                    mark("E1", token_major(ps[6][:, 0:256], O_GV, 256))
                    mark("E", token_major(ps[6][:, 256:512], O_MV, 256))
                    pe.wait_ge(p_dve.sem, p_dve.at(it, "gat"))
                    mark("gate", mm(ps[1][:, 32:288], GAT, WA2, start=True, stop=True))
                    token_major(ps[7][:, 0:256], O_GG, 256)
                    token_major(ps[7][:, 256:512], O_MO, 256)
                    mark("last", token_major(ps[0][:, :], O_SZ, 512))
                meet(pe, l * PHASES + 1)

                pe.sem_inc(passed, 1)
                with pe.Fori(0, TILES) as s:
                    it = l * TILES + s
                    mark = marker(c_pe)
                    pe.wait_ge(c_act.sem, c_act.at(it, "silu"))
                    pe.wait_ge(c_dve.sem, c_dve.at(it, "tok1", 1))
                    mark("t0", turn(ps[0], CO, 0))
                    mark("t1", nc.tensor.transpose(ps[1][:, 0:P], CO[:, 4 * P:5 * P], ident))
                meet(pe, l * PHASES + 2)

                pe.wait_ge(s_con, (l + 1) * 80)
                pe.sem_inc(passed, 1)
                with pe.Fori(0, TILES) as s:
                    it = l * TILES + s
                    marks = [marker(s_pe[d]) for d in (0, 1)]
                    i4 = ident[0:4, 0:4]
                    for d in (0, 1):
                        b, M = sc[d], marks[d]
                        la = b["TK"][:, 256 + VA:256 + VA + NDIR]
                        b0, b1, b2, b3 = ps[4 * d:4 * d + 4]
                        pe.wait_ge(s_ld[d].sem, s_ld[d].at(it, "ld"))
                        pe.wait_ge(s_dve[d].sem, s_dve[d].at(it, "last", 1))
                        mm(b0[:, 0:P], la[:, 0:P], TRI[d], start=True, stop=True)
                        mm(b0[:, 128:140], TRI[d], la[:, P:NDIR], start=True, stop=True)
                        mm(b0[:, 140:152], ones, la[:, P:NDIR], start=True, stop=True)
                        mm(b0[:, 152:153], la[:, 0:P], ones[:, 0:1], start=True, stop=True)
                        mm(b0[0:4, 153:154], la[:, 128:132], ones[:, 0:1], start=True, stop=True)
                        for h in range(SH):
                            i = mm((b1, b2)[h // 4][:, h % 4 * P:(h % 4 + 1) * P],
                                   la[:, 132 + h:133 + h].broadcast_to([P, P]), TRI[d], start=True, stop=True)
                        M("cum", i)
                    for d in (0, 1):
                        b, M = sc[d], marks[d]
                        b0, b1, b2, b3 = ps[4 * d:4 * d + 4]
                        pe.wait_ge(s_ls[d].sem, s_ls[d].at(it, "ls"))
                        pe.wait_ge(s_pool[d].sem, s_pool[d].at(it, "qm1"))
                        pe.wait_ge(s_dve[d].sem, s_dve[d].at(it, "g4"))
                        mm(b3[:, 0:256], b["FX"][:, 0:P], b["CTP"], start=True, stop=True)
                        M("g4r", mm(b0[0:4, 0:P], b["G4"], PERM[d], start=True, stop=True))
                    for d in (0, 1):
                        b, M = sc[d], marks[d]
                        b0, b1, b2, b3 = ps[4 * d:4 * d + 4]
                        pe.wait_ge(s_dve[d].sem, s_dve[d].at(it, "r4"))
                        mm(b0[:, 128:132], b["R4"], i4, start=True, stop=True)
                        mm(b0[:, 132:136], b["R4"][:, P - 1:P].broadcast_to([4, P]), i4, start=True, stop=True)
                        pe.wait_ge(s_dve[d].sem, s_dve[d].at(it, "ex7"))
                        nc.tensor.transpose(b2[:, 0:P], b["FT"][:, 4 * P:5 * P], ident)
                        M("km", nc.tensor.transpose(b2[:, P:2 * P], b["FT"][:, 5 * P:6 * P], ident))
                        for j in (0, 1):
                            i = mm(b3[:, 256 * j:256 * j + 256], b["FT"][:, (4 + j) * P:(5 + j) * P],
                                   b["QMP"][:, 256 * j:256 * j + 256], start=True, stop=True)
                        M("qk", i)
                    for d in (0, 1):
                        b, M = sc[d], marks[d]
                        b0, b1, b2, b3 = ps[4 * d:4 * d + 4]
                        pe.wait_ge(s_dve[d].sem, s_dve[d].at(it, "kdm"))
                        mm(b0[:, 136:140], PERM[d], b["GG8"][:, 0:4], start=True, stop=True)
                        M("kdt", nc.tensor.transpose(b2[:, 2 * P:3 * P], b["KD"], ident))
                    for d in (0, 1):
                        b, M = sc[d], marks[d]
                        b0, b1, b2, b3 = ps[4 * d:4 * d + 4]
                        pe.wait_ge(s_dve[d].sem, s_dve[d].at(it, "kmd"))
                        for h in range(MH):
                            i = mm(b0[:, h * P:(h + 1) * P], b["GT"][:, h:h + 1].broadcast_to([P, P]), ident,
                                   start=True, stop=True)
                        M("gb", i)
                        pe.wait_ge(s_dve[d].sem, s_dve[d].at(it, "w8"))
                        pe.wait_ge(s_pool[d].sem, s_pool[d].at(it, "xd"))
                        for h in range(SH):
                            mm(b1[:, h * HD:(h + 1) * HD], b["EX"][:, h * P:(h + 1) * P], b["XD"][:, h * HD:(h + 1) * HD],
                               start=True, stop=True)
                        M("ssd", mm(b2[:, :], b["FX"][:, P:2 * P], b["ST"][:, S_SSD:S_ML], start=True, stop=True))
                    for d in (0, 1):
                        b, M = sc[d], marks[d]
                        b0, b1, b2, b3 = ps[4 * d:4 * d + 4]
                        pe.wait_ge(s_dve[d].sem, s_dve[d].at(it, "me3"))
                        for c in range(NB):
                            i = mm(b0[:, c * GH * BL:(c + 1) * GH * BL], b["KT"][:, c * P:(c + 1) * P],
                                   b["QP"][:, c * GH * BL:(c + 1) * GH * BL], start=True, stop=True)
                        M("att", i)
                        M("ups", mm(b3[:, :], b["TX"][:, 512:640], b["XW"], start=True, stop=True))
                    for d in (0, 1):
                        b, M = sc[d], marks[d]
                        b0, b1, b2, b3 = ps[4 * d:4 * d + 4]
                        pe.wait_ge(s_dve[d].sem, s_dve[d].at(it, "wm"))
                        va = b["TK"][:, 256:256 + VA]
                        for h in range(MH):
                            mm(b1[:, h * 65:h * 65 + 65], b["ME"][:, h * P:(h + 1) * P], va[:, h * 65:h * 65 + 65],
                               start=True, stop=True)
                        for j in (0, 1):
                            i = mm(b2[:, 130 * j:130 * j + 130], b["FT"][:, (2 + j) * P:(3 + j) * P],
                                   b["ST"][:, S_ML + 130 * j:S_ML + 130 * j + 130], start=True, stop=True)
                        M("mli", i)
                        pe.wait_ge(s_dve[d].sem, s_dve[d].at(it, "t1"))
                        mm(b0[:, 0:256], b["QH"], b["ST"][:, S_GLA:S_W], start=True, stop=False)
                        for h in range(GH):
                            mm(b0[:, h * HD:(h + 1) * HD], b["AT"][:, h * P:(h + 1) * P], b["TK"][:, h * HD:(h + 1) * HD],
                               start=False, stop=(h == GH - 1))
                        M("upg", mm(b0[:, 256:512], b["KMD"][:, 2 * P:3 * P], b["TK"][:, 0:256], start=True, stop=True))
                        pe.wait_ge(s_pool[d].sem, s_pool[d].at(it, "vw"))
                        for j in (0, 1):
                            i = mm(b3[:, 130 * j:130 * j + 130], b["KMD"][:, j * P:(j + 1) * P],
                                   b["VW"][:, 130 * j:130 * j + 130], start=True, stop=True)
                        M("upm", i)
                meet(pe, l * PHASES + 3)

                pe.wait_ge(o_par, (l + 1) * 144)
                pe.sem_inc(passed, 1)
                with pe.Fori(0, TILES) as s:
                    it = l * TILES + s
                    mark = marker(o_pe)
                    pe.wait_ge(o_dve.sem, o_dve.at(it, "yn2"))
                    mark("yt0", turn(ps[0], YF, 0))
                    mark("yt1", turn(ps[1], YF, 4))
                    pe.wait_ge(o_dve.sem, o_dve.at(it, "yt0"))
                    pe.wait_ge(o_act.sem, o_act.at(it, "yt1"))
                    for h in (0, 1):
                        for k in range(KC):
                            i = mm(ps[2 + h][:, :], YT[:, k * P:(k + 1) * P], wo[:, k, 512 * h:512 * h + 512],
                                   start=(k == 0), stop=(k == KC - 1))
                    mark("out", i)
                    pe.wait_ge(o_dve.sem, o_dve.at(it, "u2c"))
                    mark("ut0", turn(ps[4], SC2, 0))
                    mark("ut1", turn(ps[5], SC2, 4))
                    pe.wait_ge(o_dve.sem, o_dve.at(it, "ut0"))
                    pe.wait_ge(o_act.sem, o_act.at(it, "ut1"))
                    for b in (0, 1):
                        for q in range(4):
                            h = 4 * b + q
                            for k in range(KC):
                                i = mm(ps[b][:, q * P:(q + 1) * P], wq[:, k, h * P:(h + 1) * P], U2T[:, k * P:(k + 1) * P],
                                       start=(k == 0), stop=(k == KC - 1))
                        mark(f"q{b}", i)
                    pe.wait_ge(o_dve.sem, o_dve.at(it, "qt0"))
                    pe.wait_ge(o_act.sem, o_act.at(it, "qt1"))
                    for b in range(4):
                        for q in (0, 1):
                            h = 2 * b + q
                            i = mm(ps[(2, 3, 4, 5)[b]][:, 256 * q:256 * q + 256], QT[:, h * P:(h + 1) * P], KEYS,
                                   start=True, stop=True)
                        mark(f"s{b}", i)
                meet(pe, l * PHASES + 4)

                pe.sem_inc(passed, 1)
                with pe.Fori(0, TILES) as s:
                    it = l * TILES + s
                    pe.sem_inc(passed, 1)
                    with pe.Fori(0, HEADS // 2) as hh:
                        jt = it * (HEADS // 2) + hh
                        mark = marker(e_pe)
                        for n in range(2 * TOPK):
                            u, j = divmod(n, TOPK)
                            if j == 0:
                                pe.wait_ge(e_dve.sem, e_dve.at(jt, f"acc{u}1", 1))
                            pe.wait_ge(e_act.sem, e_act.at(jt, f"dg{n}"))
                            for h in (0, 1):
                                i = mm(ps[2 * u + h][:, :], DG[:, n % 8 * P:(n % 8 + 1) * P],
                                       ring[:, j, D + 512 * h:D + 512 * h + 512], start=(j == 0), stop=(j == TOPK - 1))
                            mark(f"v{n}", i)
                meet(pe, l * PHASES + 5)

        @block.gpsimd
        def _(ge):
            give_credit(ge, pool_own)
            g_ = nc.gpsimd

            meet(ge, 0)
            ge.sem_inc(passed, 1)
            with ge.Fori(0, DEPTH) as l:
                meet(ge, l * PHASES + 1)
                meet(ge, l * PHASES + 2)
                for d in (0, 1):
                    for t in ("CTP", "QMP", "QP"):
                        g_.memset(sc[d][t], 0.0).then_inc(s_pad, 1)
                apart(ge, s_pad, (l + 1) * 6)
                ge.sem_inc(passed, 1)
                with ge.Fori(0, TILES) as s:
                    it = l * TILES + s
                    links = [linker(ge, s_pool[d], it, alone=True) for d in (0, 1)]
                    for d in (0, 1):
                        b, L = sc[d], links[d]
                        ge.wait_ge(s_ld[d].sem, s_ld[d].at(it, "ld"))
                        ge.wait_ge(s_ls[d].sem, s_ls[d].at(it, "ls"))
                        apart(ge, s_pe[d].sem, s_pe[d].at(it, "upm", 1))
                        for g in (0, 1):
                            r = slice(HD * g, HD * g + HD)
                            L(f"ct{g}", g_.tensor_copy(b["CTP"][r, g * P:(g + 1) * P], b["FX"][r, P:2 * P]))
                            L(f"qm{g}", g_.tensor_copy(
                                b["QMP"][r, :].rearrange("p (j h s) -> p j h s", j=2, h=2)[:, :, g, :],
                                b["FT"][r, 2 * P:4 * P].rearrange("p (j s) -> p j s", j=2)))
                        L("xd", g_.tensor_tensor(grp(b["XD"], a=SH), grp(b["TX"][:, 0:512], a=SH),
                                                 b["TK"][:, 256 + VA + NDIR + 4:256 + VA + DB].unsqueeze(2)
                                                 .broadcast_to([P, SH, HD]), ALU.mult))
                    for d in (0, 1):
                        b, L = sc[d], links[d]
                        apart(ge, s_act[d].sem, s_act[d].at(it, "em"))
                        L("vw", g_.tensor_tensor(grp(b["VW"], a=MH), grp(b["TK"][:, 256:256 + VA], a=MH),
                                                 b["EM"][:, 8:12].unsqueeze(2).broadcast_to([P, MH, HD + 1]), ALU.mult))
                        apart(ge, s_st[d].sem, s_st[d].at(it, "st", 1))
                        sn, st = b["SN"], b["ST"]
                        L("sns", g_.tensor_tensor(grp(sn[:, 0:512], a=SH), grp(st[:, 0:512], a=SH),
                                                  b["EA"][:, 12:20].unsqueeze(2).broadcast_to([P, SH, HD]), ALU.mult))
                        L("snm", g_.tensor_tensor(grp(sn[:, S_ML:S_GLA], a=MH), grp(st[:, S_ML:S_GLA], a=MH),
                                                  b["EM"][:, 12:16].unsqueeze(2).broadcast_to([P, MH, HD + 1]), ALU.mult))
                    for d in (0, 1):
                        b, L = sc[d], links[d]
                        sn = b["SN"]
                        apart(ge, s_dve[d].sem, s_dve[d].at(it, "last"))
                        L("sna1", g_.tensor_tensor(sn[:, 0:512], sn[:, 0:512], b["T1"], ALU.add))
                        L("sna", g_.tensor_tensor(sn[:, S_ML:S_GLA], sn[:, S_ML:S_GLA], b["T2"], ALU.add))
                meet(ge, l * PHASES + 3)
                meet(ge, l * PHASES + 4)
                ixh = IXH.bitcast(U32)
                ge.sem_inc(passed, 1)
                with ge.Fori(0, TILES) as s:
                    it, p = l * TILES + s, pos(s)
                    ge.sem_inc(passed, 1)
                    with ge.Fori(0, HEADS // 2) as hh:
                        jt = it * (HEADS // 2) + hh
                        link = linker(ge, e_pool, jt, alone=True)
                        for u in (0, 1):
                            at = bass.ds(p * SLOTS + hh * 2 * TOPK + u * TOPK, TOPK)
                            apart(ge, e_dve.sem, e_dve.at(jt, f"aw{4 * u + 3}", 1))
                            link(f"ix{u}", g_.tensor_copy(ixh[:, u * TOPK:(u + 1) * TOPK], idx_all.bitcast(U32)[:, at]))
                            link(f"gw{u}", g_.tensor_copy(GWH[:, u * TOPK:(u + 1) * TOPK], gw_all[:, at]))
                            for j in range(TOPK):
                                if u == 0:
                                    apart(ge, e_pe.sem, e_pe.at(jt, f"v{TOPK + j}", 1))
                                else:
                                    apart(ge, e_pe.sem, e_pe.at(jt, f"v{j}"))
                                g_.indirect_dma_start(ring[:, j, :], None, io["experts"],
                                                      bass.IndirectOffsetOnAxis(ap=ixh[:, u * TOPK + j:u * TOPK + j + 1], axis=0)
                                                      ).then_inc(e_gat[j].sem, 16)
                meet(ge, l * PHASES + 5)


SHAPES = {
    "ident": [P, P], "x_in": [NPOS, P, D], "pos_in": [NPOS, P, D], "c2t": [P, 2 * KC],
    "w_ada": [DEPTH, D, 6 * D], "b_ada": [DEPTH, 6 * D], "w_in": [DEPTH, D, IN_W],
    "gbias": [DEPTH, 2 * NDIR], "mlstm_bi": [DEPTH, 8], "ssd_a_log": [DEPTH, 16], "wa2": [DEPTH, 32, 256],
    "sgn": [2 * NDIR], "coef": [2 * NDIR], "conv_w": [DEPTH, P, 18], "conv_b": [DEPTH, P, 6],
    "tri": [2, P, P], "perm": [2, P, P], "gmask": [P, S_W], "w_out": [DEPTH, D, D], "peer_wq": [DEPTH, D, D],
    "keys": [DEPTH, P, 256], "gnorm_w": [DEPTH, D], "ln1_w": [DEPTH, D], "ln1_b": [DEPTH, D],
    "ln2_w": [DEPTH, D], "ln2_b": [DEPTH, D], "ssd_d": [DEPTH, SH], "iota": [TOPK], "lofs": [DEPTH, 1],
    "state0": [DEPTH, 2, 2, P, S_W], "m0": [DEPTH, 2, 2, MH], "zeros": [P, 6, P], "experts": [DEPTH * NE, 2 * D],
}


def program(nc, scratch="Internal"):
    io = {k: nc.dram_tensor("in_" + k, s, F32, kind="ExternalInput").ap() for k, s in SHAPES.items()}
    for k, s in (("xres", [NPOS, P, D]), ("state", [DEPTH, 2, 7, P, S_W]), ("mstate", [DEPTH, 2, 7, MH])):
        io[k] = nc.dram_tensor(k, s, F32, kind="ExternalOutput").ap()
    io["scratch"] = lambda name, shape, dt: nc.dram_tensor(name, shape, dt, kind=scratch).ap()
    build(nc, io)


def pos_rows():
    n = DEC_TILES * P
    f = np.float32
    r = np.repeat(np.arange(n // GRID_W, dtype=f), GRID_W)
    c = np.tile(np.arange(GRID_W, dtype=f), n // GRID_W)
    q = D // 4
    inv = f(1) / np.power(f(POS_BASE), np.arange(q, dtype=f) / f(q)).astype(f)
    ar, ac = r[:, None] * inv, c[:, None] * inv
    t = np.concatenate([np.sin(ar), np.cos(ar), np.sin(ac), np.cos(ac)], axis=-1).astype(f)
    out = np.zeros((NPOS, P, D), f)
    out[2:] = t.reshape(DEC_TILES, P, D)
    return out


def lay_out(i):
    f = np.float32
    a = {k: np.asarray(v) for k, v in i.items()}
    L = DEPTH
    x = np.zeros((NPOS, P, D), f)
    x[0] = a["x_prompt"][0]
    x[2:] = a["x_sample"][0].reshape(DEC_TILES, P, D)
    c2 = np.stack([a["c_ctx"], a["c"][0]])
    gb = np.concatenate([a["gla_ba"], a["mlstm_bf"], a["ssd_dt_bias"]], axis=2).reshape(L, 2 * NDIR)
    wa2 = np.zeros((L, 32, 256), f)
    keys = np.zeros((L, P, 256), f)
    for d in (0, 1):
        wa2[:, RANK * d:RANK * d + RANK, P * d:P * d + P] = a["gla_wa2"][:, d]
        keys[:, 64 * d:64 * d + 64, P * d:P * d + P] = a["peer_keys"][:, d].transpose(0, 2, 1)
    sgn = np.tile(np.concatenate([-np.ones(132, f), np.ones(8, f)]), 2)
    coef = np.tile(np.concatenate([np.full(128, -1.0 / 16.0, f), -np.ones(4, f), np.zeros(8, f)]), 2)
    up = np.triu(np.ones((P, P), f))
    eye = np.eye(P, dtype=f)
    st = np.zeros((L, 2, 2, P, S_W), f)
    mask = np.zeros((P, S_W), f)
    for h in range(SH):
        g = h // 4
        st[:, :, 1, HD * g:HD * g + HD, h * HD:(h + 1) * HD] = a["state_ssd"][0, :, :, h].transpose(0, 1, 3, 2)
        mask[HD * g:HD * g + HD, h * HD:(h + 1) * HD] = 1
    for h in range(MH):
        r, c = slice(HD * (h % 2), HD * (h % 2) + HD), S_ML + 65 * h
        st[:, :, 1, r, c:c + HD] = a["state_mlstm_c"][0, :, :, h].transpose(0, 1, 3, 2)
        st[:, :, 1, r, c + HD] = a["state_mlstm_n"][0, :, :, h]
        mask[r, c:c + 65] = 1
        r, c = slice(GDK * h, GDK * h + GDK), S_GLA + HD * h
        st[:, :, 1, r, c:c + HD] = a["state_gla"][0, :, :, h]
        mask[r, c:c + HD] = 1
    m0 = np.zeros((L, 2, 2, MH), f)
    m0[:, :, 1] = a["state_mlstm_m"][0]
    return {
        "ident": eye, "x_in": x, "pos_in": pos_rows(),
        "c2t": c2.reshape(2, KC, P).transpose(2, 1, 0).reshape(P, 2 * KC),
        "w_ada": a["w_ada"], "b_ada": a["b_ada"], "w_in": a["w_in"], "gbias": gb,
        "mlstm_bi": a["mlstm_bi"].reshape(L, 8), "ssd_a_log": a["ssd_a_log"].reshape(L, 16), "wa2": wa2,
        "sgn": sgn, "coef": coef,
        "conv_w": a["conv_w"].reshape(L, 3, 6, P).transpose(0, 3, 2, 1).reshape(L, P, 18),
        "conv_b": a["conv_b"].reshape(L, 6, P).transpose(0, 2, 1),
        "tri": np.stack([up, up.T]), "perm": np.stack([eye, eye[::-1]]), "gmask": mask,
        "w_out": a["w_out"], "peer_wq": a["peer_wq"], "keys": keys, "gnorm_w": a["gnorm_w"],
        "ln1_w": a["ln1_w"], "ln1_b": a["ln1_b"], "ln2_w": a["ln2_w"], "ln2_b": a["ln2_b"], "ssd_d": a["ssd_d"],
        "iota": np.arange(TOPK, dtype=f), "lofs": np.arange(L, dtype=f)[:, None] * f(NE),
        "state0": st, "m0": m0, "zeros": np.zeros((P, 6, P), f),
        "experts": np.concatenate([a["peer_u"], a["peer_v"]], axis=2).reshape(L * NE, 2 * D),
    }


def kernel(**inputs):
    import concourse.bacc as bacc
    from concourse.bass_utils import run_bass_kernel_spmd as run

    nc = bacc.Bacc("TRN2", target_bir_lowering=False, num_devices=1)
    program(nc)
    data = {"in_" + k: np.ascontiguousarray(v) for k, v in lay_out(inputs).items()}
    r = run(nc, [data], core_ids=[0]).results[0]
    x, m = r["xres"], r["mstate"]
    st = np.stack([r["state"][:, 0, 1], r["state"][:, 1, 0]], axis=1)
    gla = np.stack([st[:, :, GDK * h:GDK * h + GDK, S_GLA + HD * h:S_GLA + HD * h + HD] for h in range(GH)], axis=2)
    mc = np.stack([st[:, :, HD * (h % 2):HD * (h % 2) + HD, S_ML + 65 * h:S_ML + 65 * h + HD] for h in range(MH)], axis=2)
    mn = np.stack([st[:, :, HD * (h % 2):HD * (h % 2) + HD, S_ML + 65 * h + HD] for h in range(MH)], axis=2)
    ssd = np.stack([st[:, :, HD * (h // 4):HD * (h // 4) + HD, h * HD:h * HD + HD] for h in range(SH)], axis=2)
    mm = np.stack([m[:, 0, 1], m[:, 1, 0]], axis=1)
    return (x[0:1], x[2:].reshape(1, DEC_TILES * P, D), gla[None], mc.transpose(0, 1, 2, 4, 3)[None], mn[None],
            mm[None], ssd.transpose(0, 1, 2, 4, 3)[None])
```

```python
import math
from contextlib import ExitStack

import numpy as np

import concourse.bass as bass
from concourse import mybir

F32 = mybir.dt.float32
U32 = mybir.dt.uint32
ALU = mybir.AluOpType
ACT = mybir.ActivationFunctionType
AX = mybir.AxisListType.X

P = 128
D = 1024
KC = D // P
DEPTH = 2
TILES = 5
NPOS = 6
SEQ_TILES = 1
DEC_TILES = 4
GRID_W = 64
POS_BASE = 10000.0
HD = 64
GH, MH, SH = 4, 4, 8
GDK = 32
RANK = 16
IN_W = 3136
O_GQ, O_GK, O_GV, O_GG, O_GA = 0, 128, 256, 512, 768
O_MQ, O_MK, O_MV, O_MO, O_MI = 800, 1056, 1312, 1568, 1824
O_SX, O_SZ, O_SB, O_SDT = 1840, 2352, 2864, 3120
NDIR = 140
DB = NDIR + 4 + 8
VA = MH * (HD + 1)
TOK_W = 256 + VA + 2 * DB
S_SSD, S_ML, S_GLA, S_W = 0, 512, 512 + VA, 512 + VA + 256
NE = 16384
HEADS = 8
TOPK = 16
SLOTS = HEADS * TOPK
ALPHA = (2 * DEPTH) ** 0.25
EPS = 1e-6
BL = 16
NB = P // BL
CLAMP = 40.0
PHASES = 4
DVE_STEPS = {5: 2, 6: 2, 7: 2, 8: 1, 14: 2, 15: 1, 21: 1, 34: 2, 35: 2, 36: 2, 41: 2, 42: 2, 43: 2, 44: 1,
             49: 2, 50: 2, 54: 1, 65: 1}
TOP_FIRST, TOP_LAST, SUM_FIRST = 77, 115, 122
ACT_STEPS = {10: 1, 20: 1, 36: 1, 44: 1, 54: 1, 66: 1, 72: 1, 118: 1}
PE_STEPS = (16, *range(22, 30), 49, *range(56, 64), 68)
ROUNDS = TILES + 1
RING = 8
DIAGS = 4
GRP = 2


EVENTS = {
    "m_pe": ["mod0", "mod1"],
    "m_dve": ["mod0", "mod1"],
    "i_dve": ["add"],
    "n_dve": ["st0", "st1", "mv", "rs", "xn", "xs", "xsh"],
    "n_act": ["sd"],
    "p_dve": ["ut0", "gat", "c4", "z0", "z1", "z2", "ig", "zs", "za", "vg", "vm", "sp", "la", "dt"],
    "p_act": ["ut1", "a1", "a2", "b1", "b2", "ze", "ln", "silug", "siluz", "sigmo"],
    "p_pe": ["tr0", "tr1", "A", "B", "C", "D", "E1", "E", "gate", "last"],
    "pl_dve": ["coef", "vone"],
    "pl_act": ["ea"],
    "c_dve": [
        "a0", "b0", "c0", "a1", "b1", "c1", "a2", "b2", "c2", "a3", "b3", "c3", "a4", "b4", "c4", "a5",
        "b5", "c5",
    ],
    "c_act": [
        "silu0", "silu1", "four0", "alone0", "silu2", "four1", "alone1", "silu3", "four2", "alone2",
        "silu4", "four3", "alone3", "silu5", "four4", "alone4",
    ],
    "c_pe": ["t0", "t1", "t2", "t3", "t4"],
    "s_dve0": [
        "cs", "f4", "dec", "g4", "ex0", "ex1", "ex2", "ex3", "ex4", "ex5", "ex6", "ex7", "cbm", "g4r",
        "r4", "kta", "ktb", "qba", "qbb", "gg8", "qh", "kdm", "qp0", "qp1", "qp2", "qp3", "ktm", "gt",
        "kmd", "em0", "em1", "em2", "em3", "w8", "xw", "qkm", "me0", "me1", "me2", "me3", "ys0", "ys1",
        "wm", "at", "t1", "hm0", "hm1", "dn0", "dn1", "rc", "ym", "yg", "t3", "sng", "t2", "last",
    ],
    "s_dve1": [
        "cs", "f4", "dec", "g4", "ex0", "ex1", "ex2", "ex3", "ex4", "ex5", "ex6", "ex7", "cbm", "g4r",
        "r4", "kta", "ktb", "qba", "qbb", "gg8", "qh", "kdm", "qp0", "qp1", "qp2", "qp3", "ktm", "gt",
        "kmd", "em0", "em1", "em2", "em3", "w8", "xw", "qkm", "me0", "me1", "me2", "me3", "ys0", "ys1",
        "wm", "at", "t1", "hm0", "hm1", "dn0", "dn1", "rc", "ym", "yg", "t3", "sng", "t2", "last",
    ],
    "s_act0": ["ea", "eb", "kd", "ex0", "ex1", "kt", "qb", "em", "me"],
    "s_act1": ["ea", "eb", "kd", "ex0", "ex1", "kt", "qb", "em", "me"],
    "s_pe0": ["cum", "g4r", "km", "qk", "kdt", "gb", "ssd", "att", "ups", "mli", "upg", "upm"],
    "s_pe1": ["cum", "g4r", "km", "qk", "kdt", "gb", "ssd", "att", "ups", "mli", "upg", "upm"],
    "s_pool0": ["ct0", "qm0", "ct1", "qm1", "xd", "vw", "sns", "snm", "sna1", "sna"],
    "s_pool1": ["ct0", "qm0", "ct1", "qm1", "xd", "vw", "sns", "snm", "sna1", "sna"],
    "o_dve": [
        "y0", "y1", "y2", "y3", "sq", "hr", "hrm", "hrr", "yn1", "yn2", "yt0", "g0", "g1", "r1", "st0a",
        "st1a", "mva", "rsa", "x1a", "x1b", "x1c", "st0b", "st1b", "mvb", "rsb", "u2a", "u2b", "u2c",
    ],
    "o_act": ["hsd", "yt1", "sda", "sdb"],
    "o_pe": ["yt0", "yt1", "out"],
    "q_dve": [
        "ut0", "qt0", "half0.0", "half0.1", "half0.2", "half0.3", "half0.4", "half1.0", "half1.1",
        "half1.2", "half1.3", "half1.4", "half2.0", "half2.1", "half2.2", "half2.3", "half2.4",
        "half3.0", "half3.1", "half3.2", "half3.3", "half3.4", "half4.0", "half4.1", "half4.2",
        "half4.3", "half4.4", "half5.0", "half5.1", "half5.2", "half5.3", "half5.4", "half6.0",
        "half6.1", "half6.2", "half6.3", "half6.4", "half7.0", "half7.1", "half7.2", "half7.3",
        "half7.4", "half8.0", "half8.1", "half8.2", "half8.3", "half8.4", "half9.0", "half9.1",
        "half9.2", "half9.3", "half9.4", "half10.0", "half10.1", "half10.2", "half10.3", "half10.4",
        "half11.0", "half11.1", "half11.2", "half11.3", "half11.4", "half12.0", "half12.1", "half12.2",
        "half12.3", "half12.4", "half13.0", "half13.1", "half13.2", "half13.3", "half13.4", "half14.0",
        "half14.1", "half14.2", "half14.3", "half14.4", "half15.0", "half15.1", "half15.2", "half15.3",
        "half15.4", "tf", "can", "pair0.0", "pair0.1", "pair0.2", "pair0.3", "pair0.4", "pair1.0",
        "pair1.1", "pair1.2", "pair1.3", "pair1.4", "pair2.0", "pair2.1", "pair2.2", "pair2.3",
        "pair2.4", "pair3.0", "pair3.1", "pair3.2", "pair3.3", "pair3.4", "pair4.0", "pair4.1",
        "pair4.2", "pair4.3", "pair4.4", "pair5.0", "pair5.1", "pair5.2", "pair5.3", "pair5.4",
        "pair6.0", "pair6.1", "pair6.2", "pair6.3", "pair6.4", "pair7.0", "pair7.1", "pair7.2",
        "pair7.3", "pair7.4", "ba0", "bf0", "oh0", "oi0", "oj0", "ba1", "bf1", "oh1", "oi1", "oj1",
        "ixa", "ixb", "sma", "smb", "smc", "smd",
    ],
    "q_act": ["ut1", "qt1", "sc0", "sc1", "sc2", "sc3", "sme"],
    "q_pe": ["ut0", "ut1", "q0", "q1", "q2", "q3", "q4", "q5", "q6", "q7", "s0", "s1", "s2", "s3"],
    "e_pool": ["ix0", "ix1"],
    "e_dve": [
        "gwc", "dot0", "dot1", "dot2", "dot3", "aw0", "dot4", "dot5", "aw1", "dot6", "dot7", "aw2",
        "dot8", "dot9", "aw3", "dot10", "dot11", "aw4", "dot12", "dot13", "aw5", "dot14", "dot15",
        "aw6", "dot16", "dot17", "aw7", "dot18", "dot19", "aw8", "dot20", "dot21", "aw9", "dot22",
        "dot23", "aw10", "dot24", "dot25", "aw11", "dot26", "dot27", "aw12", "dot28", "dot29", "aw13",
        "dot30", "dot31", "aw14", "dot32", "dot33", "aw15", "dot34", "dot35", "aw16", "dot36", "dot37",
        "aw17", "dot38", "dot39", "aw18", "dot40", "dot41", "aw19", "dot42", "dot43", "aw20", "dot44",
        "dot45", "aw21", "dot46", "dot47", "aw22", "dot48", "dot49", "aw23", "dot50", "dot51", "aw24",
        "dot52", "dot53", "aw25", "dot54", "dot55", "aw26", "dot56", "dot57", "aw27", "dot58", "dot59",
        "aw28", "dot60", "dot61", "aw29", "dot62", "dot63", "aw30", "dot64", "dot65", "aw31", "dot66",
        "dot67", "aw32", "dot68", "dot69", "aw33", "dot70", "dot71", "aw34", "dot72", "dot73", "aw35",
        "dot74", "dot75", "aw36", "dot76", "dot77", "aw37", "dot78", "dot79", "aw38", "dot80", "dot81",
        "aw39", "dot82", "dot83", "aw40", "dot84", "dot85", "aw41", "dot86", "dot87", "aw42", "dot88",
        "dot89", "aw43", "dot90", "dot91", "aw44", "dot92", "dot93", "aw45", "dot94", "dot95", "aw46",
        "dot96", "dot97", "aw47", "dot98", "dot99", "aw48", "dot100", "dot101", "aw49", "dot102",
        "dot103", "aw50", "dot104", "dot105", "aw51", "dot106", "dot107", "aw52", "dot108", "dot109",
        "aw53", "dot110", "dot111", "aw54", "dot112", "dot113", "aw55", "dot114", "dot115", "aw56",
        "dot116", "dot117", "aw57", "dot118", "dot119", "aw58", "dot120", "dot121", "aw59", "dot122",
        "dot123", "aw60", "dot124", "dot125", "aw61", "dot126", "dot127", "aw62", "aw63", "r00", "r01",
        "r1", "st0", "st1", "mv", "r2", "xa", "xw", "xb",
    ],
    "e_act": [
        "ge0", "ge1", "dg0", "dg1", "ge2", "dg2", "dg3", "ge3", "dg4", "dg5", "ge4", "dg6", "dg7",
        "ge5", "dg8", "dg9", "ge6", "dg10", "dg11", "ge7", "dg12", "dg13", "ge8", "dg14", "dg15", "ge9",
        "dg16", "dg17", "ge10", "dg18", "dg19", "ge11", "dg20", "dg21", "ge12", "dg22", "dg23", "ge13",
        "dg24", "dg25", "ge14", "dg26", "dg27", "ge15", "dg28", "dg29", "ge16", "dg30", "dg31", "ge17",
        "dg32", "dg33", "ge18", "dg34", "dg35", "ge19", "dg36", "dg37", "ge20", "dg38", "dg39", "ge21",
        "dg40", "dg41", "ge22", "dg42", "dg43", "ge23", "dg44", "dg45", "ge24", "dg46", "dg47", "ge25",
        "dg48", "dg49", "ge26", "dg50", "dg51", "ge27", "dg52", "dg53", "ge28", "dg54", "dg55", "ge29",
        "dg56", "dg57", "ge30", "dg58", "dg59", "ge31", "dg60", "dg61", "ge32", "dg62", "dg63", "ge33",
        "dg64", "dg65", "ge34", "dg66", "dg67", "ge35", "dg68", "dg69", "ge36", "dg70", "dg71", "ge37",
        "dg72", "dg73", "ge38", "dg74", "dg75", "ge39", "dg76", "dg77", "ge40", "dg78", "dg79", "ge41",
        "dg80", "dg81", "ge42", "dg82", "dg83", "ge43", "dg84", "dg85", "ge44", "dg86", "dg87", "ge45",
        "dg88", "dg89", "ge46", "dg90", "dg91", "ge47", "dg92", "dg93", "ge48", "dg94", "dg95", "ge49",
        "dg96", "dg97", "ge50", "dg98", "dg99", "ge51", "dg100", "dg101", "ge52", "dg102", "dg103",
        "ge53", "dg104", "dg105", "ge54", "dg106", "dg107", "ge55", "dg108", "dg109", "ge56", "dg110",
        "dg111", "ge57", "dg112", "dg113", "ge58", "dg114", "dg115", "ge59", "dg116", "dg117", "ge60",
        "dg118", "dg119", "ge61", "dg120", "dg121", "ge62", "dg122", "dg123", "ge63", "dg124", "dg125",
        "dg126", "dg127", "sd",
    ],
    "e_pe": [
        "v0", "v1", "v2", "v3", "v4", "v5", "v6", "v7", "v8", "v9", "v10", "v11", "v12", "v13", "v14",
        "v15", "v16", "v17", "v18", "v19", "v20", "v21", "v22", "v23", "v24", "v25", "v26", "v27",
        "v28", "v29", "v30", "v31", "v32", "v33", "v34", "v35", "v36", "v37", "v38", "v39", "v40",
        "v41", "v42", "v43", "v44", "v45", "v46", "v47", "v48", "v49", "v50", "v51", "v52", "v53",
        "v54", "v55", "v56", "v57", "v58", "v59", "v60", "v61", "v62", "v63", "v64", "v65", "v66",
        "v67", "v68", "v69", "v70", "v71", "v72", "v73", "v74", "v75", "v76", "v77", "v78", "v79",
        "v80", "v81", "v82", "v83", "v84", "v85", "v86", "v87", "v88", "v89", "v90", "v91", "v92",
        "v93", "v94", "v95", "v96", "v97", "v98", "v99", "v100", "v101", "v102", "v103", "v104", "v105",
        "v106", "v107", "v108", "v109", "v110", "v111", "v112", "v113", "v114", "v115", "v116", "v117",
        "v118", "v119", "v120", "v121", "v122", "v123", "v124", "v125", "v126", "v127",
    ],
}


class Steps:

    def __init__(self, sem, names, unit=1, ahead=1):
        self.sem, self.names, self.unit, self.ahead, self.seen = sem, names, unit, ahead, 0

    def take(self, name):
        assert self.names[self.seen % len(self.names)] == name, (name, self.names, self.seen)
        self.seen += 1

    @property
    def round(self):
        return len(self.names) * self.unit

    def at(self, it, name, back=0):
        i = self.names.index(name)
        return it * self.round + ((self.ahead - back) * self.round + (i + 1) * self.unit)


def build(nc, io):
    x_in, pos_in, c2t, w_ada, b_ada = io["x_in"], io["pos_in"], io["c2t"], io["w_ada"], io["b_ada"]
    xres, state, mstate = io["xres"], io["state"], io["mstate"]

    ctx = ExitStack()
    with ctx:
        def sem(name):
            return ctx.enter_context(nc.semaphore(name))


        def dram(name, shape, dt=F32):
            return io["scratch"](name, shape, dt)

        modd = dram("modd", [DEPTH, 2, 6 * D])
        tok_d = dram("tok_d", [NPOS, P, TOK_W])
        feat_d = dram("feat_d", [NPOS, P, 6 * P])
        gate_d = dram("gate_d", [NPOS, P, D])
        conv_d = dram("conv_d", [P, 6, NPOS * P + 2])
        ctok_d = dram("ctok_d", [NPOS, P, 640])
        cfeat_d = dram("cfeat_d", [NPOS, P, 2 * P])
        y_d = dram("y_d", [2, NPOS, P, D])
        u2_d = dram("u2_d", [NPOS, P, D])
        x1_d = dram("x1_d", [NPOS, P, D])

        big = ctx.enter_context(nc.sbuf_tensor("big", [P, 53200], F32))
        ps = [ctx.enter_context(nc.psum_tensor(f"bank{b}", [P, 512], F32)) for b in range(8)]

        class Area:
            def __init__(self, base):
                self.top = base

            def __call__(self, cols, parts=P):
                a = self.top
                self.top += cols
                assert self.top <= 53200, self.top
                return big[0:parts, a:a + cols]

        keep = Area(0)
        ident = keep(P)
        ones = keep(P)
        eps = keep(1)
        base = keep.top

        met = sem("met")
        credit = sem("credit")
        passed = sem("passed")
        start_ld = sem("start_ld")
        sem_ones = sem("sem_ones")
        sem_silu = sem("sem_silu")
        fill_st = sem("fill_st")

        def apart(eng, s, value):
            eng.wait_ge(s, value)
            eng.sem_inc(passed, 1)

        def meet(eng, n):
            eng.sem_inc(passed, 1)
            eng.drain().then_inc(met, 1)
            apart(eng, met, n * 5 + 5)

        def linker(eng, s, it, alone=False):
            s.seen = 0

            def link(name, ins):
                s.take(name)
                ins.then_inc(s.sem, 1)
                eng.wait_ge(s.sem, s.at(it, name))
                if alone:
                    eng.sem_inc(passed, 1)
            return link

        def marker(s):
            s.seen = 0

            def mark(name, ins):
                s.take(name)
                ins.then_inc(s.sem, 1)
            return mark

        def pos(s):
            return nc.s_assert_within(s + ((s + 3) >> 2), 0, NPOS - 1,
                                      skip_runtime_bounds_check_because="s is 0..4: 0, 2, 3, 4, 5")

        def bwd_pos(s):
            return nc.s_assert_within(((s + 3) >> 2) * 6 - s, 0, NPOS - 1,
                                      skip_runtime_bounds_check_because="s is 0..4: 0, 5, 4, 3, 2")

        def next_pos(s):
            return nc.s_assert_within((s & 3) + 2, 0, NPOS - 1,
                                      skip_runtime_bounds_check_because="s is 0..4: 2, 3, 4, 5, 2")

        def group(s):
            return nc.s_assert_within((s + 3) >> 2, 0, 1,
                                      skip_runtime_bounds_check_because="s is 0..4: 0, 1, 1, 1, 1")

        def at1(t, i):
            v = t[bass.ds(i, 1)]
            return v.rearrange("a " + " ".join("bcde"[:len(v.shape) - 1]) + " -> (a b) "
                               + " ".join("cde"[:len(v.shape) - 2]))

        def grp(ap, **k):
            return ap.rearrange("p (a b) -> p a b", **k)

        def rows(ap):
            return ap.partition_broadcast(P)

        sp_own, act_own, pe_own, dve_own, pool_own = [], [], [], [], []

        def mk(owner, name, unit=1, events=None, ahead=1):
            s = Steps(sem(name), EVENTS[name] if events is None else events, unit, ahead)
            if ahead:
                owner.append(s)
            return s

        m_w = [mk(sp_own, f"m_w{u}", 32, ["w"]) for u in (0, 1)]
        m_pe, m_dve = mk(pe_own, "m_pe"), mk(dve_own, "m_dve")
        m_out = [mk(act_own, f"m_out{u}", 16, ["out"]) for u in (0, 1)]
        i_ld, i_dve, i_st = mk(sp_own, "i_ld", 32, ["ld"]), mk(dve_own, "i_dve"), mk(sp_own, "i_st", 16, ["st"])
        p_w, p_par = [sem(f"p_w{q}") for q in range(4)], sem("p_par")
        n_dve, n_act = mk(dve_own, "n_dve"), mk(act_own, "n_act")
        p_x, p_mod = mk(sp_own, "p_x", 16, ["x"]), mk(sp_own, "p_mod", 32, ["mod"])
        p_dve, p_act, p_pe = mk(dve_own, "p_dve"), mk(act_own, "p_act"), mk(pe_own, "p_pe")
        p_st = mk(sp_own, "p_st", 64, ["st"])
        pl_dve, pl_act = mk(dve_own, "pl_dve"), mk(act_own, "pl_act")
        c_par = sem("c_par")
        c_ld = [mk(sp_own, f"c_ld{c}", 16, ["ld"]) for c in range(6)]
        c_st = mk(sp_own, "c_st", 96, ["st"])
        c_dve, c_act, c_pe = mk(dve_own, "c_dve"), mk(act_own, "c_act"), mk(pe_own, "c_pe")
        s_con = sem("s_con")
        s_pad = sem("s_pad")
        s_ld = [mk(sp_own, f"s_ld{d}", 64, ["ld"]) for d in (0, 1)]
        s_ls = [mk(sp_own, f"s_ls{d}", 64, ["ls"]) for d in (0, 1)]
        s_st = [mk(sp_own, f"s_st{d}", 48, ["st"]) for d in (0, 1)]
        s_dve = [mk(dve_own, f"s_dve{d}") for d in (0, 1)]
        s_act = [mk(act_own, f"s_act{d}") for d in (0, 1)]
        s_pe = [mk(pe_own, f"s_pe{d}") for d in (0, 1)]
        s_pool = [mk(pool_own, f"s_pool{d}") for d in (0, 1)]
        e_par, e_w = sem("e_par"), sem("e_w")
        o_ld, o_ldx, o_st = mk(sp_own, "o_ld", 64, ["ld"]), mk(sp_own, "o_ldx", 64, ["ld"]), mk(sp_own, "o_st", 32, ["st"])
        o_dve, o_act, o_pe = mk(dve_own, "o_dve"), mk(act_own, "o_act"), mk(pe_own, "o_pe")
        q_dve, q_act, q_pe = mk(dve_own, "q_dve"), mk(act_own, "q_act"), mk(pe_own, "q_pe")
        e_u, e_x, e_st = mk(sp_own, "e_u", 16, ["u"]), mk(sp_own, "e_x", 32, ["x"]), mk(sp_own, "e_st", 16, ["st"])
        e_gat = [mk(pool_own, f"e_gat{j}", 16, [f"g{r}" for r in range(SLOTS // RING)], ahead=0) for j in range(RING)]
        e_pool = mk(pool_own, "e_pool")
        e_dve, e_act, e_pe = mk(dve_own, "e_dve"), mk(act_own, "e_act"), mk(pe_own, "e_pe")

        def give_credit(eng, own):
            for s in own:
                if s.names:
                    eng.sem_inc(s.sem, s.round)
            eng.sem_inc(credit, 1)
            eng.wait_ge(credit, 5)

        a = Area(base)
        WA = [a(KC * 512) for _ in (0, 1)]
        BA = [a(512, 2) for _ in (0, 1)]
        MO = [a(512, 2) for _ in (0, 1)]
        CT, CS2 = a(2 * KC), a(2 * KC)
        XI, PI_ = a(D), a(D)

        a = Area(base)
        WIN = a(KC * IN_W)
        win = WIN.rearrange("p (k n) -> p k n", k=KC)
        X, SC, SHF, U = a(D), a(D), a(D), a(D)
        UT = a(D)
        FA, CP, GG, TB = a(6 * P), a(6 * P), a(D), a(TOK_W)
        GAT = a(P, 32)
        WA2 = a(256, 32)
        BROW, COEF, SGN = a(2 * NDIR), a(2 * NDIR), a(2 * NDIR)
        BIG_, ALOG = a(8), a(16)
        Z, ZA, ZL = a(2 * NDIR), a(2 * NDIR), a(2 * NDIR)
        ST6, MV, SD, RS = a(12), a(2), a(1), a(1)
        assert a.top <= 53200 - 2 * KC * D
        dirs = TB[:, 256 + VA:].rearrange("p (d w) -> p d w", d=2)

        a = Area(base)
        NT = NPOS * P
        CW, CB_ = a(18), a(6)
        CI = a(6 * (NT + 2)).rearrange("p (c n) -> p c n", c=6)
        CV, CO = a(6 * NT).rearrange("p (c n) -> p c n", c=6), a(6 * NT).rearrange("p (c n) -> p c n", c=6)
        CTK = a(TILES * 640).rearrange("p (s n) -> p s n", s=TILES)

        a = Area(base)
        TRI, PERM = [a(P) for _ in (0, 1)], [a(P) for _ in (0, 1)]
        GM = a(S_W)
        sc = []
        for d in (0, 1):
            v = dict(TK=a(256 + VA + DB), FT=a(6 * P), TX=a(640), FX=a(2 * P), ST=a(S_W), MB=a(4), MC=a(1, 4),
                     CS=a(162), F4=a(1, 4), EX=a(8 * P), CTP=a(2 * P), CBM=a(2 * P), XD=a(512), XW=a(512),
                     EA=a(29), KT=a(NB * P), QB=a(P), QP=a(NB * 4 * BL), QH=a(P), EB=a(P), AT=a(4 * P),
                     KD=a(P), KMD=a(3 * P), G4=a(4), G4R=a(P, 4), R4=a(P, 4), GG8=a(8), GT=a(4), EMA=a(16),
                     EM=a(16), ME=a(4 * P), QMP=a(4 * P), T1=a(512), T2=a(VA), T3=a(256), VW=a(VA), HM=a(VA),
                     DN=a(4), RC=a(4), Y=a(D), SN=a(S_W), MN=a(1, 4))
            sc.append(v)

        a = Area(53200 - 2 * KC * D)
        wo, wq = [a(KC * D).rearrange("p (k n) -> p k n", k=KC) for _ in (0, 1)]
        a = Area(base)
        ring = a(RING * 2 * D).rearrange("p (j n) -> p j n", j=RING)
        GNW, L1W, L1B, L2W, L2B = a(D), a(D), a(D), a(D), a(D)
        DROW, KEYS, IOTA, LOFS = a(8), a(2 * P), a(TOPK), a(1)
        SCO = a(2048)
        YF, YB = SCO[:, 0:D], SCO[:, D:2 * D]
        GO, TX3, XO, G1, SC2, SH2 = a(D), a(512), a(D), a(D), a(D), a(D)
        YT = a(D)
        SQ = YT
        U2T = YT
        QT = G1
        HR, HR2, HR3 = a(16), a(16), a(16)
        oST6, oMV, oSD, oRS = a(12), a(2), a(1), a(1)
        CAN = OH = SCO
        TV, TI = a(256), a(256)
        BV, BI, BA1, IFR, JFR = a(P), a(P), a(P), a(P), a(P)
        SM, SR = a(8), a(8)
        IDXN, GWN, IDXC, GWC = a(SLOTS), a(SLOTS), a(SLOTS), a(SLOTS)
        EU, EX1, EG2 = a(D), a(D), a(D)
        DOT, AG, AW = a(16), a(16), a(16)
        DG = a(DIAGS * P)
        eST6, eMV, eSD, eRS = a(12), a(2), a(1), a(1)
        assert a.top <= 53200 - 2 * KC * D

        block = ctx.enter_context(nc.Block())

        @block.sync
        def _(sp):
            give_credit(sp, sp_own)
            sp.dma_start(ident, io["ident"]).then_inc(start_ld, 16)
            sp.dma_start(CT, c2t).then_inc(start_ld, 16)
            for d, slots in ((0, (0, 2)), (1, (1, 6))):
                for w, slot in enumerate(slots):
                    sp.dma_start(state[:, d, slot], io["state0"][:, d, w]).then_inc(fill_st, 16)
                    sp.dma_start(mstate[:, d, slot], io["m0"][:, d, w]).then_inc(fill_st, 16)
            for c0, c1 in ((0, 1), (P + 1, 2 * P + 1), (NPOS * P + 1, NPOS * P + 2)):
                with nc.allow_non_contiguous_dma(reason="one column at either edge"):
                    sp.dma_start(conv_d[:, :, c0:c1], io["zeros"][:, :, 0:c1 - c0]).then_inc(fill_st, 16)

            with sp.Fori(0, DEPTH) as l:
                with sp.Fori(0, 6) as jj:
                    it = l * 6 + jj
                    for u in (0, 1):
                        cols = bass.ds(jj * 1024 + u * 512, 512)
                        apart(sp, m_pe.sem, m_pe.at(it, f"mod{u}", 1))
                        apart(sp, m_dve.sem, m_dve.at(it, f"mod{u}", 1))
                        sp.dma_start(WA[u].rearrange("p (k n) -> p k n", k=KC),
                                     at1(w_ada, l)[:, cols].rearrange("(k p) n -> p k n", p=P)
                                     ).then_inc(m_w[u].sem, 16)
                        sp.dma_start(BA[u], at1(b_ada, l)[cols].partition_broadcast(2)
                                     ).then_inc(m_w[u].sem, 16)
            with sp.Fori(0, TILES) as s:
                p = pos(s)
                apart(sp, i_dve.sem, i_dve.at(s, "add", 1))
                apart(sp, i_st.sem, i_st.at(s, "st", 1))
                sp.dma_start(XI, at1(x_in, p)).then_inc(i_ld.sem, 16)
                sp.dma_start(PI_, at1(pos_in, p)).then_inc(i_ld.sem, 16)
                apart(sp, i_dve.sem, i_dve.at(s, "add"))
                sp.dma_start(at1(xres, p), XI).then_inc(i_st.sem, 16)
            apart(sp, i_st.sem, i_st.at(TILES - 1, "st"))
            apart(sp, fill_st, 16 * 11)
            meet(sp, 0)

            with sp.Fori(0, DEPTH) as l:
                def load_tile(t, p, mrow):
                    apart(sp, n_dve.sem, n_dve.at(t, "xn", 1))
                    sp.dma_start(X, at1(xres, p)).then_inc(p_x.sem, 16)
                    apart(sp, n_dve.sem, n_dve.at(t, "xsh", 1))
                    sp.dma_start(SC, rows(mrow[D:2 * D])).then_inc(p_mod.sem, 16)
                    sp.dma_start(SHF, rows(mrow[0:D])).then_inc(p_mod.sem, 16)

                load_tile(l * ROUNDS, 0, modd[bass.ds(l, 1), 0, :].rearrange("a n -> (a n)"))
                sp.dma_start(BROW, rows(at1(io["gbias"], l))).then_inc(p_par, 16)
                sp.dma_start(BIG_, rows(at1(io["mlstm_bi"], l))).then_inc(p_par, 16)
                sp.dma_start(ALOG, rows(at1(io["ssd_a_log"], l))).then_inc(p_par, 16)
                sp.dma_start(WA2, at1(io["wa2"], l)).then_inc(p_par, 16)
                sp.dma_start(SGN, rows(io["sgn"])).then_inc(p_par, 16)
                sp.dma_start(COEF, rows(io["coef"])).then_inc(p_par, 16)
                for q, part in enumerate(W_IN_PARTS):
                    for c0, c1 in part:
                        sp.dma_start(win[:, :, c0:c1], at1(io["w_in"], l)[:, c0:c1].rearrange("(k p) n -> p k n", p=P)
                                     ).then_inc(p_w[q], 16)
                sp.dma_start(wo, at1(io["w_out"], l).rearrange("(k p) n -> p k n", p=P)).then_inc(e_w, 16)
                sp.dma_start(wq, at1(io["peer_wq"], l).rearrange("(k p) n -> p k n", p=P)).then_inc(e_w, 16)
                with sp.Fori(0, TILES) as s:
                    it, p = l * TILES + s, pos(s)
                    load_tile(l * ROUNDS + 1 + s, next_pos(s), modd[bass.ds(l, 1), 1, :].rearrange("a n -> (a n)"))
                    apart(sp, p_act.sem, p_act.at(it, "b2"))
                    sp.dma_start(at1(feat_d, p), FA).then_inc(p_st.sem, 16)
                    apart(sp, p_dve.sem, p_dve.at(it, "dt"))
                    sp.dma_start(conv_d[:, :, bass.ds(p * P + 1, P)],
                                 CP.rearrange("p (c n) -> p c n", c=6)).then_inc(p_st.sem, 16)
                    sp.dma_start(at1(tok_d, p), TB).then_inc(p_st.sem, 16)
                    apart(sp, p_act.sem, p_act.at(it, "sigmo"))
                    sp.dma_start(at1(gate_d, p), GG).then_inc(p_st.sem, 16)
                apart(sp, p_st.sem, p_st.at(l * TILES + TILES - 1, "st"))
                meet(sp, l * PHASES + 1)

                sp.dma_start(CW, at1(io["conv_w"], l)).then_inc(c_par, 16)
                sp.dma_start(CB_, at1(io["conv_b"], l)).then_inc(c_par, 16)
                for c in range(6):
                    sp.dma_start(CI[:, c, :], conv_d[:, c, :]).then_inc(c_ld[c].sem, 16)

                def token_rows(c0, c1):
                    sp.dma_start(ctok_d[0, :, c0:c1], CTK[:, 0, c0:c1]).then_inc(c_st.sem, 16)
                    sp.dma_start(ctok_d[2:, :, c0:c1].rearrange("s p n -> p s n"), CTK[:, 1:, c0:c1]).then_inc(c_st.sem, 16)

                apart(sp, c_act.sem, c_act.at(l, "alone3"))
                token_rows(0, 512)
                apart(sp, c_act.sem, c_act.at(l, "alone4"))
                token_rows(512, 640)
                apart(sp, c_act.sem, c_act.at(l, "silu5"))
                for c in (4, 5):
                    sp.dma_start(cfeat_d[:, :, (c - 4) * P:(c - 3) * P].rearrange("s p n -> p s n"),
                                 CO[:, c, :].rearrange("p (s n) -> p s n", s=NPOS)).then_inc(c_st.sem, 16)
                apart(sp, c_st.sem, c_st.at(l, "st"))
                meet(sp, l * PHASES + 2)

                for d in (0, 1):
                    sp.dma_start(TRI[d], io["tri"][d]).then_inc(s_con, 16)
                    sp.dma_start(PERM[d], io["perm"][d]).then_inc(s_con, 16)
                sp.dma_start(GM, io["gmask"]).then_inc(s_con, 16)
                with sp.Fori(0, TILES) as s:
                    it = l * TILES + s
                    for d in (0, 1):
                        v = sc[d]
                        p = pos(s) if d == 0 else bwd_pos(s)
                        src = p if d == 0 else p + 1
                        apart(sp, s_pe[d].sem, s_pe[d].at(it, "upm", 1))
                        apart(sp, s_dve[d].sem, s_dve[d].at(it, "last", 1))
                        apart(sp, s_pool[d].sem, s_pool[d].at(it, "sna", 1))
                        sp.dma_start(v["TK"][:, 0:256 + VA], at1(tok_d, p)[:, 0:256 + VA]).then_inc(s_ld[d].sem, 16)
                        sp.dma_start(v["TK"][:, 256 + VA:],
                                     at1(tok_d, p)[:, 256 + VA + d * DB:256 + VA + (d + 1) * DB]
                                     ).then_inc(s_ld[d].sem, 16)
                        sp.dma_start(v["FT"], at1(feat_d, p)).then_inc(s_ld[d].sem, 16)
                        sp.dma_start(v["TX"], at1(ctok_d, p)).then_inc(s_ld[d].sem, 16)
                        sp.dma_start(v["FX"], at1(cfeat_d, p)).then_inc(s_ls[d].sem, 16)
                        apart(sp, s_st[d].sem, s_st[d].at(it, "st", 1))
                        stl, msl = (t[bass.ds(l, 1), d, bass.ds(src, 1)] for t in (state, mstate))
                        sp.dma_start(v["ST"], stl.rearrange("a b p n -> (a b p) n")).then_inc(s_ls[d].sem, 16)
                        sp.dma_start(v["MB"], rows(msl.rearrange("a b n -> (a b n)"))).then_inc(s_ls[d].sem, 16)
                        sp.dma_start(v["MC"], msl.rearrange("a b (n c) -> (a b n) c", c=1)).then_inc(s_ls[d].sem, 16)
                    for d in (0, 1):
                        v = sc[d]
                        p = pos(s) if d == 0 else bwd_pos(s)
                        dst = p + 1 if d == 0 else p
                        apart(sp, s_dve[d].sem, s_dve[d].at(it, "last"))
                        apart(sp, s_pool[d].sem, s_pool[d].at(it, "sna"))
                        ydst = y_d[d, bass.ds(p, 1)].rearrange("a p n -> (a p) n")
                        sp.dma_start(ydst, v["Y"]).then_inc(s_st[d].sem, 16)
                        stl, msl = (t[bass.ds(l, 1), d, bass.ds(dst, 1)] for t in (state, mstate))
                        sp.dma_start(stl.rearrange("a b p n -> (a b p) n"), v["SN"]).then_inc(s_st[d].sem, 16)
                        sp.dma_start(msl.rearrange("a b (n c) -> (a b n) c", c=1), v["MN"]).then_inc(s_st[d].sem, 16)
                for d in (0, 1):
                    apart(sp, s_st[d].sem, s_st[d].at(l * TILES + TILES - 1, "st"))
                meet(sp, l * PHASES + 3)

                for dst, src in ((GNW, "gnorm_w"), (L1W, "ln1_w"), (L1B, "ln1_b"), (DROW, "ssd_d"),
                                 (L2W, "ln2_w"), (L2B, "ln2_b"), (LOFS, "lofs")):
                    sp.dma_start(dst, rows(at1(io[src], l))).then_inc(e_par, 16)
                sp.dma_start(KEYS, at1(io["keys"], l)).then_inc(e_par, 16)
                sp.dma_start(IOTA, rows(io["iota"])).then_inc(e_par, 16)

                def mix(t, p, mrow):
                    apart(sp, q_dve.sem, q_dve.at(t, "smd", 1))
                    for dst, src in ((YF, y_d[0, bass.ds(p, 1)].rearrange("a p n -> (a p) n")),
                                     (YB, y_d[1, bass.ds(p, 1)].rearrange("a p n -> (a p) n")),
                                     (GO, at1(gate_d, p)), (TX3, at1(ctok_d, p)[:, 0:512])):
                        sp.dma_start(dst, src).then_inc(o_ld.sem, 16)
                    apart(sp, q_pe.sem, q_pe.at(t, "s3", 1))
                    apart(sp, o_st.sem, o_st.at(t, "st", 1))
                    for dst, src in ((XO, at1(xres, p)), (G1, rows(mrow[2 * D:3 * D])),
                                     (SC2, rows(mrow[4 * D:5 * D])), (SH2, rows(mrow[3 * D:4 * D]))):
                        sp.dma_start(dst, src).then_inc(o_ldx.sem, 16)
                    apart(sp, o_dve.sem, o_dve.at(t, "u2c"))
                    sp.dma_start(at1(x1_d, p), XO).then_inc(o_st.sem, 16)
                    sp.dma_start(at1(u2_d, p), SC2).then_inc(o_st.sem, 16)

                mix(l * ROUNDS, 0, modd[bass.ds(l, 1), 0, :].rearrange("a n -> (a n)"))
                with sp.Fori(0, TILES) as s:
                    it, p = l * TILES + s, pos(s)
                    mrow = modd[bass.ds(l, 1), bass.ds(group(s), 1), :].rearrange("a b n -> (a b n)")
                    apart(sp, e_dve.sem, e_dve.at(it, f"dot{SLOTS - 1}", 1))
                    apart(sp, o_st.sem, o_st.at(l * ROUNDS + s, "st"))
                    sp.dma_start(EU, at1(u2_d, p)).then_inc(e_u.sem, 16)
                    apart(sp, e_st.sem, e_st.at(it, "st", 1))
                    sp.dma_start(EX1, at1(x1_d, p)).then_inc(e_x.sem, 16)
                    sp.dma_start(EG2, rows(mrow[5 * D:6 * D])).then_inc(e_x.sem, 16)
                    mix(l * ROUNDS + 1 + s, next_pos(s), modd[bass.ds(l, 1), 1, :].rearrange("a n -> (a n)"))
                    apart(sp, e_dve.sem, e_dve.at(it, "xb"))
                    sp.dma_start(at1(xres, p), EX1).then_inc(e_st.sem, 16)
                apart(sp, e_st.sem, e_st.at(l * TILES + TILES - 1, "st"))
                apart(sp, o_st.sem, o_st.at(l * ROUNDS + TILES, "st"))
                meet(sp, l * PHASES + 4)

        @block.vector
        def _(ve):
            give_credit(ve, dve_own)
            v_ = nc.vector

            def stats(link, tag, x, st6, mv):
                for h in (0, 1):
                    link(f"st{h}{tag}", v_.bn_stats(st6[:, 6 * h:6 * h + 6], x[:, 512 * h:512 * h + 512]))
                    yield
                ve.sem_inc(passed, 1)
                link("mv" + tag, v_.bn_aggr(mv, st6))
                yield

            v_.memset(ones, 1.0).then_inc(sem_ones, 1)
            v_.memset(eps, EPS).then_inc(sem_ones, 1)
            ve.wait_ge(sem_ones, 2)

            ve.sem_inc(passed, 1)
            with ve.Fori(0, DEPTH) as l:
                ve.sem_inc(passed, 1)
                with ve.Fori(0, 6) as jj:
                    it = l * 6 + jj
                    link = linker(ve, m_dve, it)
                    for u in (0, 1):
                        ve.wait_ge(m_pe.sem, m_pe.at(it, f"mod{u}"))
                        ve.wait_ge(m_w[u].sem, m_w[u].at(it, "w"))
                        ve.wait_ge(m_out[u].sem, m_out[u].at(it, "out", 1))
                        link(f"mod{u}", v_.tensor_tensor(MO[u], ps[u][0:2, :], BA[u], ALU.add))
            ve.sem_inc(passed, 1)
            with ve.Fori(0, TILES) as s:
                link = linker(ve, i_dve, s)
                ve.wait_ge(i_ld.sem, i_ld.at(s, "ld"))
                link("add", v_.tensor_tensor(XI, XI, PI_, ALU.add))
            meet(ve, 0)

            ve.sem_inc(passed, 1)
            with ve.Fori(0, DEPTH) as l:
                ve.wait_ge(p_par, (l + 1) * 96)
                link = linker(ve, pl_dve, l)
                ve.wait_ge(pl_act.sem, pl_act.at(l, "ea"))
                cf = grp(COEF, a=2)
                link("coef", v_.tensor_scalar(cf[:, :, 132:140], grp(ALOG, a=2), -1.0, None, ALU.mult))
                link("vone", v_.memset(TB[:, 256:256 + VA].rearrange("p (h e) -> p h e", h=MH)[:, :, HD:HD + 1], 1.0))

                def normed(t):
                    link = linker(ve, n_dve, t)
                    ve.wait_ge(p_x.sem, p_x.at(t, "x"))
                    for _ in stats(link, "", X, ST6, MV):
                        pass
                    ve.wait_ge(n_act.sem, n_act.at(t, "sd"))
                    link("rs", v_.reciprocal(RS, SD))
                    link("xn", v_.tensor_scalar(U, X, MV[:, 0:1], RS, ALU.subtract, ALU.mult))
                    ve.wait_ge(p_mod.sem, p_mod.at(t, "mod"))
                    link("xs", v_.scalar_tensor_tensor(U, SC, 1.0, U, ALU.add, ALU.mult))
                    link("xsh", v_.tensor_tensor(U, U, SHF, ALU.add))

                normed(l * ROUNDS)
                ve.sem_inc(passed, 1)
                with ve.Fori(0, TILES) as s:
                    it = l * TILES + s
                    link = linker(ve, p_dve, it)
                    ve.wait_ge(p_pe.sem, p_pe.at(it, "tr0"))
                    ve.wait_ge(p_pe.sem, p_pe.at(it, "last", 1))
                    link("ut0", v_.tensor_copy(UT[:, 0:512], ps[0][:, :]))
                    ve.wait_ge(p_st.sem, p_st.at(it, "st", 1))
                    ve.wait_ge(p_pe.sem, p_pe.at(it, "D"))
                    link("gat", v_.tensor_copy(GAT, ps[5][0:32, 0:P]))
                    link("c4", v_.tensor_copy(CP[:, 2 * P:6 * P], ps[4][:, :]))
                    normed(l * ROUNDS + 1 + s)
                    ve.wait_ge(p_pe.sem, p_pe.at(it, "gate"))
                    z, br = grp(Z, a=2), grp(BROW, a=2)
                    link("z0", v_.tensor_tensor(z[:, :, 0:128], grp(ps[5][:, 160:416], a=2), br[:, :, 0:128], ALU.add))
                    link("z1", v_.tensor_tensor(z[:, :, 128:132], grp(ps[5][:, 136:144], a=2), br[:, :, 128:132], ALU.add))
                    link("z2", v_.tensor_tensor(z[:, :, 132:140], grp(ps[5][:, 144:160], a=2), br[:, :, 132:140], ALU.add))
                    link("ig", v_.tensor_tensor(dirs[:, :, NDIR:NDIR + 4], grp(ps[5][:, 128:136], a=2),
                                                grp(BIG_, a=2), ALU.add))
                    link("zs", v_.tensor_tensor(Z, Z, SGN, ALU.mult))
                    link("za", v_.scalar_tensor_tensor(ZA, Z, -1.0, Z, ALU.mult, ALU.max))
                    ve.wait_ge(p_pe.sem, p_pe.at(it, "E"))
                    link("vg", v_.tensor_copy(TB[:, 0:256], ps[6][:, 0:256]))
                    link("vm", v_.tensor_copy(TB[:, 256:256 + VA].rearrange("p (h e) -> p h e", h=MH)[:, :, 0:HD],
                                              ps[6][:, 256:512].rearrange("p (h e) -> p h e", h=MH)))
                    ve.wait_ge(p_act.sem, p_act.at(it, "ln"))
                    link("sp", v_.scalar_tensor_tensor(Z, Z, 0.0, ZL, ALU.max, ALU.add))
                    link("la", v_.tensor_tensor(dirs[:, :, 0:NDIR], grp(Z, a=2), cf, ALU.mult))
                    link("dt", v_.tensor_copy(dirs[:, :, NDIR + 4:DB], grp(Z, a=2)[:, :, 132:140]))
                meet(ve, l * PHASES + 1)

                ve.wait_ge(c_par, (l + 1) * 32)
                link = linker(ve, c_dve, l)
                for c in range(6):
                    ve.wait_ge(c_ld[c].sem, c_ld[c].at(l, "ld"))
                    link(f"a{c}", v_.tensor_scalar(CV[:, c, :], CI[:, c, 0:NT], CW[:, 3 * c:3 * c + 1], None, ALU.mult))
                    link(f"b{c}", v_.scalar_tensor_tensor(CV[:, c, :], CI[:, c, 1:NT + 1], CW[:, 3 * c + 1:3 * c + 2],
                                                          CV[:, c, :], ALU.mult, ALU.add))
                    link(f"c{c}", v_.scalar_tensor_tensor(CV[:, c, :], CI[:, c, 2:NT + 2], CW[:, 3 * c + 2:3 * c + 3],
                                                          CV[:, c, :], ALU.mult, ALU.add))
                meet(ve, l * PHASES + 2)

                ve.wait_ge(s_con, (l + 1) * 80)
                ve.wait_ge(s_pad, (l + 1) * 6)
                ve.sem_inc(passed, 1)
                with ve.Fori(0, TILES) as s:
                    it = l * TILES + s
                    links = [linker(ve, s_dve[d], it) for d in (0, 1)]
                    V = [{k: x for k, x in sc[d].items()} for d in (0, 1)]

                    def hb(ap, h, n):
                        return ap.unsqueeze(2).broadcast_to([P, h, n])

                    for d in (0, 1):
                        b, L = V[d], links[d]
                        cs = b["CS"]
                        ve.wait_ge(s_pe[d].sem, s_pe[d].at(it, "cum"))
                        L("cs", v_.tensor_copy(cs[:, 0:153], ps[4 * d][:, 0:153]))
                        L("f4", v_.tensor_copy(b["F4"], ps[4 * d][0:4, 153:154]))
                        L("dec", v_.tensor_tensor(cs[:, 153:161], cs[:, 144:152], cs[:, 132:140], ALU.subtract))
                        L("g4", v_.tensor_tensor(b["G4"], b["TK"][:, 256 + VA + NDIR:256 + VA + NDIR + 4],
                                                 cs[:, 128:132], ALU.subtract))
                        for h in range(SH):
                            L(f"ex{h}", v_.tensor_scalar(b["EX"][:, h * P:(h + 1) * P],
                                                         ps[4 * d + 1 + h // 4][:, h % 4 * P:(h % 4 + 1) * P],
                                                         cs[:, 132 + h:133 + h], 0.0, ALU.subtract, ALU.min))
                    for d in (0, 1):
                        b, L = V[d], links[d]
                        cs = b["CS"]
                        ve.wait_ge(s_pe[d].sem, s_pe[d].at(it, "g4r"))
                        L("cbm", v_.tensor_tensor(grp(b["CBM"], a=2), grp(ps[4 * d + 3][:, 0:256], a=2),
                                                  TRI[d].unsqueeze(1).broadcast_to([P, 2, P]), ALU.mult))
                        L("g4r", v_.tensor_copy(b["G4R"], ps[4 * d][0:4, 0:P]))
                        L("r4", v_.tensor_tensor_scan(b["R4"], b["G4R"], b["G4R"], b["MC"], ALU.max, ALU.max))
                        mid = cs[:, BL // 2:P:BL]
                        kt = grp(b["KT"], a=NB)
                        L("kta", v_.tensor_tensor(kt, cs[:, 0:P].unsqueeze(1).broadcast_to([P, NB, P]),
                                                  hb(mid, NB, P), ALU.subtract))
                        L("ktb", v_.tensor_scalar(b["KT"], b["KT"], -CLAMP, None, ALU.max))
                        L("qba", v_.tensor_tensor(grp(b["QB"], a=NB), grp(cs[:, 0:P], a=NB), hb(mid, NB, BL),
                                                  ALU.subtract))
                        L("qbb", v_.tensor_scalar(b["QB"], b["QB"], CLAMP, None, ALU.min))
                    for d in (0, 1):
                        b, L = V[d], links[d]
                        gqT, gkT = b["FT"][:, 0:P], b["FT"][:, P:2 * P]
                        ve.wait_ge(s_pe[d].sem, s_pe[d].at(it, "km"))
                        L("gg8", v_.tensor_copy(b["GG8"], ps[4 * d][:, 128:136]))
                        ve.wait_ge(s_act[d].sem, s_act[d].at(it, "kd"))
                        L("qh", v_.tensor_tensor(b["QH"], b["EB"], gqT, ALU.mult))
                        L("kdm", v_.tensor_tensor(b["KD"], b["KD"], gkT, ALU.mult))
                        ve.wait_ge(s_act[d].sem, s_act[d].at(it, "qb"))
                        for h in range(GH):
                            r = slice(GDK * h, GDK * h + GDK)
                            L(f"qp{h}", v_.tensor_tensor(
                                b["QP"][r, :].rearrange("p (b h i) -> p b h i", b=NB, h=GH)[:, :, h, :],
                                b["QB"][r, :].rearrange("p (b i) -> p b i", b=NB),
                                b["FT"][r, 0:P].rearrange("p (b i) -> p b i", b=NB), ALU.mult))
                        L("ktm", v_.tensor_tensor(grp(b["KT"], a=NB), grp(b["KT"], a=NB),
                                                  gkT.unsqueeze(1).broadcast_to([P, NB, P]), ALU.mult))
                    for d in (0, 1):
                        b, L = V[d], links[d]
                        cs, ema = b["CS"], b["EMA"]
                        ve.wait_ge(s_pe[d].sem, s_pe[d].at(it, "kdt"))
                        L("gt", v_.tensor_copy(b["GT"], ps[4 * d][:, 136:140]))
                        L("kmd", v_.tensor_copy(b["KMD"], ps[4 * d + 2][:, 0:3 * P]))
                        L("em0", v_.tensor_tensor(ema[:, 0:4], b["MB"], b["GT"], ALU.subtract))
                        L("em1", v_.scalar_tensor_tensor(ema[:, 4:8], cs[:, 128:132], -1.0, b["GT"],
                                                         ALU.mult, ALU.subtract))
                        L("em2", v_.tensor_tensor(ema[:, 8:12], b["G4"], b["GG8"][:, 4:8], ALU.subtract))
                        L("em3", v_.tensor_tensor(ema[:, 12:16], b["MB"], b["GG8"][:, 4:8], ALU.subtract))
                        ve.wait_ge(s_act[d].sem, s_act[d].at(it, "ex1"))
                        ex = b["EX"].rearrange("p (g r s) -> p g r s", g=2, r=4)
                        L("w8", v_.tensor_tensor(ex, ex, grp(b["CBM"], a=2).unsqueeze(2).broadcast_to([P, 2, 4, P]),
                                                 ALU.mult))
                        ve.wait_ge(s_act[d].sem, s_act[d].at(it, "ea"))
                        ve.wait_ge(s_pool[d].sem, s_pool[d].at(it, "xd"))
                        L("xw", v_.tensor_tensor(grp(b["XW"], a=SH), grp(b["XD"], a=SH),
                                                 hb(b["EA"][:, 21:29], SH, HD), ALU.mult))
                        ve.wait_ge(s_pe[d].sem, s_pe[d].at(it, "qk"))
                        L("qkm", v_.tensor_tensor(grp(b["T1"], a=4), grp(ps[4 * d + 3][:, :], a=4),
                                                  TRI[d].unsqueeze(1).broadcast_to([P, 4, P]), ALU.mult))
                    for d in (0, 1):
                        b, L = V[d], links[d]
                        ve.wait_ge(s_pe[d].sem, s_pe[d].at(it, "gb"))
                        for h in range(MH):
                            L(f"me{h}", v_.tensor_scalar(b["ME"][:, h * P:(h + 1) * P], ps[4 * d][:, h * P:(h + 1) * P],
                                                         b["G4"][:, h:h + 1], 0.0, ALU.subtract, ALU.max))
                        ve.wait_ge(s_pe[d].sem, s_pe[d].at(it, "ssd"))
                        ve.wait_ge(s_st[d].sem, s_st[d].at(it, "st", 1))
                        L("ys0", v_.tensor_tensor(grp(b["Y"][:, 512:], a=SH), grp(ps[4 * d + 2][:, :], a=SH),
                                                  hb(b["EA"][:, 0:8], SH, HD), ALU.mult))
                        L("ys1", v_.tensor_tensor(b["Y"][:, 512:], b["Y"][:, 512:], ps[4 * d + 1][:, :], ALU.add))
                    for d in (0, 1):
                        b, L = V[d], links[d]
                        ve.wait_ge(s_act[d].sem, s_act[d].at(it, "me"))
                        L("wm", v_.tensor_tensor(b["ME"], b["ME"], b["T1"], ALU.mult))
                        ve.wait_ge(s_pe[d].sem, s_pe[d].at(it, "att"))
                        L("at", v_.tensor_tensor(
                            b["AT"].rearrange("p (h b i) -> p h b i", h=GH, b=NB),
                            ps[4 * d][:, :].rearrange("p (b h i) -> p h b i", b=NB, h=GH),
                            TRI[d].rearrange("p (b i) -> p b i", b=NB).unsqueeze(1).broadcast_to([P, GH, NB, BL]),
                            ALU.mult))
                        ve.wait_ge(s_pe[d].sem, s_pe[d].at(it, "ups"))
                        L("t1", v_.tensor_tensor(b["T1"], ps[4 * d + 3][:, :], GM[:, S_SSD:S_ML], ALU.mult))
                    for d in (0, 1):
                        b, L = V[d], links[d]
                        sn, st, em = b["SN"], b["ST"], b["EM"]
                        ve.wait_ge(s_pe[d].sem, s_pe[d].at(it, "mli"))
                        L("hm0", v_.tensor_tensor(grp(b["HM"], a=MH), grp(ps[4 * d + 2][:, 0:VA], a=MH),
                                                  hb(em[:, 0:4], MH, HD + 1), ALU.mult))
                        L("hm1", v_.tensor_tensor(b["HM"], b["HM"], ps[4 * d + 1][:, 0:VA], ALU.add))
                        hm = grp(b["HM"], a=MH)
                        L("dn0", v_.scalar_tensor_tensor(b["DN"].unsqueeze(2), hm[:, :, HD:HD + 1], -1.0,
                                                         hm[:, :, HD:HD + 1], ALU.mult, ALU.max))
                        L("dn1", v_.tensor_tensor(b["DN"], b["DN"], em[:, 4:8], ALU.max))
                        L("rc", v_.reciprocal(b["RC"], b["DN"]))
                        L("ym", v_.tensor_tensor(grp(b["Y"][:, 256:512], a=MH), hm[:, :, 0:HD], hb(b["RC"], MH, HD), ALU.mult))
                        ve.wait_ge(s_pe[d].sem, s_pe[d].at(it, "upg"))
                        L("yg", v_.tensor_copy(b["Y"][:, 0:256], ps[4 * d][:, 0:256]))
                        L("t3", v_.tensor_tensor(b["T3"], ps[4 * d][:, 256:512], GM[:, S_GLA:S_W], ALU.mult))
                        L("sng", v_.scalar_tensor_tensor(sn[:, S_GLA:S_W], st[:, S_GLA:S_W], b["EA"][:, 20:21], b["T3"],
                                                         ALU.mult, ALU.add))
                        ve.wait_ge(s_pe[d].sem, s_pe[d].at(it, "upm"))
                        L("t2", v_.tensor_tensor(b["T2"], ps[4 * d + 3][:, 0:VA], GM[:, S_ML:S_GLA], ALU.mult))
                        L("last", v_.tensor_tensor(b["MN"], b["F4"], b["R4"][:, P - 1:P], ALU.add))
                meet(ve, l * PHASES + 3)

                ve.wait_ge(e_par, (l + 1) * 144)

                def mix(t):
                    link = linker(ve, o_dve, t)
                    ve.wait_ge(o_ld.sem, o_ld.at(t, "ld"))
                    yf = YF
                    link("y0", v_.tensor_tensor(yf, YF, YB, ALU.add))
                    yield
                    tx = grp(TX3, a=SH)
                    link("y1", v_.tensor_tensor(tx, tx, DROW.unsqueeze(2).broadcast_to([P, SH, HD]), ALU.mult))
                    yield
                    link("y2", v_.tensor_tensor(yf[:, 512:], yf[:, 512:], TX3, ALU.add))
                    yield
                    link("y3", v_.tensor_tensor(yf, yf, GO, ALU.mult))
                    yield
                    ve.wait_ge(q_pe.sem, q_pe.at(t, "q7", 1))
                    link("sq", v_.tensor_tensor(SQ, yf, yf, ALU.mult))
                    yield
                    link("hr", v_.tensor_reduce(HR, grp(SQ, a=16), AX, ALU.add))
                    yield
                    link("hrm", v_.tensor_scalar(HR2, HR, 1.0 / HD, EPS, ALU.mult, ALU.add))
                    yield
                    ve.wait_ge(o_act.sem, o_act.at(t, "hsd"))
                    link("hrr", v_.reciprocal(HR3, HR3))
                    yield
                    link("yn1", v_.tensor_tensor(grp(yf, a=16), grp(yf, a=16),
                                                 HR3.unsqueeze(2).broadcast_to([P, 16, HD]), ALU.mult))
                    yield
                    link("yn2", v_.tensor_tensor(yf, yf, GNW, ALU.mult))
                    yield
                    ve.wait_ge(o_pe.sem, o_pe.at(t, "yt0"))
                    link("yt0", v_.tensor_copy(YT[:, 0:512], ps[0][:, :]))
                    yield
                    ve.wait_ge(o_pe.sem, o_pe.at(t, "out"))
                    ve.wait_ge(o_ldx.sem, o_ldx.at(t, "ld"))
                    for h in (0, 1):
                        c = slice(512 * h, 512 * h + 512)
                        link(f"g{h}", v_.tensor_tensor(G1[:, c], ps[2 + h][:, :], G1[:, c], ALU.mult))
                        yield
                    link("r1", v_.scalar_tensor_tensor(XO, XO, ALPHA, G1, ALU.mult, ALU.add))
                    yield
                    yield from stats(link, "a", XO, oST6, oMV)
                    ve.wait_ge(o_act.sem, o_act.at(t, "sda"))
                    link("rsa", v_.reciprocal(oRS, oSD))
                    yield
                    link("x1a", v_.tensor_scalar(XO, XO, oMV[:, 0:1], oRS, ALU.subtract, ALU.mult))
                    yield
                    link("x1b", v_.tensor_tensor(XO, XO, L1W, ALU.mult))
                    yield
                    link("x1c", v_.tensor_tensor(XO, XO, L1B, ALU.add))
                    yield
                    yield from stats(link, "b", XO, oST6, oMV)
                    ve.wait_ge(o_act.sem, o_act.at(t, "sdb"))
                    link("rsb", v_.reciprocal(oRS, oSD))
                    yield
                    link("u2a", v_.tensor_scalar(G1, XO, oMV[:, 0:1], oRS, ALU.subtract, ALU.mult))
                    yield
                    link("u2b", v_.scalar_tensor_tensor(SC2, SC2, 1.0, G1, ALU.add, ALU.mult))
                    yield
                    link("u2c", v_.tensor_tensor(SC2, SC2, SH2, ALU.add))
                    yield

                def scores(t, indices_taken):
                    link = linker(ve, q_dve, t)

                    def best(n, rows_, top, at):
                        steps = (lambda: v_.max(top[:, 0:8], rows_),
                                 lambda: v_.max_index(at[:, 0:8], top[:, 0:8], rows_),
                                 lambda: v_.match_replace(rows_, top[:, 0:8], rows_, -3.0e38),
                                 lambda: v_.max(top[:, 8:16], rows_),
                                 lambda: v_.max_index(at[:, 8:16], top[:, 8:16], rows_))
                        for k, step in enumerate(steps):
                            ve.sem_inc(passed, 1)
                            link(f"{n}.{k}", step())
                            yield

                    ve.wait_ge(q_pe.sem, q_pe.at(t, "ut0"))
                    link("ut0", v_.tensor_copy(U2T[:, 0:512], ps[0][:, :]))
                    yield
                    ve.wait_ge(q_pe.sem, q_pe.at(t, "q3"))
                    link("qt0", v_.tensor_copy(QT[:, 0:512], ps[2][:, :]))
                    yield
                    ve.wait_ge(q_act.sem, q_act.at(t, "sc3"))
                    for i in range(16):
                        yield from best(f"half{i}", SCO[:, i * P:(i + 1) * P], TV[:, 16 * i:16 * i + 16],
                                        TI[:, 16 * i:16 * i + 16].bitcast(U32))
                    link("tf", v_.tensor_copy(TI, TI.bitcast(U32)))
                    yield
                    tv4 = TV.rearrange("p (h q a) -> p h q a", h=HEADS, q=2)
                    tf4 = TI.rearrange("p (h q a) -> p h q a", h=HEADS, q=2)
                    can4 = CAN.rearrange("p (h a b) -> p h a b", h=HEADS, a=TOPK)
                    full = [P, HEADS, TOPK, TOPK]
                    link("can", v_.tensor_tensor(can4, tv4[:, :, 0, :].unsqueeze(3).broadcast_to(full),
                                                 tv4[:, :, 1, :].unsqueeze(2).broadcast_to(full), ALU.add))
                    yield
                    for h in range(HEADS):
                        yield from best(f"pair{h}", CAN[:, h * 256:(h + 1) * 256], BV[:, 16 * h:16 * h + 16],
                                        BI[:, 16 * h:16 * h + 16].bitcast(U32))
                    for q, (op, by, dst) in enumerate(((ALU.logical_shift_right, 4, IFR), (ALU.bitwise_and, 15, JFR))):
                        link(f"ba{q}", v_.tensor_scalar(BA1.bitcast(U32), BI.bitcast(U32), by, None, op))
                        yield
                        link(f"bf{q}", v_.tensor_copy(BA1, BA1.bitcast(U32)))
                        yield
                        link(f"oh{q}", v_.tensor_tensor(grp(OH, a=P), BA1.unsqueeze(2).broadcast_to([P, P, TOPK]),
                                                        IOTA.unsqueeze(1).broadcast_to([P, P, TOPK]), ALU.is_equal))
                        yield
                        link(f"oi{q}", v_.tensor_tensor(can4, can4, tf4[:, :, q, :].unsqueeze(2).broadcast_to(full), ALU.mult))
                        yield
                        link(f"oj{q}", v_.tensor_reduce(dst, grp(OH, a=P), AX, ALU.add))
                        yield
                    link("ixa", v_.scalar_tensor_tensor(IFR, IFR, 128.0, JFR, ALU.mult, ALU.add))
                    yield
                    ve.wait_ge(e_pool.sem, indices_taken)
                    link("ixb", v_.tensor_scalar(IDXN.bitcast(U32), IFR, LOFS, None, ALU.add))
                    yield
                    bv3 = grp(BV, a=HEADS)
                    link("sma", v_.tensor_tensor(grp(JFR, a=HEADS), bv3, bv3[:, :, 0:1].broadcast_to([P, HEADS, TOPK]),
                                                 ALU.subtract))
                    yield
                    ve.wait_ge(q_act.sem, q_act.at(t, "sme"))
                    link("smb", v_.tensor_reduce(SM, grp(IFR, a=HEADS), AX, ALU.add))
                    yield
                    link("smc", v_.reciprocal(SR, SM))
                    yield
                    link("smd", v_.tensor_tensor(grp(GWN, a=HEADS), grp(IFR, a=HEADS),
                                                 SR.unsqueeze(2).broadcast_to([P, HEADS, TOPK]), ALU.mult))

                def whole_round(t, indices_taken):
                    yield from mix(t)
                    yield from scores(t, indices_taken)

                for _ in whole_round(l * ROUNDS, e_pool.at(l * TILES, "ix1", 1)):
                    pass
                ve.sem_inc(passed, 1)
                with ve.Fori(0, TILES) as s:
                    it = l * TILES + s
                    link = linker(ve, e_dve, it)
                    beside = whole_round(l * ROUNDS + 1 + s, e_pool.at(it, "ix1"))
                    link("gwc", v_.tensor_copy(GWC, GWN))
                    ve.wait_ge(e_u.sem, e_u.at(it, "u"))

                    def dots(g):
                        for n in range(GRP * g, GRP * g + GRP):
                            r, j = divmod(n, RING)
                            ve.wait_ge(e_gat[j].sem, e_gat[j].at(it, f"g{r}"))
                            link(f"dot{n}", v_.tensor_tensor_reduce(
                                ring[:, j, 0:D], ring[:, j, 0:D], EU, 1.0, 0.0, ALU.mult, ALU.add,
                                DOT[:, n % 16:n % 16 + 1]))
                            steps = DVE_STEPS.get(n, 0)
                            if TOP_FIRST <= n < TOP_LAST or n >= SUM_FIRST:
                                steps = 3 + n % 2
                            for _ in range(steps):
                                next(beside, None)

                    def weigh(g):
                        c = slice(GRP * g % 16, GRP * g % 16 + GRP)
                        ve.wait_ge(e_act.sem, e_act.at(it, f"ge{g}"))
                        link(f"aw{g}", v_.tensor_tensor(AW[:, c], AG[:, c], GWC[:, GRP * g:GRP * g + GRP], ALU.mult))

                    dots(0)
                    for g in range(1, SLOTS // GRP):
                        dots(g)
                        weigh(g - 1)
                    weigh(SLOTS // GRP - 1)
                    for _ in beside:
                        pass
                    ve.wait_ge(e_x.sem, e_x.at(it, "x"))
                    ve.wait_ge(e_pe.sem, e_pe.at(it, f"v{SLOTS - 1}"))
                    for h in (0, 1):
                        c = slice(512 * h, 512 * h + 512)
                        link(f"r0{h}", v_.tensor_tensor(EG2[:, c], ps[4 + h][:, :], EG2[:, c], ALU.mult))
                    link("r1", v_.scalar_tensor_tensor(EX1, EX1, ALPHA, EG2, ALU.mult, ALU.add))
                    for _ in stats(link, "", EX1, eST6, eMV):
                        pass
                    ve.wait_ge(e_act.sem, e_act.at(it, "sd"))
                    link("r2", v_.reciprocal(eRS, eSD))
                    link("xa", v_.tensor_scalar(EX1, EX1, eMV[:, 0:1], eRS, ALU.subtract, ALU.mult))
                    link("xw", v_.tensor_tensor(EX1, EX1, L2W, ALU.mult))
                    link("xb", v_.tensor_tensor(EX1, EX1, L2B, ALU.add))
                meet(ve, l * PHASES + 4)

        @block.scalar
        def _(ae):
            give_credit(ae, act_own)
            a_ = nc.scalar

            ae.wait_ge(start_ld, 32)
            ae.activation(CS2, CT, ACT.Silu).then_inc(sem_silu, 1)
            ae.wait_ge(sem_ones, 2)
            ae.sem_inc(passed, 1)
            with ae.Fori(0, DEPTH) as l:
                with ae.Fori(0, 6) as jj:
                    it = l * 6 + jj
                    for u in (0, 1):
                        cols = bass.ds(jj * 1024 + u * 512, 512)
                        apart(ae, m_dve.sem, m_dve.at(it, f"mod{u}"))
                        ae.dma_start(at1(modd, l)[:, cols], MO[u]).then_inc(m_out[u].sem, 16)
            for u in (0, 1):
                apart(ae, m_out[u].sem, m_out[u].at(DEPTH * 6 - 1, "out"))
            meet(ae, 0)
            ae.sem_inc(passed, 1)
            with ae.Fori(0, DEPTH) as l:
                link = linker(ae, pl_act, l)
                ae.wait_ge(p_par, (l + 1) * 96)
                link("ea", a_.activation(ALOG, ALOG, ACT.Exp))

                def root(t):
                    link = linker(ae, n_act, t)
                    ae.wait_ge(n_dve.sem, n_dve.at(t, "mv"))
                    link("sd", a_.activation(SD, MV[:, 1:2], ACT.Sqrt, bias=eps))

                root(l * ROUNDS)
                ae.sem_inc(passed, 1)
                with ae.Fori(0, TILES) as s:
                    it = l * TILES + s
                    link = linker(ae, p_act, it)
                    ae.wait_ge(p_pe.sem, p_pe.at(it, "tr1"))
                    ae.wait_ge(p_pe.sem, p_pe.at(it, "last", 1))
                    link("ut1", a_.activation(UT[:, 512:1024], ps[1][:, :], ACT.Copy))
                    ae.wait_ge(p_pe.sem, p_pe.at(it, "A"))
                    ae.wait_ge(p_st.sem, p_st.at(it, "st", 1))
                    link("a1", a_.activation(FA[:, 0:P], ps[2][:, 0:P], ACT.Copy, scale=GDK ** -0.5))
                    link("a2", a_.activation(FA[:, P:4 * P], ps[2][:, P:4 * P], ACT.Copy))
                    ae.wait_ge(p_pe.sem, p_pe.at(it, "B"))
                    link("b1", a_.activation(CP[:, 0:2 * P], ps[3][:, 2 * P:4 * P], ACT.Copy))
                    link("b2", a_.activation(FA[:, 4 * P:6 * P], ps[3][:, 0:2 * P], ACT.Copy, scale=HD ** -0.5))
                    root(l * ROUNDS + 1 + s)
                    ae.wait_ge(p_dve.sem, p_dve.at(it, "za"))
                    link("ze", a_.activation(ZA, ZA, ACT.Exp, scale=-1.0))
                    link("ln", a_.activation(ZL, ZA, ACT.Ln, bias=ones[:, 0:1]))
                    ae.wait_ge(p_pe.sem, p_pe.at(it, "last"))
                    link("silug", a_.activation(GG[:, 0:256], ps[7][:, 0:256], ACT.Silu))
                    link("siluz", a_.activation(GG[:, 512:1024], ps[4][:, :], ACT.Silu))
                    link("sigmo", a_.activation(GG[:, 256:512], ps[7][:, 256:512], ACT.Sigmoid))
                meet(ae, l * PHASES + 1)

                ae.wait_ge(c_par, (l + 1) * 32)
                link = linker(ae, c_act, l)

                def tokens(c):
                    w = slice(c * P, c * P + P)
                    ae.wait_ge(c_pe.sem, c_pe.at(l, f"t{c}"))
                    link(f"four{c}", a_.activation(CTK[:, 1:, w], grp(ps[2 * (c % 4)][:, :], a=4), ACT.Copy))
                    link(f"alone{c}", a_.activation(CTK[:, 0, w], ps[2 * (c % 4) + 1][:, 0:P], ACT.Copy))

                for c in range(6):
                    ae.wait_ge(c_dve.sem, c_dve.at(l, f"c{c}"))
                    link(f"silu{c}", a_.activation(CO[:, c, :], CV[:, c, :], ACT.Silu, bias=CB_[:, c:c + 1]))
                    if c:
                        tokens(c - 1)
                meet(ae, l * PHASES + 2)

                ae.sem_inc(passed, 1)
                with ae.Fori(0, TILES) as s:
                    it = l * TILES + s
                    links = [linker(ae, s_act[d], it) for d in (0, 1)]
                    for d in (0, 1):
                        b, L = sc[d], links[d]
                        cs = b["CS"]
                        ae.wait_ge(s_dve[d].sem, s_dve[d].at(it, "dec"))
                        L("ea", a_.activation(b["EA"], cs[:, 132:161], ACT.Exp))
                        L("eb", a_.activation(b["EB"], cs[:, 0:P], ACT.Exp))
                        L("kd", a_.activation(b["KD"], cs[:, 0:P], ACT.Exp, bias=cs[:, 152:153], scale=-1.0))
                        for q in (0, 1):
                            ae.wait_ge(s_dve[d].sem, s_dve[d].at(it, f"ex{4 * q + 3}"))
                            L(f"ex{q}", a_.activation(b["EX"][:, 512 * q:512 * q + 512],
                                                      b["EX"][:, 512 * q:512 * q + 512], ACT.Exp))
                    for d in (0, 1):
                        b, L = sc[d], links[d]
                        ae.wait_ge(s_dve[d].sem, s_dve[d].at(it, "qbb"))
                        L("kt", a_.activation(b["KT"], b["KT"], ACT.Exp, scale=-1.0))
                        L("qb", a_.activation(b["QB"], b["QB"], ACT.Exp))
                    for d in (0, 1):
                        b, L = sc[d], links[d]
                        ae.wait_ge(s_dve[d].sem, s_dve[d].at(it, "em3"))
                        L("em", a_.activation(b["EM"], b["EMA"], ACT.Exp))
                    for d in (0, 1):
                        b, L = sc[d], links[d]
                        ae.wait_ge(s_dve[d].sem, s_dve[d].at(it, "me3"))
                        L("me", a_.activation(b["ME"], b["ME"], ACT.Exp, scale=-1.0))
                meet(ae, l * PHASES + 3)

                def mix(t):
                    link = linker(ae, o_act, t)
                    ae.wait_ge(o_dve.sem, o_dve.at(t, "hrm"))
                    link("hsd", a_.activation(HR3, HR2, ACT.Sqrt))
                    yield
                    ae.wait_ge(o_pe.sem, o_pe.at(t, "yt1"))
                    link("yt1", a_.activation(YT[:, 512:1024], ps[1][:, :], ACT.Copy))
                    yield
                    ae.wait_ge(o_dve.sem, o_dve.at(t, "mva"))
                    link("sda", a_.activation(oSD, oMV[:, 1:2], ACT.Sqrt, bias=eps))
                    yield
                    ae.wait_ge(o_dve.sem, o_dve.at(t, "mvb"))
                    link("sdb", a_.activation(oSD, oMV[:, 1:2], ACT.Sqrt, bias=eps))
                    yield

                def scores(t):
                    link = linker(ae, q_act, t)
                    ae.wait_ge(q_pe.sem, q_pe.at(t, "ut1"))
                    link("ut1", a_.activation(U2T[:, 512:1024], ps[1][:, :], ACT.Copy))
                    yield
                    ae.wait_ge(q_pe.sem, q_pe.at(t, "q7"))
                    link("qt1", a_.activation(QT[:, 512:1024], ps[3][:, :], ACT.Copy))
                    yield
                    for b in range(4):
                        ae.wait_ge(q_pe.sem, q_pe.at(t, f"s{b}"))
                        link(f"sc{b}", a_.activation(SCO[:, 512 * b:512 * b + 512], ps[b][:, :], ACT.Copy))
                    yield
                    ae.wait_ge(q_dve.sem, q_dve.at(t, "sma"))
                    link("sme", a_.activation(IFR, JFR, ACT.Exp))

                def whole_round(t):
                    yield from mix(t)
                    yield from scores(t)

                for _ in whole_round(l * ROUNDS):
                    pass
                ae.sem_inc(passed, 1)
                with ae.Fori(0, TILES) as s:
                    it = l * TILES + s
                    link = linker(ae, e_act, it)
                    beside = whole_round(l * ROUNDS + 1 + s)

                    def gelu(g):
                        c = slice(GRP * g % 16, GRP * g % 16 + GRP)
                        ae.wait_ge(e_dve.sem, e_dve.at(it, f"dot{GRP * g + GRP - 1}"))
                        link(f"ge{g}", a_.activation(AG[:, c], DOT[:, c], ACT.Gelu))

                    def diag(g):
                        ae.wait_ge(e_dve.sem, e_dve.at(it, f"aw{g}"))
                        for n in range(GRP * g, GRP * g + GRP):
                            if n < DIAGS:
                                ae.wait_ge(e_pe.sem, e_pe.at(it, f"v{n + SLOTS - DIAGS}", 1))
                            else:
                                ae.wait_ge(e_pe.sem, e_pe.at(it, f"v{n - DIAGS}"))
                            link(f"dg{n}", a_.activation(DG[:, n % DIAGS * P:(n % DIAGS + 1) * P], ident, ACT.Copy,
                                                         scale=AW[:, n % 16:n % 16 + 1]))
                    gelu(0)
                    for g in range(1, SLOTS // GRP):
                        gelu(g)
                        diag(g - 1)
                        for _ in range(ACT_STEPS.get(GRP * g, 0)):
                            next(beside, None)
                    diag(SLOTS // GRP - 1)
                    ae.wait_ge(e_dve.sem, e_dve.at(it, "mv"))
                    link("sd", a_.activation(eSD, eMV[:, 1:2], ACT.Sqrt, bias=eps))
                meet(ae, l * PHASES + 4)

        @block.tensor
        def _(pe):
            give_credit(pe, pe_own)
            mm = nc.tensor.matmul

            pe.wait_ge(sem_silu, 1)
            pe.wait_ge(sem_ones, 2)
            pe.sem_inc(passed, 1)
            with pe.Fori(0, DEPTH) as l:
                pe.sem_inc(passed, 1)
                with pe.Fori(0, 6) as jj:
                    it = l * 6 + jj
                    mark = marker(m_pe)
                    for u in (0, 1):
                        pe.wait_ge(m_w[u].sem, m_w[u].at(it, "w"))
                        pe.wait_ge(m_dve.sem, m_dve.at(it, f"mod{u}", 1))
                        for k in range(KC):
                            i = mm(ps[u][0:2, :], CS2[:, 2 * k:2 * k + 2], WA[u][:, 512 * k:512 * k + 512],
                                   start=(k == 0), stop=(k == KC - 1))
                        mark(f"mod{u}", i)
            meet(pe, 0)

            def turn(bank, src, first):
                for c in range(4):
                    i = nc.tensor.transpose(bank[:, c * P:(c + 1) * P], src[:, (first + c) * P:(first + c + 1) * P], ident)
                return i

            pe.sem_inc(passed, 1)
            with pe.Fori(0, DEPTH) as l:
                pe.wait_ge(p_par, (l + 1) * 96)
                pe.sem_inc(passed, 1)
                with pe.Fori(0, TILES) as s:
                    it = l * TILES + s
                    mark = marker(p_pe)

                    def weights(q):
                        pe.wait_ge(p_w[q], (l + 1) * 16 * len(W_IN_PARTS[q]))
                    pe.wait_ge(n_dve.sem, n_dve.at(l * ROUNDS + s, "xsh"))
                    mark("tr0", turn(ps[0], U, 0))
                    mark("tr1", turn(ps[1], U, 4))
                    pe.wait_ge(p_dve.sem, p_dve.at(it, "ut0"))
                    pe.wait_ge(p_act.sem, p_act.at(it, "ut1"))

                    def feature_major(bank, blocks):
                        for q, (c0, m) in enumerate(blocks):
                            for k in range(KC):
                                i = mm(bank[0:m, q * P:(q + 1) * P], win[:, k, c0:c0 + m], UT[:, k * P:(k + 1) * P],
                                       start=(k == 0), stop=(k == KC - 1))
                        return i

                    def token_major(out, c0, n):
                        for k in range(KC):
                            i = mm(out, UT[:, k * P:(k + 1) * P], win[:, k, c0:c0 + n], start=(k == 0), stop=(k == KC - 1))
                        return i

                    weights(0)
                    mark("A", feature_major(ps[2], [(O_GQ, P), (O_GK, P), (O_MQ, P), (O_MQ + P, P)]))
                    weights(1)
                    mark("B", feature_major(ps[3], [(O_MK, P), (O_MK + P, P), (O_SX, P), (O_SX + P, P)]))
                    pe.wait_ge(p_act.sem, p_act.at(it, "sigmo", 1))
                    mark("C", feature_major(ps[4], [(O_SX + 2 * P, P), (O_SX + 3 * P, P), (O_SB, P), (O_SB + P, P)]))
                    pe.wait_ge(p_dve.sem, p_dve.at(it, "dt", 1))
                    token_major(ps[5][:, 128:144], O_MI, 16)
                    token_major(ps[5][:, 144:160], O_SDT, 16)
                    mark("D", feature_major(ps[5], [(O_GA, 32)]))
                    weights(2)
                    mark("E1", token_major(ps[6][:, 0:256], O_GV, 256))
                    mark("E", token_major(ps[6][:, 256:512], O_MV, 256))
                    pe.wait_ge(p_dve.sem, p_dve.at(it, "gat"))
                    mark("gate", mm(ps[5][:, 160:416], GAT, WA2, start=True, stop=True))
                    token_major(ps[7][:, 0:256], O_GG, 256)
                    token_major(ps[7][:, 256:512], O_MO, 256)
                    weights(3)
                    pe.wait_ge(p_dve.sem, p_dve.at(it, "c4"))
                    mark("last", token_major(ps[4][:, :], O_SZ, 512))
                meet(pe, l * PHASES + 1)

                mark = marker(c_pe)
                for c in range(5):
                    pe.wait_ge(c_act.sem, c_act.at(l, f"silu{c}"))
                    if c >= 4:
                        pe.wait_ge(c_act.sem, c_act.at(l, f"alone{c - 4}"))
                    for q in range(4):
                        nc.tensor.transpose(ps[2 * (c % 4)][:, q * P:(q + 1) * P], CO[:, c, (2 + q) * P:(3 + q) * P], ident)
                    mark(f"t{c}", nc.tensor.transpose(ps[2 * (c % 4) + 1][:, 0:P], CO[:, c, 0:P], ident))
                meet(pe, l * PHASES + 2)

                pe.wait_ge(s_con, (l + 1) * 80)
                pe.sem_inc(passed, 1)
                with pe.Fori(0, TILES) as s:
                    it = l * TILES + s
                    marks = [marker(s_pe[d]) for d in (0, 1)]
                    i4 = ident[0:4, 0:4]
                    for d in (0, 1):
                        b, M = sc[d], marks[d]
                        la = b["TK"][:, 256 + VA:256 + VA + NDIR]
                        b0, b1, b2, b3 = ps[4 * d:4 * d + 4]
                        pe.wait_ge(s_ld[d].sem, s_ld[d].at(it, "ld"))
                        pe.wait_ge(s_dve[d].sem, s_dve[d].at(it, "last", 1))
                        mm(b0[:, 0:P], la[:, 0:P], TRI[d], start=True, stop=True)
                        mm(b0[:, 128:140], TRI[d], la[:, P:NDIR], start=True, stop=True)
                        mm(b0[:, 140:152], ones, la[:, P:NDIR], start=True, stop=True)
                        mm(b0[:, 152:153], la[:, 0:P], ones[:, 0:1], start=True, stop=True)
                        mm(b0[0:4, 153:154], la[:, 128:132], ones[:, 0:1], start=True, stop=True)
                        for h in range(SH):
                            i = mm((b1, b2)[h // 4][:, h % 4 * P:(h % 4 + 1) * P],
                                   la[:, 132 + h:133 + h].broadcast_to([P, P]), TRI[d], start=True, stop=True)
                        M("cum", i)
                    for d in (0, 1):
                        b, M = sc[d], marks[d]
                        b0, b1, b2, b3 = ps[4 * d:4 * d + 4]
                        pe.wait_ge(s_ls[d].sem, s_ls[d].at(it, "ls"))
                        pe.wait_ge(s_pool[d].sem, s_pool[d].at(it, "qm1"))
                        pe.wait_ge(s_dve[d].sem, s_dve[d].at(it, "g4"))
                        mm(b3[:, 0:256], b["FX"][:, 0:P], b["CTP"], start=True, stop=True)
                        M("g4r", mm(b0[0:4, 0:P], b["G4"], PERM[d], start=True, stop=True))
                    for d in (0, 1):
                        b, M = sc[d], marks[d]
                        b0, b1, b2, b3 = ps[4 * d:4 * d + 4]
                        pe.wait_ge(s_dve[d].sem, s_dve[d].at(it, "r4"))
                        mm(b0[:, 128:132], b["R4"], i4, start=True, stop=True)
                        mm(b0[:, 132:136], b["R4"][:, P - 1:P].broadcast_to([4, P]), i4, start=True, stop=True)
                        pe.wait_ge(s_dve[d].sem, s_dve[d].at(it, "ex7"))
                        nc.tensor.transpose(b2[:, 0:P], b["FT"][:, 4 * P:5 * P], ident)
                        M("km", nc.tensor.transpose(b2[:, P:2 * P], b["FT"][:, 5 * P:6 * P], ident))
                        for j in (0, 1):
                            i = mm(b3[:, 256 * j:256 * j + 256], b["FT"][:, (4 + j) * P:(5 + j) * P],
                                   b["QMP"][:, 256 * j:256 * j + 256], start=True, stop=True)
                        M("qk", i)
                    for d in (0, 1):
                        b, M = sc[d], marks[d]
                        b0, b1, b2, b3 = ps[4 * d:4 * d + 4]
                        pe.wait_ge(s_dve[d].sem, s_dve[d].at(it, "kdm"))
                        mm(b0[:, 136:140], PERM[d], b["GG8"][:, 0:4], start=True, stop=True)
                        M("kdt", nc.tensor.transpose(b2[:, 2 * P:3 * P], b["KD"], ident))
                    for d in (0, 1):
                        b, M = sc[d], marks[d]
                        b0, b1, b2, b3 = ps[4 * d:4 * d + 4]
                        pe.wait_ge(s_dve[d].sem, s_dve[d].at(it, "kmd"))
                        for h in range(MH):
                            i = mm(b0[:, h * P:(h + 1) * P], b["GT"][:, h:h + 1].broadcast_to([P, P]), ident,
                                   start=True, stop=True)
                        M("gb", i)
                        pe.wait_ge(s_dve[d].sem, s_dve[d].at(it, "w8"))
                        pe.wait_ge(s_pool[d].sem, s_pool[d].at(it, "xd"))
                        for h in range(SH):
                            mm(b1[:, h * HD:(h + 1) * HD], b["EX"][:, h * P:(h + 1) * P], b["XD"][:, h * HD:(h + 1) * HD],
                               start=True, stop=True)
                        M("ssd", mm(b2[:, :], b["FX"][:, P:2 * P], b["ST"][:, S_SSD:S_ML], start=True, stop=True))
                    for d in (0, 1):
                        b, M = sc[d], marks[d]
                        b0, b1, b2, b3 = ps[4 * d:4 * d + 4]
                        pe.wait_ge(s_dve[d].sem, s_dve[d].at(it, "me3"))
                        for c in range(NB):
                            i = mm(b0[:, c * GH * BL:(c + 1) * GH * BL], b["KT"][:, c * P:(c + 1) * P],
                                   b["QP"][:, c * GH * BL:(c + 1) * GH * BL], start=True, stop=True)
                        M("att", i)
                        M("ups", mm(b3[:, :], b["TX"][:, 512:640], b["XW"], start=True, stop=True))
                    for d in (0, 1):
                        b, M = sc[d], marks[d]
                        b0, b1, b2, b3 = ps[4 * d:4 * d + 4]
                        pe.wait_ge(s_dve[d].sem, s_dve[d].at(it, "wm"))
                        va = b["TK"][:, 256:256 + VA]
                        for h in range(MH):
                            mm(b1[:, h * 65:h * 65 + 65], b["ME"][:, h * P:(h + 1) * P], va[:, h * 65:h * 65 + 65],
                               start=True, stop=True)
                        for j in (0, 1):
                            i = mm(b2[:, 130 * j:130 * j + 130], b["FT"][:, (2 + j) * P:(3 + j) * P],
                                   b["ST"][:, S_ML + 130 * j:S_ML + 130 * j + 130], start=True, stop=True)
                        M("mli", i)
                        pe.wait_ge(s_dve[d].sem, s_dve[d].at(it, "t1"))
                        mm(b0[:, 0:256], b["QH"], b["ST"][:, S_GLA:S_W], start=True, stop=False)
                        for h in range(GH):
                            mm(b0[:, h * HD:(h + 1) * HD], b["AT"][:, h * P:(h + 1) * P], b["TK"][:, h * HD:(h + 1) * HD],
                               start=False, stop=(h == GH - 1))
                        M("upg", mm(b0[:, 256:512], b["KMD"][:, 2 * P:3 * P], b["TK"][:, 0:256], start=True, stop=True))
                        pe.wait_ge(s_pool[d].sem, s_pool[d].at(it, "vw"))
                        for j in (0, 1):
                            i = mm(b3[:, 130 * j:130 * j + 130], b["KMD"][:, j * P:(j + 1) * P],
                                   b["VW"][:, 130 * j:130 * j + 130], start=True, stop=True)
                        M("upm", i)
                meet(pe, l * PHASES + 3)

                pe.wait_ge(e_w, (l + 1) * 32)
                pe.wait_ge(e_par, (l + 1) * 144)

                def mix(t):
                    mark = marker(o_pe)
                    pe.wait_ge(o_dve.sem, o_dve.at(t, "yn2"))
                    pe.wait_ge(q_act.sem, q_act.at(t, "sc3", 1))
                    mark("yt0", turn(ps[0], YF, 0))
                    mark("yt1", turn(ps[1], YF, 4))
                    yield
                    pe.wait_ge(o_dve.sem, o_dve.at(t, "yt0"))
                    pe.wait_ge(o_act.sem, o_act.at(t, "yt1"))
                    for h in (0, 1):
                        for k in range(KC):
                            i = mm(ps[2 + h][:, :], YT[:, k * P:(k + 1) * P], wo[:, k, 512 * h:512 * h + 512],
                                   start=(k == 0), stop=(k == KC - 1))
                            if k % 2 and (h, k) != (1, KC - 1):
                                yield
                    mark("out", i)
                    yield

                def scores(t):
                    mark = marker(q_pe)
                    pe.wait_ge(o_dve.sem, o_dve.at(t, "u2c"))
                    mark("ut0", turn(ps[0], SC2, 0))
                    mark("ut1", turn(ps[1], SC2, 4))
                    yield
                    pe.wait_ge(q_dve.sem, q_dve.at(t, "ut0"))
                    pe.wait_ge(q_act.sem, q_act.at(t, "ut1"))
                    for h in range(HEADS):
                        for k in range(KC):
                            i = mm(ps[2 + h // 4][:, h % 4 * P:(h % 4 + 1) * P], wq[:, k, h * P:(h + 1) * P],
                                   U2T[:, k * P:(k + 1) * P], start=(k == 0), stop=(k == KC - 1))
                        mark(f"q{h}", i)
                        yield
                    pe.wait_ge(q_dve.sem, q_dve.at(t, "qt0"))
                    pe.wait_ge(q_act.sem, q_act.at(t, "qt1"))
                    for b in range(4):
                        for h in (2 * b, 2 * b + 1):
                            i = mm(ps[b][:, 256 * (h % 2):256 * (h % 2) + 256], QT[:, h * P:(h + 1) * P], KEYS,
                                   start=True, stop=True)
                        mark(f"s{b}", i)

                def whole_round(t):
                    yield from mix(t)
                    yield from scores(t)

                for _ in whole_round(l * ROUNDS):
                    pass
                pe.sem_inc(passed, 1)
                with pe.Fori(0, TILES) as s:
                    it = l * TILES + s
                    mark = marker(e_pe)
                    beside = whole_round(l * ROUNDS + 1 + s)
                    pe.wait_ge(e_dve.sem, e_dve.at(it, "r01", 1))
                    for n in range(SLOTS):
                        pe.wait_ge(e_act.sem, e_act.at(it, f"dg{n}"))
                        for h in (0, 1):
                            i = mm(ps[4 + h][:, :], DG[:, n % DIAGS * P:(n % DIAGS + 1) * P],
                                   ring[:, n % RING, D + 512 * h:D + 512 * h + 512], start=(n == 0), stop=(n == SLOTS - 1))
                        mark(f"v{n}", i)
                        if n in PE_STEPS:
                            next(beside, None)
                meet(pe, l * PHASES + 4)

        @block.gpsimd
        def _(ge):
            give_credit(ge, pool_own)
            g_ = nc.gpsimd

            meet(ge, 0)
            ge.sem_inc(passed, 1)
            with ge.Fori(0, DEPTH) as l:
                meet(ge, l * PHASES + 1)
                meet(ge, l * PHASES + 2)
                for d in (0, 1):
                    for t in ("CTP", "QMP", "QP"):
                        g_.memset(sc[d][t], 0.0).then_inc(s_pad, 1)
                apart(ge, s_pad, (l + 1) * 6)
                ge.sem_inc(passed, 1)
                with ge.Fori(0, TILES) as s:
                    it = l * TILES + s
                    links = [linker(ge, s_pool[d], it, alone=True) for d in (0, 1)]
                    for d in (0, 1):
                        b, L = sc[d], links[d]
                        ge.wait_ge(s_ld[d].sem, s_ld[d].at(it, "ld"))
                        ge.wait_ge(s_ls[d].sem, s_ls[d].at(it, "ls"))
                        apart(ge, s_pe[d].sem, s_pe[d].at(it, "upm", 1))
                        for g in (0, 1):
                            r = slice(HD * g, HD * g + HD)
                            L(f"ct{g}", g_.tensor_copy(b["CTP"][r, g * P:(g + 1) * P], b["FX"][r, P:2 * P]))
                            L(f"qm{g}", g_.tensor_copy(
                                b["QMP"][r, :].rearrange("p (j h s) -> p j h s", j=2, h=2)[:, :, g, :],
                                b["FT"][r, 2 * P:4 * P].rearrange("p (j s) -> p j s", j=2)))
                        L("xd", g_.tensor_tensor(grp(b["XD"], a=SH), grp(b["TX"][:, 0:512], a=SH),
                                                 b["TK"][:, 256 + VA + NDIR + 4:256 + VA + DB].unsqueeze(2)
                                                 .broadcast_to([P, SH, HD]), ALU.mult))
                    for d in (0, 1):
                        b, L = sc[d], links[d]
                        apart(ge, s_act[d].sem, s_act[d].at(it, "em"))
                        L("vw", g_.tensor_tensor(grp(b["VW"], a=MH), grp(b["TK"][:, 256:256 + VA], a=MH),
                                                 b["EM"][:, 8:12].unsqueeze(2).broadcast_to([P, MH, HD + 1]), ALU.mult))
                        apart(ge, s_st[d].sem, s_st[d].at(it, "st", 1))
                        sn, st = b["SN"], b["ST"]
                        L("sns", g_.tensor_tensor(grp(sn[:, 0:512], a=SH), grp(st[:, 0:512], a=SH),
                                                  b["EA"][:, 12:20].unsqueeze(2).broadcast_to([P, SH, HD]), ALU.mult))
                        L("snm", g_.tensor_tensor(grp(sn[:, S_ML:S_GLA], a=MH), grp(st[:, S_ML:S_GLA], a=MH),
                                                  b["EM"][:, 12:16].unsqueeze(2).broadcast_to([P, MH, HD + 1]), ALU.mult))
                    for d in (0, 1):
                        b, L = sc[d], links[d]
                        sn = b["SN"]
                        apart(ge, s_dve[d].sem, s_dve[d].at(it, "last"))
                        L("sna1", g_.tensor_tensor(sn[:, 0:512], sn[:, 0:512], b["T1"], ALU.add))
                        L("sna", g_.tensor_tensor(sn[:, S_ML:S_GLA], sn[:, S_ML:S_GLA], b["T2"], ALU.add))
                meet(ge, l * PHASES + 3)
                with ge.Fori(0, TILES) as s:
                    it = l * TILES + s
                    link = linker(ge, e_pool, it, alone=True)
                    half = SLOTS // 2
                    for u in (0, 1):
                        c = slice(u * half, (u + 1) * half)
                        if u == 0:
                            apart(ge, q_dve.sem, q_dve.at(l * ROUNDS + s, "smd"))
                        apart(ge, e_dve.sem, e_dve.at(it, f"dot{(u + 1) * half - 1}", 1))
                        link(f"ix{u}", g_.tensor_copy(IDXC.bitcast(U32)[:, c], IDXN.bitcast(U32)[:, c]))
                        for n in range(u * half, (u + 1) * half):
                            if n < RING:
                                apart(ge, e_pe.sem, e_pe.at(it, f"v{n + SLOTS - RING}", 1))
                            else:
                                apart(ge, e_pe.sem, e_pe.at(it, f"v{n - RING}"))
                            g_.indirect_dma_start(ring[:, n % RING, :], None, io["experts"],
                                                  bass.IndirectOffsetOnAxis(ap=IDXC.bitcast(U32)[:, n:n + 1], axis=0)
                                                  ).then_inc(e_gat[n % RING].sem, 16)
                meet(ge, l * PHASES + 4)


W_IN_PARTS = (((O_GQ, O_GV), (O_MQ, O_MV)), ((O_MI, O_SZ), (O_SB, IN_W), (O_GG, O_MQ)),
              ((O_GV, O_GG), (O_MV, O_MI)), ((O_SZ, O_SB),))

SHAPES = {
    "ident": [P, P], "x_in": [NPOS, P, D], "pos_in": [NPOS, P, D], "c2t": [P, 2 * KC],
    "w_ada": [DEPTH, D, 6 * D], "b_ada": [DEPTH, 6 * D], "w_in": [DEPTH, D, IN_W],
    "gbias": [DEPTH, 2 * NDIR], "mlstm_bi": [DEPTH, 8], "ssd_a_log": [DEPTH, 16], "wa2": [DEPTH, 32, 256],
    "sgn": [2 * NDIR], "coef": [2 * NDIR], "conv_w": [DEPTH, P, 18], "conv_b": [DEPTH, P, 6],
    "tri": [2, P, P], "perm": [2, P, P], "gmask": [P, S_W], "w_out": [DEPTH, D, D], "peer_wq": [DEPTH, D, D],
    "keys": [DEPTH, P, 256], "gnorm_w": [DEPTH, D], "ln1_w": [DEPTH, D], "ln1_b": [DEPTH, D],
    "ln2_w": [DEPTH, D], "ln2_b": [DEPTH, D], "ssd_d": [DEPTH, SH], "iota": [TOPK], "lofs": [DEPTH, 1],
    "state0": [DEPTH, 2, 2, P, S_W], "m0": [DEPTH, 2, 2, MH], "zeros": [P, 6, P], "experts": [DEPTH * NE, 2 * D],
}


def program(nc, scratch="Internal"):
    io = {k: nc.dram_tensor("in_" + k, s, F32, kind="ExternalInput").ap() for k, s in SHAPES.items()}
    for k, s in (("xres", [NPOS, P, D]), ("state", [DEPTH, 2, 7, P, S_W]), ("mstate", [DEPTH, 2, 7, MH])):
        io[k] = nc.dram_tensor(k, s, F32, kind="ExternalOutput").ap()
    io["scratch"] = lambda name, shape, dt: nc.dram_tensor(name, shape, dt, kind=scratch).ap()
    build(nc, io)


def pos_rows():
    n = DEC_TILES * P
    f = np.float32
    r = np.repeat(np.arange(n // GRID_W, dtype=f), GRID_W)
    c = np.tile(np.arange(GRID_W, dtype=f), n // GRID_W)
    q = D // 4
    inv = f(1) / np.power(f(POS_BASE), np.arange(q, dtype=f) / f(q)).astype(f)
    ar, ac = r[:, None] * inv, c[:, None] * inv
    t = np.concatenate([np.sin(ar), np.cos(ar), np.sin(ac), np.cos(ac)], axis=-1).astype(f)
    out = np.zeros((NPOS, P, D), f)
    out[2:] = t.reshape(DEC_TILES, P, D)
    return out


def lay_out(i):
    f = np.float32
    a = {k: np.asarray(v) for k, v in i.items()}
    L = DEPTH
    x = np.zeros((NPOS, P, D), f)
    x[0] = a["x_prompt"][0]
    x[2:] = a["x_sample"][0].reshape(DEC_TILES, P, D)
    c2 = np.stack([a["c_ctx"], a["c"][0]])
    gb = np.concatenate([a["gla_ba"], a["mlstm_bf"], a["ssd_dt_bias"]], axis=2).reshape(L, 2 * NDIR)
    wa2 = np.zeros((L, 32, 256), f)
    keys = np.zeros((L, P, 256), f)
    for d in (0, 1):
        wa2[:, RANK * d:RANK * d + RANK, P * d:P * d + P] = a["gla_wa2"][:, d]
        keys[:, 64 * d:64 * d + 64, P * d:P * d + P] = a["peer_keys"][:, d].transpose(0, 2, 1)
    sgn = np.tile(np.concatenate([-np.ones(132, f), np.ones(8, f)]), 2)
    coef = np.tile(np.concatenate([np.full(128, -1.0 / 16.0, f), -np.ones(4, f), np.zeros(8, f)]), 2)
    up = np.triu(np.ones((P, P), f))
    eye = np.eye(P, dtype=f)
    st = np.zeros((L, 2, 2, P, S_W), f)
    mask = np.zeros((P, S_W), f)
    for h in range(SH):
        g = h // 4
        st[:, :, 1, HD * g:HD * g + HD, h * HD:(h + 1) * HD] = a["state_ssd"][0, :, :, h].transpose(0, 1, 3, 2)
        mask[HD * g:HD * g + HD, h * HD:(h + 1) * HD] = 1
    for h in range(MH):
        r, c = slice(HD * (h % 2), HD * (h % 2) + HD), S_ML + 65 * h
        st[:, :, 1, r, c:c + HD] = a["state_mlstm_c"][0, :, :, h].transpose(0, 1, 3, 2)
        st[:, :, 1, r, c + HD] = a["state_mlstm_n"][0, :, :, h]
        mask[r, c:c + 65] = 1
        r, c = slice(GDK * h, GDK * h + GDK), S_GLA + HD * h
        st[:, :, 1, r, c:c + HD] = a["state_gla"][0, :, :, h]
        mask[r, c:c + HD] = 1
    m0 = np.zeros((L, 2, 2, MH), f)
    m0[:, :, 1] = a["state_mlstm_m"][0]
    return {
        "ident": eye, "x_in": x, "pos_in": pos_rows(),
        "c2t": c2.reshape(2, KC, P).transpose(2, 1, 0).reshape(P, 2 * KC),
        "w_ada": a["w_ada"], "b_ada": a["b_ada"], "w_in": a["w_in"], "gbias": gb,
        "mlstm_bi": a["mlstm_bi"].reshape(L, 8), "ssd_a_log": a["ssd_a_log"].reshape(L, 16), "wa2": wa2,
        "sgn": sgn, "coef": coef,
        "conv_w": a["conv_w"].reshape(L, 3, 6, P).transpose(0, 3, 2, 1).reshape(L, P, 18),
        "conv_b": a["conv_b"].reshape(L, 6, P).transpose(0, 2, 1),
        "tri": np.stack([up, up.T]), "perm": np.stack([eye, eye[::-1]]), "gmask": mask,
        "w_out": a["w_out"], "peer_wq": a["peer_wq"], "keys": keys, "gnorm_w": a["gnorm_w"],
        "ln1_w": a["ln1_w"], "ln1_b": a["ln1_b"], "ln2_w": a["ln2_w"], "ln2_b": a["ln2_b"], "ssd_d": a["ssd_d"],
        "iota": np.arange(TOPK, dtype=f), "lofs": np.arange(L, dtype=f)[:, None] * f(NE),
        "state0": st, "m0": m0, "zeros": np.zeros((P, 6, P), f),
        "experts": np.concatenate([a["peer_u"], a["peer_v"]], axis=2).reshape(L * NE, 2 * D),
    }


def kernel(**inputs):
    import concourse.bacc as bacc
    from concourse.bass_utils import run_bass_kernel_spmd as run

    nc = bacc.Bacc("TRN2", target_bir_lowering=False, num_devices=1)
    program(nc)
    data = {"in_" + k: np.ascontiguousarray(v) for k, v in lay_out(inputs).items()}
    r = run(nc, [data], core_ids=[0]).results[0]
    x, m = r["xres"], r["mstate"]
    st = np.stack([r["state"][:, 0, 1], r["state"][:, 1, 0]], axis=1)
    gla = np.stack([st[:, :, GDK * h:GDK * h + GDK, S_GLA + HD * h:S_GLA + HD * h + HD] for h in range(GH)], axis=2)
    mc = np.stack([st[:, :, HD * (h % 2):HD * (h % 2) + HD, S_ML + 65 * h:S_ML + 65 * h + HD] for h in range(MH)], axis=2)
    mn = np.stack([st[:, :, HD * (h % 2):HD * (h % 2) + HD, S_ML + 65 * h + HD] for h in range(MH)], axis=2)
    ssd = np.stack([st[:, :, HD * (h // 4):HD * (h // 4) + HD, h * HD:h * HD + HD] for h in range(SH)], axis=2)
    mm = np.stack([m[:, 0, 1], m[:, 1, 0]], axis=1)
    return (x[0:1], x[2:].reshape(1, DEC_TILES * P, D), gla[None], mc.transpose(0, 1, 2, 4, 3)[None], mn[None],
            mm[None], ssd.transpose(0, 1, 2, 4, 3)[None])
```

```python
import math
from contextlib import ExitStack

import numpy as np

import concourse.bass as bass
from concourse import mybir

F32 = mybir.dt.float32
U32 = mybir.dt.uint32
ALU = mybir.AluOpType
ACT = mybir.ActivationFunctionType
AX = mybir.AxisListType.X

P = 128
D = 1024
KC = D // P
DEPTH = 2
TILES = 5
NPOS = 6
SEQ_TILES = 1
DEC_TILES = 4
GRID_W = 64
POS_BASE = 10000.0
HD = 64
GH, MH, SH = 4, 4, 8
GDK = 32
RANK = 16
IN_W = 3136
O_GQ, O_GK, O_GV, O_GG, O_GA = 0, 128, 256, 512, 768
O_MQ, O_MK, O_MV, O_MO, O_MI = 800, 1056, 1312, 1568, 1824
O_SX, O_SZ, O_SB, O_SDT = 1840, 2352, 2864, 3120
NDIR = 140
DB = NDIR + 4 + 8
VA = MH * (HD + 1)
TOK_W = 256 + VA + 2 * DB
S_SSD, S_ML, S_GLA, S_W = 0, 512, 512 + VA, 512 + VA + 256
NE = 16384
HEADS = 8
TOPK = 16
SLOTS = HEADS * TOPK
ALPHA = (2 * DEPTH) ** 0.25
EPS = 1e-6
BL = 16
NB = P // BL
CLAMP = 40.0
E_CLAMP = float(np.exp(np.float32(CLAMP)))
PHASES = 4
DVE_STEPS = {4: 2, 5: 2, 6: 2, 7: 1, 11: 2, 12: 1, 18: 1, 32: 2, 33: 2, 34: 2, 38: 2, 39: 2, 40: 2, 41: 1,
             45: 2, 46: 2, 49: 1, 58: 1}
TOP_FIRST, SUM_FIRST = 66, 120
ACT_STEPS = {8: 1, 16: 1, 34: 1, 42: 1, 48: 1, 62: 1, 66: 1, 116: 1}
PE_STEPS = (13, *range(19, 27), 44, *range(50, 58), 58)
ROUNDS = TILES + 1
RING = 8
DIAGS = 4
GRP = 2


EVENTS = {
    "m_pe": ["mod0", "mod1", "mod2", "mod3"],
    "m_dve": ["mod0", "mod1", "mod2", "mod3"],
    "i_dve": ["add0", "add1"],
    "n_dve": ["st0", "st1", "mv", "rs", "xn", "xs", "xsh"],
    "n_act": ["sd"],
    "n_pe": ["tr0", "tr1"],
    "p_dve": ["ut0", "ut1", "gat", "c4", "z0", "z1", "z2", "ig", "zs", "za", "vg", "vm", "sp", "la", "dt"],
    "p_act": ["a1", "a2", "b1", "b2", "ze", "ln", "silug", "siluz", "sigmo"],
    "p_pe": ["A", "B", "C", "D", "E1", "E", "gate", "last"],
    "pl_dve": ["coef", "vone"],
    "pl_act": ["ea"],
    "c_dve": [
        "a0", "b0", "c0", "a1", "b1", "c1", "a2", "b2", "c2", "a3", "b3", "c3", "a4", "b4", "c4", "a5",
        "b5", "c5",
    ],
    "c_act": [
        "silu0", "silu1", "four0", "alone0", "silu2", "four1", "alone1", "silu3", "four2", "alone2",
        "silu4", "four3", "alone3", "silu5", "four4", "alone4",
    ],
    "c_pe": ["t0", "t1", "t2", "t3", "t4"],
    "s_dve0": [
        "cs", "f4", "dec", "g4", "ng", "cbm", "g4r", "r4", "mn", "kta", "qba", "gg8", "qh", "kdm",
        "qp0", "qp1", "qp2", "qp3", "ktm", "gt", "em0", "em1", "em2", "em3", "w8", "qkm", "wm", "ys0",
        "ys1", "at", "t1", "hm0", "hm1", "dn0", "dn1", "rc", "ym", "t2", "t3", "sng",
    ],
    "s_dve1": [
        "cs", "f4", "dec", "g4", "ng", "cbm", "g4r", "r4", "mn", "kta", "qba", "gg8", "qh", "kdm",
        "qp0", "qp1", "qp2", "qp3", "ktm", "gt", "em0", "em1", "em2", "em3", "w8", "qkm", "wm", "ys0",
        "ys1", "at", "t1", "hm0", "hm1", "dn0", "dn1", "rc", "ym", "t2", "t3", "sng",
    ],
    "s_act0": [
        "ea", "eb", "kd", "rx4", "rx5", "rx6", "rx7", "ex1", "rx0", "rx1", "rx2", "rx3", "ex0", "kt",
        "qb", "kmd", "em", "me0", "me1", "me2", "me3", "me", "yg",
    ],
    "s_act1": [
        "ea", "eb", "kd", "rx4", "rx5", "rx6", "rx7", "ex1", "kt", "qb", "rx0", "rx1", "rx2", "rx3",
        "ex0", "kmd", "em", "me0", "me1", "me2", "me3", "me", "yg",
    ],
    "s_pe0": ["sum", "cum", "g4r", "km", "qk", "kdt", "gb", "ssd", "att", "ups", "mli", "upg", "upm"],
    "s_pe1": ["sum", "cum", "g4r", "km", "qk", "kdt", "gb", "ssd", "att", "ups", "mli", "upg", "upm"],
    "s_pool0": ["xd", "xw", "sns", "vw", "snm", "sna1", "sna"],
    "s_pool1": ["xd", "xw", "sns", "vw", "snm", "sna1", "sna"],
    "o_dve": [
        "y0", "y1", "y2", "y3", "sq", "hr", "hrm", "hrr", "yn1", "yn2", "yt0", "g0", "g1", "r1", "st0a",
        "st1a", "mva", "rsa", "x1a", "x1b", "x1c", "st0b", "st1b", "mvb", "rsb", "u2a", "u2b", "u2c",
    ],
    "o_act": ["hsd", "yt1", "sda", "sdb"],
    "o_pe": ["yt0", "yt1", "out"],
    "q_dve": [
        "ut0", "qt0", "half0.0.0", "half0.0.1", "half0.0.2", "half0.0.3", "half0.1.0", "half0.1.1",
        "half0.1.2", "half0.1.3", "half0.2.0", "half0.2.1", "half0.2.2", "half0.2.3", "half0.3.0",
        "half0.3.1", "half0.3.2", "half0.3.3", "half0.4.0", "half0.4.1", "half0.4.2", "half0.4.3",
        "half1.0.0", "half1.0.1", "half1.0.2", "half1.0.3", "half1.1.0", "half1.1.1", "half1.1.2",
        "half1.1.3", "half1.2.0", "half1.2.1", "half1.2.2", "half1.2.3", "half1.3.0", "half1.3.1",
        "half1.3.2", "half1.3.3", "half1.4.0", "half1.4.1", "half1.4.2", "half1.4.3", "half2.0.0",
        "half2.0.1", "half2.0.2", "half2.0.3", "half2.1.0", "half2.1.1", "half2.1.2", "half2.1.3",
        "half2.2.0", "half2.2.1", "half2.2.2", "half2.2.3", "half2.3.0", "half2.3.1", "half2.3.2",
        "half2.3.3", "half2.4.0", "half2.4.1", "half2.4.2", "half2.4.3", "half3.0.0", "half3.0.1",
        "half3.0.2", "half3.0.3", "half3.1.0", "half3.1.1", "half3.1.2", "half3.1.3", "half3.2.0",
        "half3.2.1", "half3.2.2", "half3.2.3", "half3.3.0", "half3.3.1", "half3.3.2", "half3.3.3",
        "half3.4.0", "half3.4.1", "half3.4.2", "half3.4.3", "tf", "can", "pair0.0.0", "pair0.0.1",
        "pair0.0.2", "pair0.0.3", "pair0.1.0", "pair0.1.1", "pair0.1.2", "pair0.1.3", "pair0.2.0",
        "pair0.2.1", "pair0.2.2", "pair0.2.3", "pair0.3.0", "pair0.3.1", "pair0.3.2", "pair0.3.3",
        "pair0.4.0", "pair0.4.1", "pair0.4.2", "pair0.4.3", "pair1.0.0", "pair1.0.1", "pair1.0.2",
        "pair1.0.3", "pair1.1.0", "pair1.1.1", "pair1.1.2", "pair1.1.3", "pair1.2.0", "pair1.2.1",
        "pair1.2.2", "pair1.2.3", "pair1.3.0", "pair1.3.1", "pair1.3.2", "pair1.3.3", "pair1.4.0",
        "pair1.4.1", "pair1.4.2", "pair1.4.3", "ba0", "bf0", "oh0", "oi0", "oj0", "ba1", "bf1", "oh1",
        "oi1", "oj1", "ixa", "ixb", "sma", "smb", "smc", "smd",
    ],
    "q_act": ["ut1", "sc0", "sc1", "qt1", "sc2", "sc3", "sme"],
    "q_pe": ["ut0", "ut1", "q0", "q1", "q2", "q3", "q4", "q5", "s0", "s1", "q6", "q7", "s2", "s3"],
    "e_pool": ["ix0", "ix1"],
    "e_dve": [
        "gwc", "eu", "dot0", "dot1", "dot2", "dot3", "aw0", "dot4", "dot5", "aw1", "dot6", "dot7",
        "aw2", "dot8", "dot9", "aw3", "dot10", "dot11", "aw4", "dot12", "dot13", "aw5", "dot14",
        "dot15", "aw6", "dot16", "dot17", "aw7", "dot18", "dot19", "aw8", "dot20", "dot21", "aw9",
        "dot22", "dot23", "aw10", "dot24", "dot25", "aw11", "dot26", "dot27", "aw12", "dot28", "dot29",
        "aw13", "dot30", "dot31", "aw14", "dot32", "dot33", "aw15", "dot34", "dot35", "aw16", "dot36",
        "dot37", "aw17", "dot38", "dot39", "aw18", "dot40", "dot41", "aw19", "dot42", "dot43", "aw20",
        "dot44", "dot45", "aw21", "dot46", "dot47", "aw22", "dot48", "dot49", "aw23", "dot50", "dot51",
        "aw24", "dot52", "dot53", "aw25", "dot54", "dot55", "aw26", "dot56", "dot57", "aw27", "dot58",
        "dot59", "aw28", "dot60", "dot61", "aw29", "dot62", "dot63", "aw30", "dot64", "dot65", "aw31",
        "dot66", "dot67", "aw32", "dot68", "dot69", "aw33", "dot70", "dot71", "aw34", "dot72", "dot73",
        "aw35", "dot74", "dot75", "aw36", "dot76", "dot77", "aw37", "dot78", "dot79", "aw38", "dot80",
        "dot81", "aw39", "dot82", "dot83", "aw40", "dot84", "dot85", "aw41", "dot86", "dot87", "aw42",
        "dot88", "dot89", "aw43", "dot90", "dot91", "aw44", "dot92", "dot93", "aw45", "dot94", "dot95",
        "aw46", "dot96", "dot97", "aw47", "dot98", "dot99", "aw48", "dot100", "dot101", "aw49",
        "dot102", "dot103", "aw50", "dot104", "dot105", "aw51", "dot106", "dot107", "aw52", "dot108",
        "dot109", "aw53", "dot110", "dot111", "aw54", "dot112", "dot113", "aw55", "dot114", "dot115",
        "aw56", "dot116", "dot117", "aw57", "dot118", "dot119", "aw58", "dot120", "dot121", "aw59",
        "dot122", "dot123", "aw60", "dot124", "dot125", "aw61", "dot126", "dot127", "aw62", "aw63",
        "r00", "r01", "r1", "st0", "st1", "mv", "r2", "xa", "xw", "xb",
    ],
    "e_act": [
        "ge0", "ex", "ge1", "dg0", "dg1", "ge2", "dg2", "dg3", "ge3", "dg4", "dg5", "ge4", "dg6", "dg7",
        "ge5", "dg8", "dg9", "ge6", "dg10", "dg11", "ge7", "dg12", "dg13", "ge8", "dg14", "dg15", "ge9",
        "dg16", "dg17", "ge10", "dg18", "dg19", "ge11", "dg20", "dg21", "ge12", "dg22", "dg23", "ge13",
        "dg24", "dg25", "ge14", "dg26", "dg27", "ge15", "dg28", "dg29", "ge16", "dg30", "dg31", "ge17",
        "dg32", "dg33", "ge18", "dg34", "dg35", "ge19", "dg36", "dg37", "ge20", "dg38", "dg39", "ge21",
        "dg40", "dg41", "ge22", "dg42", "dg43", "ge23", "dg44", "dg45", "ge24", "dg46", "dg47", "ge25",
        "dg48", "dg49", "ge26", "dg50", "dg51", "ge27", "dg52", "dg53", "ge28", "dg54", "dg55", "ge29",
        "dg56", "dg57", "ge30", "dg58", "dg59", "ge31", "dg60", "dg61", "ge32", "dg62", "dg63", "ge33",
        "dg64", "dg65", "ge34", "dg66", "dg67", "ge35", "dg68", "dg69", "ge36", "dg70", "dg71", "ge37",
        "dg72", "dg73", "ge38", "dg74", "dg75", "ge39", "dg76", "dg77", "ge40", "dg78", "dg79", "ge41",
        "dg80", "dg81", "ge42", "dg82", "dg83", "ge43", "dg84", "dg85", "ge44", "dg86", "dg87", "ge45",
        "dg88", "dg89", "ge46", "dg90", "dg91", "ge47", "dg92", "dg93", "ge48", "dg94", "dg95", "ge49",
        "dg96", "dg97", "ge50", "dg98", "dg99", "ge51", "dg100", "dg101", "ge52", "dg102", "dg103",
        "ge53", "dg104", "dg105", "ge54", "dg106", "dg107", "ge55", "dg108", "dg109", "ge56", "dg110",
        "dg111", "ge57", "dg112", "dg113", "ge58", "dg114", "dg115", "ge59", "dg116", "dg117", "ge60",
        "dg118", "dg119", "ge61", "dg120", "dg121", "ge62", "dg122", "dg123", "ge63", "dg124", "dg125",
        "dg126", "dg127", "sd",
    ],
    "e_pe": [
        "v0", "v1", "v2", "v3", "v4", "v5", "v6", "v7", "v8", "v9", "v10", "v11", "v12", "v13", "v14",
        "v15", "v16", "v17", "v18", "v19", "v20", "v21", "v22", "v23", "v24", "v25", "v26", "v27",
        "v28", "v29", "v30", "v31", "v32", "v33", "v34", "v35", "v36", "v37", "v38", "v39", "v40",
        "v41", "v42", "v43", "v44", "v45", "v46", "v47", "v48", "v49", "v50", "v51", "v52", "v53",
        "v54", "v55", "v56", "v57", "v58", "v59", "v60", "v61", "v62", "v63", "v64", "v65", "v66",
        "v67", "v68", "v69", "v70", "v71", "v72", "v73", "v74", "v75", "v76", "v77", "v78", "v79",
        "v80", "v81", "v82", "v83", "v84", "v85", "v86", "v87", "v88", "v89", "v90", "v91", "v92",
        "v93", "v94", "v95", "v96", "v97", "v98", "v99", "v100", "v101", "v102", "v103", "v104", "v105",
        "v106", "v107", "v108", "v109", "v110", "v111", "v112", "v113", "v114", "v115", "v116", "v117",
        "v118", "v119", "v120", "v121", "v122", "v123", "v124", "v125", "v126", "v127",
    ],
}


class Steps:

    def __init__(self, sem, names, unit=1, ahead=1):
        self.sem, self.names, self.unit, self.ahead, self.seen = sem, names, unit, ahead, 0

    def take(self, name):
        assert self.names[self.seen % len(self.names)] == name, (name, self.names, self.seen)
        self.seen += 1

    @property
    def round(self):
        return len(self.names) * self.unit

    def at(self, it, name, back=0):
        i = self.names.index(name)
        return it * self.round + ((self.ahead - back) * self.round + (i + 1) * self.unit)


def build(nc, io):
    x_in, pos_in, c2t, w_ada, b_ada = io["x_in"], io["pos_in"], io["c2t"], io["w_ada"], io["b_ada"]
    xres, state, mstate = io["xres"], io["state"], io["mstate"]

    ctx = ExitStack()
    with ctx:
        def sem(name):
            return ctx.enter_context(nc.semaphore(name))


        def dram(name, shape, dt=F32):
            return io["scratch"](name, shape, dt)

        modd = dram("modd", [DEPTH, 2, 6 * D])
        tok_d = dram("tok_d", [NPOS, P, TOK_W])
        feat_d = dram("feat_d", [NPOS, P, 6 * P])
        gate_d = dram("gate_d", [NPOS, P, D])
        conv_d = dram("conv_d", [P, 6, NPOS * P + 2])
        ctok_d = dram("ctok_d", [NPOS, P, 640])
        cfeat_d = dram("cfeat_d", [NPOS, P, 2 * P])
        y_d = dram("y_d", [2, NPOS, P, D])

        big = ctx.enter_context(nc.sbuf_tensor("big", [P, 53200], F32))
        ps = [ctx.enter_context(nc.psum_tensor(f"bank{b}", [P, 512], F32)) for b in range(8)]

        class Area:
            def __init__(self, base):
                self.top = base

            def __call__(self, cols, parts=P):
                a = self.top
                self.top += cols
                assert self.top <= 53200, self.top
                return big[0:parts, a:a + cols]

        keep = Area(0)
        ident = keep(P)
        ones = keep(P)
        eps = keep(1)
        TRI, PERM = [keep(P) for _ in (0, 1)], [keep(P) for _ in (0, 1)]
        base = keep.top

        met = sem("met")
        credit = sem("credit")
        passed = sem("passed")
        start_ld = sem("start_ld")
        sem_ones = sem("sem_ones")
        sem_tri = sem("sem_tri")
        sem_silu = sem("sem_silu")
        fill_st, fill_cv = sem("fill_st"), sem("fill_cv")

        def apart(eng, s, value):
            eng.wait_ge(s, value)
            eng.sem_inc(passed, 1)

        def meet(eng, n):
            eng.sem_inc(passed, 1)
            eng.drain().then_inc(met, 1)
            apart(eng, met, n * 5 + 5)

        def linker(eng, s, it, alone=False):
            s.seen = 0

            def link(name, ins, hold=True):
                s.take(name)
                ins.then_inc(s.sem, 1)
                if not hold:
                    return
                eng.wait_ge(s.sem, s.at(it, name))
                if alone:
                    eng.sem_inc(passed, 1)
            return link

        def marker(s):
            s.seen = 0

            def mark(name, ins):
                s.take(name)
                ins.then_inc(s.sem, 1)
            return mark

        def pos(s):
            return nc.s_assert_within(s + ((s + 3) >> 2), 0, NPOS - 1,
                                      skip_runtime_bounds_check_because="s is 0..4: 0, 2, 3, 4, 5")

        def bwd_pos(s):
            return nc.s_assert_within(((s + 3) >> 2) * 6 - s, 0, NPOS - 1,
                                      skip_runtime_bounds_check_because="s is 0..4: 0, 5, 4, 3, 2")

        def next_pos(s):
            return nc.s_assert_within((s & 3) + 2, 0, NPOS - 1,
                                      skip_runtime_bounds_check_because="s is 0..4: 2, 3, 4, 5, 2")

        def second_pos(s):
            return nc.s_assert_within((s & 3) - ((s + 1) >> 2) + 3, 0, NPOS - 1,
                                      skip_runtime_bounds_check_because="s is 0..4: 3, 4, 5, 5, 2")

        def next_bwd_pos(s):
            return nc.s_assert_within((s & 3) * -1 + 5, 0, NPOS - 1,
                                      skip_runtime_bounds_check_because="s is 0..4: 5, 4, 3, 2, 5")

        def group(s):
            return nc.s_assert_within((s + 3) >> 2, 0, 1,
                                      skip_runtime_bounds_check_because="s is 0..4: 0, 1, 1, 1, 1")

        def at1(t, i):
            v = t[bass.ds(i, 1)]
            return v.rearrange("a " + " ".join("bcde"[:len(v.shape) - 1]) + " -> (a b) "
                               + " ".join("cde"[:len(v.shape) - 2]))

        def grp(ap, **k):
            return ap.rearrange("p (a b) -> p a b", **k)

        def rows(ap):
            return ap.partition_broadcast(P)

        sp_own, act_own, pe_own, dve_own, pool_own = [], [], [], [], []

        def mk(owner, name, unit=1, events=None, ahead=1):
            s = Steps(sem(name), EVENTS[name] if events is None else events, unit, ahead)
            if ahead:
                owner.append(s)
            return s

        m_w = [mk(sp_own, f"m_w{u}", 32, ["w"]) for u in range(4)]
        m_pe, m_dve = mk(pe_own, "m_pe"), mk(dve_own, "m_dve")
        m_out = [mk(act_own, f"m_out{u}", 16, ["out"]) for u in range(4)]
        i_ld, i_dve, i_st = mk(sp_own, "i_ld", 64, ["ld"]), mk(dve_own, "i_dve"), mk(sp_own, "i_st", 32, ["st"])
        p_w, p_par = [sem(f"p_w{q}") for q in range(4)], sem("p_par")
        n_dve, n_act, n_pe = mk(dve_own, "n_dve"), mk(act_own, "n_act"), mk(pe_own, "n_pe")
        p_x, p_mod = mk(sp_own, "p_x", 16, ["x"]), mk(sp_own, "p_mod", 32, ["mod"])
        p_dve, p_act, p_pe = mk(dve_own, "p_dve"), mk(act_own, "p_act"), mk(pe_own, "p_pe")
        p_st = mk(sp_own, "p_st", 64, ["st"])
        pl_dve, pl_act = mk(dve_own, "pl_dve"), mk(act_own, "pl_act")
        c_par = sem("c_par")
        c_ld = [mk(sp_own, f"c_ld{c}", 16, ["ld"]) for c in range(6)]
        c_st = mk(sp_own, "c_st", 96, ["st"])
        c_dve, c_act, c_pe = mk(dve_own, "c_dve"), mk(act_own, "c_act"), mk(pe_own, "c_pe")
        s_con = sem("s_con")
        s_pad = sem("s_pad")
        loads = dict(la=1, qc=5, tx=1, ft=1, tv=1, mb=2, ls=1, sm=1, st=2)
        s_la, s_qc, s_tx, s_ft, s_tv, s_mb, s_ls, s_sm, s_st = (
            [mk(sp_own, f"s_{k}{d}", 16 * n, [k]) for d in (0, 1)] for k, n in loads.items())
        s_dve = [mk(dve_own, f"s_dve{d}") for d in (0, 1)]
        s_act = [mk(act_own, f"s_act{d}") for d in (0, 1)]
        s_pe = [mk(pe_own, f"s_pe{d}") for d in (0, 1)]
        s_pool = [mk(pool_own, f"s_pool{d}") for d in (0, 1)]
        e_par, e_par2, e_w = sem("e_par"), sem("e_par2"), sem("e_w")
        o_ld, o_ldx = mk(sp_own, "o_ld", 64, ["ld"]), mk(sp_own, "o_ldx", 64, ["ld"])
        o_dve, o_act, o_pe = mk(dve_own, "o_dve"), mk(act_own, "o_act"), mk(pe_own, "o_pe")
        q_dve, q_act, q_pe = mk(dve_own, "q_dve"), mk(act_own, "q_act"), mk(pe_own, "q_pe")
        e_x, e_st = mk(sp_own, "e_x", 16, ["x"]), mk(sp_own, "e_st", 16, ["st"])
        e_gat = [mk(pool_own, f"e_gat{j}", 16, [f"g{r}" for r in range(SLOTS // RING)], ahead=0) for j in range(RING)]
        e_pool = mk(pool_own, "e_pool")
        e_dve, e_act, e_pe = mk(dve_own, "e_dve"), mk(act_own, "e_act"), mk(pe_own, "e_pe")

        def give_credit(eng, own):
            for s in own:
                if s.names:
                    eng.sem_inc(s.sem, s.round)
            eng.sem_inc(credit, 1)
            eng.wait_ge(credit, 5)

        a = Area(base)
        WA = [a(KC * 512) for _ in range(4)]
        BA = [a(512, 2) for _ in range(4)]
        MO = [a(512, 2) for _ in range(4)]
        CT, CS2 = a(2 * KC), a(2 * KC)
        XI, PI_ = [a(TILES * D).rearrange("p (s n) -> p s n", s=TILES) for _ in (0, 1)]

        a = Area(base)
        WIN = a(KC * IN_W)
        win = WIN.rearrange("p (k n) -> p k n", k=KC)
        X, SC, SHF, U = a(D), a(D), a(D), a(D)
        UT = a(D)
        FA, CP, GG, TB = a(6 * P), a(6 * P), a(D), a(TOK_W)
        GAT = a(P, 32)
        WA2 = a(256, 32)
        BROW, COEF, SGN = a(2 * NDIR), a(2 * NDIR), a(2 * NDIR)
        BIG_, ALOG = a(8), a(16)
        Z, ZA, ZL = a(2 * NDIR), a(2 * NDIR), a(2 * NDIR)
        ST6, MV, SD, RS = a(12), a(2), a(1), a(1)
        assert a.top <= 53200 - 2 * KC * D
        dirs = TB[:, 256 + VA:].rearrange("p (d w) -> p d w", d=2)

        a = Area(base)
        NT = NPOS * P
        CW, CB_ = a(18), a(6)
        CI = a(6 * (NT + 2)).rearrange("p (c n) -> p c n", c=6)
        CV, CO = a(6 * NT).rearrange("p (c n) -> p c n", c=6), a(6 * NT).rearrange("p (c n) -> p c n", c=6)
        CTK = a(TILES * 640).rearrange("p (s n) -> p s n", s=TILES)

        a = Area(base)
        GM = a(S_W)
        sc = []
        for d in (0, 1):
            v = dict(TK=a(256 + VA + DB), FT=a(6 * P), TX=a(640), FX=a(2 * P), ST=a(S_W), MB=a(4), MC=a(1, 4),
                     CS=a(162), F4=a(1, 4), EX=a(8 * P), CTP=a(2 * P), CBM=a(2 * P), XD=a(512), XW=a(512),
                     EA=a(29), KT=a(NB * P), QB=a(P), QP=a(NB * 4 * BL), QH=a(P), EB=a(P), AT=a(4 * P),
                     KD=a(P), KMD=a(3 * P), G4=a(4), NG=a(4), G4R=a(P, 4), R4=a(P, 4), GG8=a(8), GT=a(4), EMA=a(16),
                     EM=a(16), ME=a(4 * P), QMP=a(4 * P), T1=a(512), T2=a(VA), T3=a(256), VW=a(VA), HM=a(VA),
                     DN=a(4), RC=a(4), Y=a(D), SN=a(S_W), MN=a(1, 4))
            sc.append(v)
        scan_top = a.top

        a = Area(53200 - 2 * KC * D)
        wo, wq = [a(KC * D).rearrange("p (k n) -> p k n", k=KC) for _ in (0, 1)]
        a = Area(53200 - 2 * KC * D - 3 * D - 8 - 2 * P - TOPK - 1)
        assert scan_top <= a.top
        peer_top = a.top
        GNW, L1W, L1B = a(D), a(D), a(D)
        DROW, KEYS, IOTA, LOFS = a(8), a(2 * P), a(TOPK), a(1)
        a = Area(base)
        ring = a(RING * 2 * D).rearrange("p (j n) -> p j n", j=RING)
        L2W, L2B = a(D), a(D)
        PARAMS_A = ((GNW, "gnorm_w"), (L1W, "ln1_w"), (L1B, "ln1_b"), (DROW, "ssd_d"), (LOFS, "lofs"))
        PARAMS_B = ((L2W, "ln2_w"), (L2B, "ln2_b"))
        SCO = a(2048)
        YF, YB = SCO[:, 0:D], SCO[:, D:2 * D]
        GO, TX3, XO, G1, SC2, SH2 = a(D), a(512), a(D), a(D), a(D), a(D)
        YT = a(D)
        SQ = YT
        U2T = YT
        QT = G1
        HR, HR2, HR3 = a(16), a(16), a(16)
        oST6, oMV, oSD, oRS = a(12), a(2), a(1), a(1)
        CAN = OH = SCO
        TV, TI = a(256), a(256)
        BV, BI, BA1, IFR, JFR = a(P), a(P), a(P), a(P), a(P)
        SM, SR = a(8), a(8)
        IDXN, GWN, IDXC, GWC = a(SLOTS), a(SLOTS), a(SLOTS), a(SLOTS)
        EU, EX1, EG2 = a(D), a(D), a(D)
        DOT, AG, AW = a(16), a(16), a(16)
        DG = a(DIAGS * P)
        eST6, eMV, eSD, eRS = a(12), a(2), a(1), a(1)
        assert a.top <= peer_top

        block = ctx.enter_context(nc.Block())

        @block.sync
        def _(sp):
            give_credit(sp, sp_own)
            sp.dma_start(ident, io["ident"]).then_inc(start_ld, 16)
            sp.dma_start(CT, c2t).then_inc(start_ld, 16)
            with sp.Fori(0, DEPTH) as l:
                with sp.Fori(0, 3) as jj:
                    it = l * 3 + jj
                    for u in range(4):
                        cols = bass.ds(jj * 2048 + u * 512, 512)
                        apart(sp, m_pe.sem, m_pe.at(it, f"mod{u}", 1))
                        apart(sp, m_dve.sem, m_dve.at(it, f"mod{u}", 1))
                        sp.dma_start(WA[u].rearrange("p (k n) -> p k n", k=KC),
                                     at1(w_ada, l)[:, cols].rearrange("(k p) n -> p k n", p=P)
                                     ).then_inc(m_w[u].sem, 16)
                        sp.dma_start(BA[u], at1(b_ada, l)[cols].partition_broadcast(2)
                                     ).then_inc(m_w[u].sem, 16)
            for d in (0, 1):
                sp.dma_start(TRI[d], io["tri"][d]).then_inc(sem_tri, 16)
                sp.dma_start(PERM[d], io["perm"][d]).then_inc(sem_tri, 16)
            for c0, c1 in ((0, 1), (P + 1, 2 * P + 1), (NPOS * P + 1, NPOS * P + 2)):
                with nc.allow_non_contiguous_dma(reason="one column at either edge"):
                    sp.dma_start(conv_d[:, :, c0:c1], io["zeros"][:, :, 0:c1 - c0]).then_inc(fill_cv, 16)
            for dst, src in ((XI, x_in), (PI_, pos_in)):
                sp.dma_start(dst[:, 0, :], src[0]).then_inc(i_ld.sem, 16)
                sp.dma_start(dst[:, 1:, :], src[2:].rearrange("s p n -> p s n")).then_inc(i_ld.sem, 16)
            apart(sp, i_dve.sem, i_dve.at(0, "add0"))
            sp.dma_start(xres[0], XI[:, 0, :]).then_inc(i_st.sem, 16)
            apart(sp, i_dve.sem, i_dve.at(0, "add1"))
            sp.dma_start(xres[2:].rearrange("s p n -> p s n"), XI[:, 1:, :]).then_inc(i_st.sem, 16)
            apart(sp, i_st.sem, i_st.at(0, "st"))
            meet(sp, 0)

            with sp.Fori(0, DEPTH) as l:
                def load_tile(r, p, mrow):
                    if not isinstance(r, int) or r:
                        apart(sp, n_dve.sem, n_dve.at(l * ROUNDS + r, "xn", 1))
                    sp.dma_start(X, at1(xres, p) if not isinstance(p, int) else xres[p]).then_inc(p_x.sem, 16)
                    if not isinstance(r, int) or r:
                        apart(sp, n_dve.sem, n_dve.at(l * ROUNDS + r, "xsh", 1))
                    sp.dma_start(SC, rows(mrow[D:2 * D])).then_inc(p_mod.sem, 16)
                    sp.dma_start(SHF, rows(mrow[0:D])).then_inc(p_mod.sem, 16)

                def load_w(q):
                    for c0, c1 in W_IN_PARTS[q]:
                        sp.dma_start(win[:, :, c0:c1], at1(io["w_in"], l)[:, c0:c1].rearrange("(k p) n -> p k n", p=P)
                                     ).then_inc(p_w[q], 16)

                mod_row = [modd[bass.ds(l, 1), g, :].rearrange("a n -> (a n)") for g in (0, 1)]
                load_tile(0, 0, mod_row[0])
                load_w(0)
                sp.dma_start(ALOG, rows(at1(io["ssd_a_log"], l))).then_inc(p_par, 16)
                sp.dma_start(BROW, rows(at1(io["gbias"], l))).then_inc(p_par, 16)
                sp.dma_start(BIG_, rows(at1(io["mlstm_bi"], l))).then_inc(p_par, 16)
                sp.dma_start(WA2, at1(io["wa2"], l)).then_inc(p_par, 16)
                sp.dma_start(SGN, rows(io["sgn"])).then_inc(p_par, 16)
                sp.dma_start(COEF, rows(io["coef"])).then_inc(p_par, 16)
                load_w(1)
                load_tile(1, 2, mod_row[1])
                load_w(2)
                load_w(3)
                for d, slots in ((0, (0, 2)), (1, (1, 6))):
                    for w, slot in enumerate(slots):
                        sp.dma_start(state[bass.ds(l, 1), d, slot], io["state0"][bass.ds(l, 1), d, w]).then_inc(fill_st, 16)
                        sp.dma_start(mstate[bass.ds(l, 1), d, slot], io["m0"][bass.ds(l, 1), d, w]).then_inc(fill_st, 16)
                sp.dma_start(wo, at1(io["w_out"], l).rearrange("(k p) n -> p k n", p=P)).then_inc(e_w, 16)
                sp.dma_start(wq, at1(io["peer_wq"], l).rearrange("(k p) n -> p k n", p=P)).then_inc(e_w, 16)
                with sp.Fori(0, TILES) as s:
                    it, p = l * TILES + s, pos(s)
                    load_tile(s + 2, second_pos(s), mod_row[1])
                    apart(sp, p_act.sem, p_act.at(it, "b2"))
                    sp.dma_start(at1(feat_d, p), FA).then_inc(p_st.sem, 16)
                    apart(sp, p_dve.sem, p_dve.at(it, "dt"))
                    sp.dma_start(conv_d[:, :, bass.ds(p * P + 1, P)],
                                 CP.rearrange("p (c n) -> p c n", c=6)).then_inc(p_st.sem, 16)
                    sp.dma_start(at1(tok_d, p), TB).then_inc(p_st.sem, 16)
                    apart(sp, p_act.sem, p_act.at(it, "sigmo"))
                    sp.dma_start(at1(gate_d, p), GG).then_inc(p_st.sem, 16)
                apart(sp, p_st.sem, p_st.at(l * TILES + TILES - 1, "st"))
                apart(sp, p_x.sem, p_x.at(l * (ROUNDS + 1) + ROUNDS, "x"))
                apart(sp, p_mod.sem, p_mod.at(l * (ROUNDS + 1) + ROUNDS, "mod"))
                meet(sp, l * PHASES + 1)

                apart(sp, fill_cv, 48)
                sp.dma_start(CW, at1(io["conv_w"], l)).then_inc(c_par, 16)
                sp.dma_start(CB_, at1(io["conv_b"], l)).then_inc(c_par, 16)
                for c in range(6):
                    sp.dma_start(CI[:, c, :], conv_d[:, c, :]).then_inc(c_ld[c].sem, 16)

                def token_rows(c0, c1):
                    sp.dma_start(ctok_d[0, :, c0:c1], CTK[:, 0, c0:c1]).then_inc(c_st.sem, 16)
                    sp.dma_start(ctok_d[2:, :, c0:c1].rearrange("s p n -> p s n"), CTK[:, 1:, c0:c1]).then_inc(c_st.sem, 16)

                apart(sp, c_act.sem, c_act.at(l, "alone3"))
                token_rows(0, 512)
                apart(sp, c_act.sem, c_act.at(l, "alone4"))
                token_rows(512, 640)
                apart(sp, c_act.sem, c_act.at(l, "silu5"))
                for c in (4, 5):
                    sp.dma_start(cfeat_d[:, :, (c - 4) * P:(c - 3) * P].rearrange("s p n -> p s n"),
                                 CO[:, c, :].rearrange("p (s n) -> p s n", s=NPOS)).then_inc(c_st.sem, 16)
                apart(sp, c_st.sem, c_st.at(l, "st"))
                meet(sp, l * PHASES + 2)


                def at_l(t, d, i):
                    return t[bass.ds(l, 1), d, i:i + 1] if isinstance(i, int) else t[bass.ds(l, 1), d, bass.ds(i, 1)]

                def one(t, i):
                    return t[i] if isinstance(i, int) else at1(t, i)

                dd = 256 + VA

                def load_la(d, p):
                    sp.dma_start(sc[d]["TK"][:, dd:], one(tok_d, p)[:, dd + d * DB:dd + (d + 1) * DB]).then_inc(s_la[d].sem, 16)

                def load_qc(d, p):
                    v = sc[d]
                    for g in (0, 1):
                        r = slice(HD * g, HD * g + HD)
                        sp.dma_start(v["CTP"][r, g * P:(g + 1) * P], one(cfeat_d, p)[r, P:2 * P]).then_inc(s_qc[d].sem, 16)
                        sp.dma_start(v["QMP"][r, :].rearrange("p (j h s) -> p j h s", j=2, h=2)[:, :, g, :],
                                     one(feat_d, p)[r, 2 * P:4 * P].rearrange("p (j s) -> p j s", j=2)
                                     ).then_inc(s_qc[d].sem, 16)

                def load_fx(d, p):
                    sp.dma_start(sc[d]["FX"], one(cfeat_d, p)).then_inc(s_qc[d].sem, 16)

                def load_mb(d, slot):
                    m = at_l(mstate, d, slot)
                    sp.dma_start(sc[d]["MB"], rows(m.rearrange("a b n -> (a b n)"))).then_inc(s_mb[d].sem, 16)
                    sp.dma_start(sc[d]["MC"], m.rearrange("a b (n c) -> (a b n) c", c=1)).then_inc(s_mb[d].sem, 16)

                def load_tx(d, p):
                    sp.dma_start(sc[d]["TX"], one(ctok_d, p)).then_inc(s_tx[d].sem, 16)

                def load_ft(d, p):
                    sp.dma_start(sc[d]["FT"], one(feat_d, p)).then_inc(s_ft[d].sem, 16)

                def load_tv(d, p):
                    sp.dma_start(sc[d]["TK"][:, 0:dd], one(tok_d, p)[:, 0:dd]).then_inc(s_tv[d].sem, 16)

                def load_st(d, slot):
                    sp.dma_start(sc[d]["ST"], at_l(state, d, slot).rearrange("a b p n -> (a b p) n")).then_inc(s_ls[d].sem, 16)

                apart(sp, fill_st, (l + 1) * 128)
                for d in (0, 1):
                    load_la(d, 0)
                for d in (0, 1):
                    apart(sp, s_pad, (l + 1) * 6)
                    load_tx(d, 0)
                    load_fx(d, 0)
                    load_qc(d, 0)
                    load_mb(d, d)
                    load_ft(d, 0)
                for d in (0, 1):
                    load_tv(d, 0)
                sp.dma_start(GM, io["gmask"]).then_inc(s_con, 16)
                for dst, src in PARAMS_A:
                    sp.dma_start(dst, rows(at1(io[src], l))).then_inc(e_par, 16)
                sp.dma_start(KEYS, at1(io["keys"], l)).then_inc(e_par, 16)
                sp.dma_start(IOTA, rows(io["iota"])).then_inc(e_par, 16)
                with sp.Fori(0, TILES) as s:
                    it, t = l * TILES + s, l * ROUNDS + s
                    p = (pos(s), bwd_pos(s))
                    q = (next_pos(s), next_bwd_pos(s))
                    both = (0, 1)
                    for d in both:
                        apart(sp, s_st[d].sem, s_st[d].at(it, "st", 1))
                        load_st(d, p[d] + d)
                    for d in both:
                        apart(sp, s_dve[d].sem, s_dve[d].at(it, "g4"))
                        apart(sp, s_pe[d].sem, s_pe[d].at(it, "cum"))
                        apart(sp, s_pool[d].sem, s_pool[d].at(it, "xd"))
                        load_la(d, q[d])
                    for d in both:
                        apart(sp, s_pe[d].sem, s_pe[d].at(it, "qk"))
                        load_qc(d, q[d])
                    for d in both:
                        apart(sp, s_dve[d].sem, s_dve[d].at(it, "em3"))
                        sp.dma_start(at_l(mstate, d, p[d] + 1 - d).rearrange("a b (n c) -> (a b n) c", c=1),
                                     sc[d]["MN"]).then_inc(s_sm[d].sem, 16)
                    for d in both:
                        apart(sp, s_pe[d].sem, s_pe[d].at(it, "ssd"))
                        load_fx(d, q[d])
                    for d in both:
                        apart(sp, s_sm[d].sem, s_sm[d].at(it, "sm"))
                        load_mb(d, q[d] + d)
                    for d in both:
                        apart(sp, s_pe[d].sem, s_pe[d].at(it, "ups"))
                        load_tx(d, q[d])
                    for d in both:
                        apart(sp, s_pe[d].sem, s_pe[d].at(it, "mli"))
                        load_ft(d, q[d])
                        apart(sp, s_pe[d].sem, s_pe[d].at(it, "upm"))
                        load_tv(d, q[d])
                    for d in both:
                        apart(sp, s_act[d].sem, s_act[d].at(it, "yg"))
                        apart(sp, s_dve[d].sem, s_dve[d].at(it, "sng"))
                        apart(sp, s_pool[d].sem, s_pool[d].at(it, "sna"))
                        sp.dma_start(at_l(state, d, p[d] + 1 - d).rearrange("a b p n -> (a b p) n"),
                                     sc[d]["SN"]).then_inc(s_st[d].sem, 16)
                        sp.dma_start(y_d[d, bass.ds(p[d], 1)].rearrange("a p n -> (a p) n"), sc[d]["Y"]
                                     ).then_inc(s_st[d].sem, 16)
                for d in (0, 1):
                    for k, c in (("la", s_la), ("qc", s_qc), ("tx", s_tx), ("ft", s_ft), ("tv", s_tv), ("mb", s_mb)):
                        apart(sp, c[d].sem, c[d].at(l * ROUNDS + TILES, k))
                    apart(sp, s_st[d].sem, s_st[d].at(l * TILES + TILES - 1, "st"))
                meet(sp, l * PHASES + 3)

                def mix(t, p, mrow):
                    apart(sp, q_dve.sem, q_dve.at(t, "smd", 1))
                    for dst, src in ((YF, y_d[0, bass.ds(p, 1)].rearrange("a p n -> (a p) n")),
                                     (YB, y_d[1, bass.ds(p, 1)].rearrange("a p n -> (a p) n")),
                                     (GO, at1(gate_d, p)), (TX3, at1(ctok_d, p)[:, 0:512])):
                        sp.dma_start(dst, src).then_inc(o_ld.sem, 16)
                    apart(sp, q_pe.sem, q_pe.at(t, "s3", 1))
                    for dst, src in ((XO, at1(xres, p)), (G1, rows(mrow[2 * D:3 * D])),
                                     (SC2, rows(mrow[4 * D:5 * D])), (SH2, rows(mrow[3 * D:4 * D]))):
                        sp.dma_start(dst, src).then_inc(o_ldx.sem, 16)

                mix(l * ROUNDS, 0, modd[bass.ds(l, 1), 0, :].rearrange("a n -> (a n)"))
                for dst, src in PARAMS_B:
                    sp.dma_start(dst, rows(at1(io[src], l))).then_inc(e_par2, 16)
                with sp.Fori(0, TILES) as s:
                    it, p = l * TILES + s, pos(s)
                    mrow = modd[bass.ds(l, 1), bass.ds(group(s), 1), :].rearrange("a b n -> (a b n)")
                    apart(sp, e_dve.sem, e_dve.at(it, "r1", 1))
                    sp.dma_start(EG2, rows(mrow[5 * D:6 * D])).then_inc(e_x.sem, 16)
                    apart(sp, e_dve.sem, e_dve.at(it, "eu"))
                    apart(sp, e_act.sem, e_act.at(it, "ex"))
                    mix(l * ROUNDS + 1 + s, next_pos(s), modd[bass.ds(l, 1), 1, :].rearrange("a n -> (a n)"))
                    apart(sp, e_dve.sem, e_dve.at(it, "xb"))
                    sp.dma_start(at1(xres, p), EX1).then_inc(e_st.sem, 16)
                apart(sp, e_st.sem, e_st.at(l * TILES + TILES - 1, "st"))
                apart(sp, o_ld.sem, o_ld.at(l * ROUNDS + TILES, "ld"))
                apart(sp, o_ldx.sem, o_ldx.at(l * ROUNDS + TILES, "ld"))
                meet(sp, l * PHASES + 4)

        @block.vector
        def _(ve):
            give_credit(ve, dve_own)
            v_ = nc.vector

            def stats(link, tag, x, st6, mv):
                for h in (0, 1):
                    link(f"st{h}{tag}", v_.bn_stats(st6[:, 6 * h:6 * h + 6], x[:, 512 * h:512 * h + 512]))
                    yield
                ve.sem_inc(passed, 1)
                link("mv" + tag, v_.bn_aggr(mv, st6))
                yield

            v_.memset(ones, 1.0).then_inc(sem_ones, 1)
            v_.memset(eps, EPS).then_inc(sem_ones, 1)
            ve.wait_ge(sem_ones, 2)

            ve.sem_inc(passed, 1)
            with ve.Fori(0, DEPTH) as l:
                ve.sem_inc(passed, 1)
                with ve.Fori(0, 3) as jj:
                    it = l * 3 + jj
                    link = linker(ve, m_dve, it)
                    for u in range(4):
                        ve.wait_ge(m_pe.sem, m_pe.at(it, f"mod{u}"))
                        ve.wait_ge(m_w[u].sem, m_w[u].at(it, "w"))
                        ve.wait_ge(m_out[u].sem, m_out[u].at(it, "out", 1))
                        link(f"mod{u}", v_.tensor_tensor(MO[u], ps[u][0:2, :], BA[u], ALU.add))
            link = linker(ve, i_dve, 0)
            ve.wait_ge(i_ld.sem, i_ld.at(0, "ld"))
            link("add0", v_.tensor_tensor(XI[:, 0, :], XI[:, 0, :], PI_[:, 0, :], ALU.add))
            link("add1", v_.tensor_tensor(XI[:, 1:, :], XI[:, 1:, :], PI_[:, 1:, :], ALU.add))
            meet(ve, 0)

            ve.sem_inc(passed, 1)
            with ve.Fori(0, DEPTH) as l:

                def normed(r):
                    t, ld = l * ROUNDS + r, l * (ROUNDS + 1) + r
                    link = linker(ve, n_dve, t)
                    ve.wait_ge(p_x.sem, p_x.at(ld, "x"))
                    for _ in stats(link, "", X, ST6, MV):
                        pass
                    ve.wait_ge(n_act.sem, n_act.at(t, "sd"))
                    link("rs", v_.reciprocal(RS, SD))
                    ve.wait_ge(n_pe.sem, n_pe.at(t, "tr1", 1))
                    link("xn", v_.tensor_scalar(U, X, MV[:, 0:1], RS, ALU.subtract, ALU.mult))
                    ve.wait_ge(p_mod.sem, p_mod.at(ld, "mod"))
                    link("xs", v_.scalar_tensor_tensor(U, SC, 1.0, U, ALU.add, ALU.mult))
                    link("xsh", v_.tensor_tensor(U, U, SHF, ALU.add))

                normed(0)
                ve.wait_ge(p_par, (l + 1) * 96)
                link = linker(ve, pl_dve, l)
                ve.wait_ge(pl_act.sem, pl_act.at(l, "ea"))
                cf = grp(COEF, a=2)
                link("coef", v_.tensor_scalar(cf[:, :, 132:140], grp(ALOG, a=2), -1.0, None, ALU.mult))
                link("vone", v_.memset(TB[:, 256:256 + VA].rearrange("p (h e) -> p h e", h=MH)[:, :, HD:HD + 1], 1.0))

                ve.sem_inc(passed, 1)
                with ve.Fori(0, TILES) as s:
                    it = l * TILES + s
                    link = linker(ve, p_dve, it)
                    ve.wait_ge(n_pe.sem, n_pe.at(l * ROUNDS + s, "tr0"))
                    ve.wait_ge(p_pe.sem, p_pe.at(it, "last", 1))
                    link("ut0", v_.tensor_copy(UT[:, 0:512], ps[0][:, :]), hold=False)
                    ve.wait_ge(n_pe.sem, n_pe.at(l * ROUNDS + s, "tr1"))
                    link("ut1", v_.tensor_copy(UT[:, 512:1024], ps[1][:, :]))
                    ve.wait_ge(p_st.sem, p_st.at(it, "st", 1))
                    ve.wait_ge(p_pe.sem, p_pe.at(it, "D"))
                    link("gat", v_.tensor_copy(GAT, ps[5][0:32, 0:P]), hold=False)
                    link("c4", v_.tensor_copy(CP[:, 2 * P:6 * P], ps[4][:, :]))
                    normed(1 + s)
                    ve.wait_ge(p_pe.sem, p_pe.at(it, "gate"))
                    z, br = grp(Z, a=2), grp(BROW, a=2)
                    link("z0", v_.tensor_tensor(z[:, :, 0:128], grp(ps[5][:, 160:416], a=2), br[:, :, 0:128], ALU.add), hold=False)
                    link("z1", v_.tensor_tensor(z[:, :, 128:132], grp(ps[5][:, 136:144], a=2), br[:, :, 128:132], ALU.add), hold=False)
                    link("z2", v_.tensor_tensor(z[:, :, 132:140], grp(ps[5][:, 144:160], a=2), br[:, :, 132:140], ALU.add))
                    link("ig", v_.tensor_tensor(dirs[:, :, NDIR:NDIR + 4], grp(ps[5][:, 128:136], a=2),
                                                grp(BIG_, a=2), ALU.add), hold=False)
                    link("zs", v_.tensor_tensor(Z, Z, SGN, ALU.mult))
                    link("za", v_.scalar_tensor_tensor(ZA, Z, -1.0, Z, ALU.mult, ALU.max))
                    ve.wait_ge(p_pe.sem, p_pe.at(it, "E"))
                    link("vg", v_.tensor_copy(TB[:, 0:256], ps[6][:, 0:256]), hold=False)
                    link("vm", v_.tensor_copy(TB[:, 256:256 + VA].rearrange("p (h e) -> p h e", h=MH)[:, :, 0:HD],
                                              ps[6][:, 256:512].rearrange("p (h e) -> p h e", h=MH)), hold=False)
                    ve.wait_ge(p_act.sem, p_act.at(it, "ln"))
                    link("sp", v_.scalar_tensor_tensor(Z, Z, 0.0, ZL, ALU.max, ALU.add))
                    link("la", v_.tensor_tensor(dirs[:, :, 0:NDIR], grp(Z, a=2), cf, ALU.mult), hold=False)
                    link("dt", v_.tensor_copy(dirs[:, :, NDIR + 4:DB], grp(Z, a=2)[:, :, 132:140]))
                meet(ve, l * PHASES + 1)

                ve.wait_ge(c_par, (l + 1) * 32)
                link = linker(ve, c_dve, l)
                for c in range(6):
                    ve.wait_ge(c_ld[c].sem, c_ld[c].at(l, "ld"))
                    link(f"a{c}", v_.tensor_scalar(CV[:, c, :], CI[:, c, 0:NT], CW[:, 3 * c:3 * c + 1], None, ALU.mult))
                    link(f"b{c}", v_.scalar_tensor_tensor(CV[:, c, :], CI[:, c, 1:NT + 1], CW[:, 3 * c + 1:3 * c + 2],
                                                          CV[:, c, :], ALU.mult, ALU.add))
                    link(f"c{c}", v_.scalar_tensor_tensor(CV[:, c, :], CI[:, c, 2:NT + 2], CW[:, 3 * c + 2:3 * c + 3],
                                                          CV[:, c, :], ALU.mult, ALU.add))
                meet(ve, l * PHASES + 2)

                ve.wait_ge(sem_tri, 64)
                ve.wait_ge(s_pad, (l + 1) * 6)
                ve.sem_inc(passed, 1)
                with ve.Fori(0, TILES) as s:
                    it = l * TILES + s
                    t = l * ROUNDS + s
                    links = [linker(ve, s_dve[d], it) for d in (0, 1)]
                    V = sc

                    def hb(ap, h, n):
                        return ap.unsqueeze(2).broadcast_to([P, h, n])

                    for d in (0, 1):
                        b, L = V[d], links[d]
                        cs = b["CS"]
                        ve.wait_ge(s_pe[d].sem, s_pe[d].at(it, "sum"))
                        L("cs", v_.tensor_copy(cs[:, 0:153], ps[4 * d][:, 0:153]), hold=False)
                        L("f4", v_.tensor_copy(b["F4"], ps[4 * d][0:4, 153:154]))
                        L("dec", v_.tensor_tensor(cs[:, 153:161], cs[:, 144:152], cs[:, 132:140], ALU.subtract), hold=False)
                        ve.wait_ge(s_la[d].sem, s_la[d].at(t, "la"))
                        L("g4", v_.tensor_tensor(b["G4"], b["TK"][:, 256 + VA + NDIR:256 + VA + NDIR + 4],
                                                 cs[:, 128:132], ALU.subtract))
                        L("ng", v_.tensor_scalar(b["NG"], b["G4"], -1.0, None, ALU.mult), hold=False)
                    for d in (0, 1):
                        b, L = V[d], links[d]
                        cs = b["CS"]
                        ve.wait_ge(s_pe[d].sem, s_pe[d].at(it, "g4r"))
                        L("cbm", v_.tensor_tensor(grp(b["CBM"], a=2), grp(ps[4 * d + 3][:, 0:256], a=2),
                                                  TRI[d].unsqueeze(1).broadcast_to([P, 2, P]), ALU.mult), hold=False)
                        L("g4r", v_.tensor_copy(b["G4R"], ps[4 * d][0:4, 0:P]))
                        ve.wait_ge(s_mb[d].sem, s_mb[d].at(t, "mb"))
                        L("r4", v_.tensor_tensor_scan(b["R4"], b["G4R"], b["G4R"], b["MC"], ALU.max, ALU.max))
                        ve.wait_ge(s_sm[d].sem, s_sm[d].at(it, "sm", 1))
                        L("mn", v_.tensor_tensor(b["MN"], b["F4"], b["R4"][:, P - 1:P], ALU.add), hold=False)
                        mid = cs[:, BL // 2:P:BL]
                        kt = grp(b["KT"], a=NB)
                        L("kta", v_.tensor_tensor(kt, cs[:, 0:P].unsqueeze(1).broadcast_to([P, NB, P]),
                                                  hb(mid, NB, P), ALU.subtract), hold=False)
                        L("qba", v_.tensor_tensor(grp(b["QB"], a=NB), grp(cs[:, 0:P], a=NB), hb(mid, NB, BL),
                                                  ALU.subtract), hold=False)
                    for d in (0, 1):
                        b, L = V[d], links[d]
                        gqT, gkT = b["FT"][:, 0:P], b["FT"][:, P:2 * P]
                        ve.wait_ge(s_pe[d].sem, s_pe[d].at(it, "km"))
                        L("gg8", v_.tensor_copy(b["GG8"], ps[4 * d][:, 128:136]), hold=False)
                        ve.wait_ge(s_act[d].sem, s_act[d].at(it, "kd"))
                        ve.wait_ge(s_ft[d].sem, s_ft[d].at(t, "ft"))
                        L("qh", v_.tensor_tensor(b["QH"], b["EB"], gqT, ALU.mult), hold=False)
                        L("kdm", v_.tensor_tensor(b["KD"], b["KD"], gkT, ALU.mult), hold=False)
                        ve.wait_ge(s_act[d].sem, s_act[d].at(it, "qb"))
                        for h in range(GH):
                            r = slice(GDK * h, GDK * h + GDK)
                            L(f"qp{h}", v_.scalar_tensor_tensor(
                                b["QP"][r, :].rearrange("p (b h i) -> p b h i", b=NB, h=GH)[:, :, h, :],
                                b["QB"][r, :].rearrange("p (b i) -> p b i", b=NB), E_CLAMP,
                                b["FT"][r, 0:P].rearrange("p (b i) -> p b i", b=NB), ALU.min, ALU.mult), hold=False)
                        L("ktm", v_.scalar_tensor_tensor(grp(b["KT"], a=NB), grp(b["KT"], a=NB), E_CLAMP,
                                                  gkT.unsqueeze(1).broadcast_to([P, NB, P]), ALU.min, ALU.mult), hold=False)
                    for d in (0, 1):
                        b, L = V[d], links[d]
                        cs, ema = b["CS"], b["EMA"]
                        ve.wait_ge(s_pe[d].sem, s_pe[d].at(it, "kdt"))
                        L("gt", v_.tensor_copy(b["GT"], ps[4 * d][:, 136:140]))
                        L("em0", v_.tensor_tensor(ema[:, 0:4], b["MB"], b["GT"], ALU.subtract), hold=False)
                        L("em1", v_.scalar_tensor_tensor(ema[:, 4:8], cs[:, 128:132], -1.0, b["GT"],
                                                         ALU.mult, ALU.subtract), hold=False)
                        L("em2", v_.tensor_tensor(ema[:, 8:12], b["G4"], b["GG8"][:, 4:8], ALU.subtract), hold=False)
                        L("em3", v_.tensor_tensor(ema[:, 12:16], b["MB"], b["GG8"][:, 4:8], ALU.subtract), hold=False)
                    for d in (0, 1):
                        b, L = V[d], links[d]
                        ve.wait_ge(s_act[d].sem, s_act[d].at(it, "ex0"))
                        ex = b["EX"].rearrange("p (g r s) -> p g r s", g=2, r=4)
                        L("w8", v_.tensor_tensor(ex, ex, grp(b["CBM"], a=2).unsqueeze(2).broadcast_to([P, 2, 4, P]),
                                                 ALU.mult), hold=False)
                        ve.wait_ge(s_pe[d].sem, s_pe[d].at(it, "qk"))
                        ve.wait_ge(s_pool[d].sem, s_pool[d].at(it, "sna1", 1))
                        L("qkm", v_.tensor_tensor(grp(b["T1"], a=4), grp(ps[4 * d + 3][:, :], a=4),
                                                  TRI[d].unsqueeze(1).broadcast_to([P, 4, P]), ALU.mult), hold=False)
                    for d in (0, 1):
                        b, L = V[d], links[d]
                        ve.wait_ge(s_act[d].sem, s_act[d].at(it, "me"))
                        ve.wait_ge(s_dve[d].sem, s_dve[d].at(it, "qkm"))
                        L("wm", v_.tensor_tensor(b["ME"], b["ME"], b["T1"], ALU.mult), hold=False)
                        ve.wait_ge(s_pe[d].sem, s_pe[d].at(it, "ssd"))
                        ve.wait_ge(s_st[d].sem, s_st[d].at(it, "st", 1))
                        L("ys0", v_.tensor_tensor(grp(b["Y"][:, 512:], a=SH), grp(ps[4 * d + 2][:, :], a=SH),
                                                  hb(b["EA"][:, 0:8], SH, HD), ALU.mult))
                        L("ys1", v_.tensor_tensor(b["Y"][:, 512:], b["Y"][:, 512:], ps[4 * d + 1][:, :], ALU.add), hold=False)
                    for d in (0, 1):
                        b, L = V[d], links[d]
                        ve.wait_ge(s_pe[d].sem, s_pe[d].at(it, "att"))
                        L("at", v_.tensor_tensor(
                            b["AT"].rearrange("p (h b i) -> p h b i", h=GH, b=NB),
                            ps[4 * d][:, :].rearrange("p (b h i) -> p h b i", b=NB, h=GH),
                            TRI[d].rearrange("p (b i) -> p b i", b=NB).unsqueeze(1).broadcast_to([P, GH, NB, BL]),
                            ALU.mult), hold=False)
                        ve.wait_ge(s_pe[d].sem, s_pe[d].at(it, "ups"))
                        ve.wait_ge(s_con, (l + 1) * 16)
                        L("t1", v_.tensor_tensor(b["T1"], ps[4 * d + 3][:, :], GM[:, S_SSD:S_ML], ALU.mult), hold=False)
                    for d in (0, 1):
                        b, L = V[d], links[d]
                        sn, st, em = b["SN"], b["ST"], b["EM"]
                        ve.wait_ge(s_pe[d].sem, s_pe[d].at(it, "mli"))
                        L("hm0", v_.tensor_tensor(grp(b["HM"], a=MH), grp(ps[4 * d + 2][:, 0:VA], a=MH),
                                                  hb(em[:, 0:4], MH, HD + 1), ALU.mult))
                        L("hm1", v_.tensor_tensor(b["HM"], b["HM"], ps[4 * d + 1][:, 0:VA], ALU.add))
                        hm = grp(b["HM"], a=MH)
                        L("dn0", v_.scalar_tensor_tensor(b["DN"].unsqueeze(2), hm[:, :, HD:HD + 1], -1.0,
                                                         hm[:, :, HD:HD + 1], ALU.mult, ALU.max))
                        L("dn1", v_.tensor_tensor(b["DN"], b["DN"], em[:, 4:8], ALU.max))
                        L("rc", v_.reciprocal(b["RC"], b["DN"]))
                        L("ym", v_.tensor_tensor(grp(b["Y"][:, 256:512], a=MH), hm[:, :, 0:HD], hb(b["RC"], MH, HD), ALU.mult), hold=False)
                        ve.wait_ge(s_pe[d].sem, s_pe[d].at(it, "upm"))
                        ve.wait_ge(s_pool[d].sem, s_pool[d].at(it, "sna", 1))
                        L("t2", v_.tensor_tensor(b["T2"], ps[4 * d + 3][:, 0:VA], GM[:, S_ML:S_GLA], ALU.mult), hold=False)
                        ve.wait_ge(s_act[d].sem, s_act[d].at(it, "yg"))
                        L("t3", v_.tensor_tensor(b["T3"], ps[4 * d][:, 256:512], GM[:, S_GLA:S_W], ALU.mult))
                        L("sng", v_.scalar_tensor_tensor(sn[:, S_GLA:S_W], st[:, S_GLA:S_W], b["EA"][:, 20:21], b["T3"],
                                                         ALU.mult, ALU.add), hold=False)
                meet(ve, l * PHASES + 3)

                ve.wait_ge(e_par, (l + 1) * 112)

                def mix(t):
                    link = linker(ve, o_dve, t)
                    ve.wait_ge(o_ld.sem, o_ld.at(t, "ld"))
                    yf = YF
                    link("y0", v_.tensor_tensor(yf, YF, YB, ALU.add))
                    yield
                    tx = grp(TX3, a=SH)
                    link("y1", v_.tensor_tensor(tx, tx, DROW.unsqueeze(2).broadcast_to([P, SH, HD]), ALU.mult))
                    yield
                    link("y2", v_.tensor_tensor(yf[:, 512:], yf[:, 512:], TX3, ALU.add))
                    yield
                    link("y3", v_.tensor_tensor(yf, yf, GO, ALU.mult))
                    yield
                    ve.wait_ge(q_pe.sem, q_pe.at(t, "q7", 1))
                    link("sq", v_.tensor_tensor(SQ, yf, yf, ALU.mult))
                    yield
                    link("hr", v_.tensor_reduce(HR, grp(SQ, a=16), AX, ALU.add))
                    yield
                    link("hrm", v_.tensor_scalar(HR2, HR, 1.0 / HD, EPS, ALU.mult, ALU.add))
                    yield
                    ve.wait_ge(o_act.sem, o_act.at(t, "hsd"))
                    link("hrr", v_.reciprocal(HR3, HR3))
                    yield
                    link("yn1", v_.tensor_tensor(grp(yf, a=16), grp(yf, a=16),
                                                 HR3.unsqueeze(2).broadcast_to([P, 16, HD]), ALU.mult))
                    yield
                    link("yn2", v_.tensor_tensor(yf, yf, GNW, ALU.mult))
                    yield
                    ve.wait_ge(o_pe.sem, o_pe.at(t, "yt0"))
                    link("yt0", v_.tensor_copy(YT[:, 0:512], ps[0][:, :]))
                    yield
                    ve.wait_ge(o_pe.sem, o_pe.at(t, "out"))
                    ve.wait_ge(o_ldx.sem, o_ldx.at(t, "ld"))
                    for h in (0, 1):
                        c = slice(512 * h, 512 * h + 512)
                        link(f"g{h}", v_.tensor_tensor(G1[:, c], ps[2 + h][:, :], G1[:, c], ALU.mult))
                        yield
                    link("r1", v_.scalar_tensor_tensor(XO, XO, ALPHA, G1, ALU.mult, ALU.add))
                    yield
                    yield from stats(link, "a", XO, oST6, oMV)
                    ve.wait_ge(o_act.sem, o_act.at(t, "sda"))
                    link("rsa", v_.reciprocal(oRS, oSD))
                    yield
                    link("x1a", v_.tensor_scalar(XO, XO, oMV[:, 0:1], oRS, ALU.subtract, ALU.mult))
                    yield
                    link("x1b", v_.tensor_tensor(XO, XO, L1W, ALU.mult))
                    yield
                    link("x1c", v_.tensor_tensor(XO, XO, L1B, ALU.add))
                    yield
                    yield from stats(link, "b", XO, oST6, oMV)
                    ve.wait_ge(o_act.sem, o_act.at(t, "sdb"))
                    link("rsb", v_.reciprocal(oRS, oSD))
                    yield
                    link("u2a", v_.tensor_scalar(G1, XO, oMV[:, 0:1], oRS, ALU.subtract, ALU.mult))
                    yield
                    link("u2b", v_.scalar_tensor_tensor(SC2, SC2, 1.0, G1, ALU.add, ALU.mult))
                    yield
                    link("u2c", v_.tensor_tensor(SC2, SC2, SH2, ALU.add))
                    yield

                def scores(t, indices_taken):
                    link = linker(ve, q_dve, t)

                    def best(name, some):
                        steps = (lambda x, top, at: v_.max(top[:, 0:8], x),
                                 lambda x, top, at: v_.max_index(at[:, 0:8], top[:, 0:8], x),
                                 lambda x, top, at: v_.match_replace(x, top[:, 0:8], x, -3.0e38),
                                 lambda x, top, at: v_.max(top[:, 8:16], x),
                                 lambda x, top, at: v_.max_index(at[:, 8:16], top[:, 8:16], x))
                        for k, step in enumerate(steps):
                            ve.sem_inc(passed, 1)
                            for n, row in enumerate(some):
                                link(f"{name}.{k}.{n}", step(*row), hold=row is some[-1])
                                yield

                    ve.wait_ge(q_pe.sem, q_pe.at(t, "ut0"))
                    link("ut0", v_.tensor_copy(U2T[:, 0:512], ps[0][:, :]))
                    yield
                    ve.wait_ge(q_pe.sem, q_pe.at(t, "q3"))
                    link("qt0", v_.tensor_copy(QT[:, 0:512], ps[2][:, :]))
                    yield
                    for b in range(4):
                        ve.wait_ge(q_act.sem, q_act.at(t, f"sc{b}"))
                        yield from best(f"half{b}", [
                            (SCO[:, i * P:(i + 1) * P], TV[:, 16 * i:16 * i + 16], TI[:, 16 * i:16 * i + 16].bitcast(U32))
                            for i in range(4 * b, 4 * b + 4)])
                    link("tf", v_.tensor_copy(TI, TI.bitcast(U32)))
                    yield
                    tv4 = TV.rearrange("p (h q a) -> p h q a", h=HEADS, q=2)
                    tf4 = TI.rearrange("p (h q a) -> p h q a", h=HEADS, q=2)
                    can4 = CAN.rearrange("p (h a b) -> p h a b", h=HEADS, a=TOPK)
                    full = [P, HEADS, TOPK, TOPK]
                    link("can", v_.tensor_tensor(can4, tv4[:, :, 0, :].unsqueeze(3).broadcast_to(full),
                                                 tv4[:, :, 1, :].unsqueeze(2).broadcast_to(full), ALU.add))
                    yield "long"
                    for b in (0, 1):
                        yield from best(f"pair{b}", [
                            (CAN[:, h * 256:(h + 1) * 256], BV[:, 16 * h:16 * h + 16], BI[:, 16 * h:16 * h + 16].bitcast(U32))
                            for h in range(4 * b, 4 * b + 4)])
                    for q, (op, by, dst) in enumerate(((ALU.logical_shift_right, 4, IFR), (ALU.bitwise_and, 15, JFR))):
                        link(f"ba{q}", v_.tensor_scalar(BA1.bitcast(U32), BI.bitcast(U32), by, None, op))
                        yield
                        link(f"bf{q}", v_.tensor_copy(BA1, BA1.bitcast(U32)))
                        yield
                        link(f"oh{q}", v_.tensor_tensor(grp(OH, a=P), BA1.unsqueeze(2).broadcast_to([P, P, TOPK]),
                                                        IOTA.unsqueeze(1).broadcast_to([P, P, TOPK]), ALU.is_equal))
                        yield "long"
                        link(f"oi{q}", v_.tensor_tensor(can4, can4, tf4[:, :, q, :].unsqueeze(2).broadcast_to(full), ALU.mult))
                        yield "long"
                        link(f"oj{q}", v_.tensor_reduce(dst, grp(OH, a=P), AX, ALU.add))
                        yield "long"
                    link("ixa", v_.scalar_tensor_tensor(IFR, IFR, 128.0, JFR, ALU.mult, ALU.add))
                    yield
                    ve.wait_ge(e_pool.sem, indices_taken)
                    link("ixb", v_.tensor_scalar(IDXN.bitcast(U32), IFR, LOFS, None, ALU.add))
                    yield
                    bv3 = grp(BV, a=HEADS)
                    link("sma", v_.tensor_tensor(grp(JFR, a=HEADS), bv3, bv3[:, :, 0:1].broadcast_to([P, HEADS, TOPK]),
                                                 ALU.subtract))
                    yield "hold"
                    ve.wait_ge(q_act.sem, q_act.at(t, "sme"))
                    link("smb", v_.tensor_reduce(SM, grp(IFR, a=HEADS), AX, ALU.add))
                    yield
                    link("smc", v_.reciprocal(SR, SM))
                    yield
                    link("smd", v_.tensor_tensor(grp(GWN, a=HEADS), grp(IFR, a=HEADS),
                                                 SR.unsqueeze(2).broadcast_to([P, HEADS, TOPK]), ALU.mult))

                def whole_round(t, indices_taken):
                    yield from mix(t)
                    yield from scores(t, indices_taken)

                for _ in whole_round(l * ROUNDS, e_pool.at(l * TILES, "ix1", 1)):
                    pass
                ve.sem_inc(passed, 1)
                with ve.Fori(0, TILES) as s:
                    it = l * TILES + s
                    link = linker(ve, e_dve, it)
                    beside = whole_round(l * ROUNDS + 1 + s, e_pool.at(it, "ix1"))
                    link("gwc", v_.tensor_copy(GWC, GWN))
                    link("eu", v_.tensor_copy(EU, SC2))

                    held, full = [], []

                    def dots(g):
                        for n in range(GRP * g, GRP * g + GRP):
                            r, j = divmod(n, RING)
                            ve.wait_ge(e_gat[j].sem, e_gat[j].at(it, f"g{r}"))
                            link(f"dot{n}", v_.tensor_tensor_reduce(
                                ring[:, j, 0:D], ring[:, j, 0:D], EU, 1.0, 0.0, ALU.mult, ALU.add,
                                DOT[:, n % 16:n % 16 + 1]))
                            steps = DVE_STEPS.get(n, 0)
                            if n >= TOP_FIRST:
                                steps = 4 if n < TOP_FIRST + 21 else 3 + n % 2
                            if n - 1 in full or held and n < SUM_FIRST:
                                steps = 0
                            if steps:
                                ve.sem_inc(passed, 1)
                            for _ in range(steps):
                                hint = next(beside, None)
                                if hint == "hold":
                                    held.append(n)
                                if hint:
                                    full.append(n)
                                    break

                    def weigh(g):
                        c = slice(GRP * g % 16, GRP * g % 16 + GRP)
                        ve.wait_ge(e_act.sem, e_act.at(it, f"ge{g}"))
                        link(f"aw{g}", v_.tensor_tensor(AW[:, c], AG[:, c], GWC[:, GRP * g:GRP * g + GRP], ALU.mult))

                    dots(0)
                    for g in range(1, SLOTS // GRP):
                        dots(g)
                        weigh(g - 1)
                    weigh(SLOTS // GRP - 1)
                    for _ in beside:
                        pass
                    ve.wait_ge(e_x.sem, e_x.at(it, "x"))
                    ve.wait_ge(e_act.sem, e_act.at(it, "ex"))
                    ve.wait_ge(e_pe.sem, e_pe.at(it, f"v{SLOTS - 1}"))
                    for h in (0, 1):
                        c = slice(512 * h, 512 * h + 512)
                        link(f"r0{h}", v_.tensor_tensor(EG2[:, c], ps[4 + h][:, :], EG2[:, c], ALU.mult))
                    link("r1", v_.scalar_tensor_tensor(EX1, EX1, ALPHA, EG2, ALU.mult, ALU.add))
                    for _ in stats(link, "", EX1, eST6, eMV):
                        pass
                    ve.wait_ge(e_act.sem, e_act.at(it, "sd"))
                    link("r2", v_.reciprocal(eRS, eSD))
                    link("xa", v_.tensor_scalar(EX1, EX1, eMV[:, 0:1], eRS, ALU.subtract, ALU.mult))
                    ve.wait_ge(e_par2, (l + 1) * 32)
                    link("xw", v_.tensor_tensor(EX1, EX1, L2W, ALU.mult))
                    link("xb", v_.tensor_tensor(EX1, EX1, L2B, ALU.add))
                meet(ve, l * PHASES + 4)

        @block.scalar
        def _(ae):
            give_credit(ae, act_own)
            a_ = nc.scalar

            ae.wait_ge(start_ld, 32)
            ae.activation(CS2, CT, ACT.Silu).then_inc(sem_silu, 1)
            ae.wait_ge(sem_ones, 2)
            ae.sem_inc(passed, 1)
            with ae.Fori(0, DEPTH) as l:
                with ae.Fori(0, 3) as jj:
                    it = l * 3 + jj
                    for u in range(4):
                        cols = bass.ds(jj * 2048 + u * 512, 512)
                        apart(ae, m_dve.sem, m_dve.at(it, f"mod{u}"))
                        ae.dma_start(at1(modd, l)[:, cols], MO[u]).then_inc(m_out[u].sem, 16)
            for u in range(4):
                apart(ae, m_out[u].sem, m_out[u].at(DEPTH * 3 - 1, "out"))
            meet(ae, 0)
            ae.sem_inc(passed, 1)
            with ae.Fori(0, DEPTH) as l:
                def root(t):
                    link = linker(ae, n_act, t)
                    ae.wait_ge(n_dve.sem, n_dve.at(t, "mv"))
                    link("sd", a_.activation(SD, MV[:, 1:2], ACT.Sqrt, bias=eps))

                root(l * ROUNDS)
                link = linker(ae, pl_act, l)
                ae.wait_ge(p_par, (l + 1) * 96)
                link("ea", a_.activation(ALOG, ALOG, ACT.Exp))
                ae.sem_inc(passed, 1)
                with ae.Fori(0, TILES) as s:
                    it = l * TILES + s
                    link = linker(ae, p_act, it)
                    ae.wait_ge(p_pe.sem, p_pe.at(it, "A"))
                    ae.wait_ge(p_st.sem, p_st.at(it, "st", 1))
                    link("a1", a_.activation(FA[:, 0:P], ps[2][:, 0:P], ACT.Copy, scale=GDK ** -0.5))
                    link("a2", a_.activation(FA[:, P:4 * P], ps[2][:, P:4 * P], ACT.Copy))
                    ae.wait_ge(p_pe.sem, p_pe.at(it, "B"))
                    link("b1", a_.activation(CP[:, 0:2 * P], ps[3][:, 2 * P:4 * P], ACT.Copy))
                    link("b2", a_.activation(FA[:, 4 * P:6 * P], ps[3][:, 0:2 * P], ACT.Copy, scale=HD ** -0.5))
                    root(l * ROUNDS + 1 + s)
                    ae.wait_ge(p_dve.sem, p_dve.at(it, "za"))
                    link("ze", a_.activation(ZA, ZA, ACT.Exp, scale=-1.0))
                    link("ln", a_.activation(ZL, ZA, ACT.Ln, bias=ones[:, 0:1]))
                    ae.wait_ge(p_pe.sem, p_pe.at(it, "last"))
                    link("silug", a_.activation(GG[:, 0:256], ps[7][:, 0:256], ACT.Silu))
                    link("siluz", a_.activation(GG[:, 512:1024], ps[4][:, :], ACT.Silu))
                    link("sigmo", a_.activation(GG[:, 256:512], ps[7][:, 256:512], ACT.Sigmoid))
                meet(ae, l * PHASES + 1)

                ae.wait_ge(c_par, (l + 1) * 32)
                link = linker(ae, c_act, l)

                def tokens(c):
                    w = slice(c * P, c * P + P)
                    ae.wait_ge(c_pe.sem, c_pe.at(l, f"t{c}"))
                    link(f"four{c}", a_.activation(CTK[:, 1:, w], grp(ps[2 * (c % 4)][:, :], a=4), ACT.Copy), hold=False)
                    link(f"alone{c}", a_.activation(CTK[:, 0, w], ps[2 * (c % 4) + 1][:, 0:P], ACT.Copy), hold=False)

                for c in range(6):
                    ae.wait_ge(c_dve.sem, c_dve.at(l, f"c{c}"))
                    link(f"silu{c}", a_.activation(CO[:, c, :], CV[:, c, :], ACT.Silu, bias=CB_[:, c:c + 1]), hold=False)
                    if c:
                        tokens(c - 1)
                meet(ae, l * PHASES + 2)

                ae.sem_inc(passed, 1)
                with ae.Fori(0, TILES) as s:
                    it = l * TILES + s
                    links = [linker(ae, s_act[d], it) for d in (0, 1)]

                    def spread(d, halves=(1, 0)):
                        b, L = sc[d], links[d]
                        ae.wait_ge(s_pe[d].sem, s_pe[d].at(it, "cum"))
                        for q in halves:
                            for h in range(4 * q, 4 * q + 4):
                                L(f"rx{h}", a_.activation(b["EX"][:, h * P:(h + 1) * P],
                                                          ps[4 * d + 1 + q][:, h % 4 * P:(h % 4 + 1) * P],
                                                          ACT.Relu, bias=b["CS"][:, 132 + h:133 + h], scale=-1.0), hold=h % 4 == 3)
                            L(f"ex{q}", a_.activation(b["EX"][:, 512 * q:512 * q + 512],
                                                      b["EX"][:, 512 * q:512 * q + 512], ACT.Exp, scale=-1.0), hold=False)

                    def blocks(d):
                        b, L = sc[d], links[d]
                        ae.wait_ge(s_dve[d].sem, s_dve[d].at(it, "qba"))
                        L("kt", a_.activation(b["KT"], b["KT"], ACT.Exp, scale=-1.0), hold=False)
                        L("qb", a_.activation(b["QB"], b["QB"], ACT.Exp), hold=False)

                    for d in (0, 1):
                        b, L = sc[d], links[d]
                        cs = b["CS"]
                        ae.wait_ge(s_dve[d].sem, s_dve[d].at(it, "dec"))
                        L("ea", a_.activation(b["EA"], cs[:, 132:161], ACT.Exp), hold=False)
                        L("eb", a_.activation(b["EB"], cs[:, 0:P], ACT.Exp), hold=False)
                        L("kd", a_.activation(b["KD"], cs[:, 0:P], ACT.Exp, bias=cs[:, 152:153], scale=-1.0), hold=False)
                    spread(0)
                    blocks(0)
                    spread(1, (1,))
                    blocks(1)
                    spread(1, (0,))
                    for d in (0, 1):
                        b, L = sc[d], links[d]
                        ae.wait_ge(s_pe[d].sem, s_pe[d].at(it, "kdt"))
                        L("kmd", a_.activation(b["KMD"], ps[4 * d + 2][:, 0:3 * P], ACT.Copy), hold=False)
                        ae.wait_ge(s_dve[d].sem, s_dve[d].at(it, "em3"))
                        ae.wait_ge(s_pool[d].sem, s_pool[d].at(it, "snm", 1))
                        L("em", a_.activation(b["EM"], b["EMA"], ACT.Exp), hold=False)
                    for d in (0, 1):
                        b, L = sc[d], links[d]
                        ae.wait_ge(s_pe[d].sem, s_pe[d].at(it, "gb"))
                        for h in range(MH):
                            L(f"me{h}", a_.activation(b["ME"][:, h * P:(h + 1) * P], ps[4 * d][:, h * P:(h + 1) * P],
                                                      ACT.Relu, bias=b["NG"][:, h:h + 1]), hold=h == MH - 1)
                        L("me", a_.activation(b["ME"], b["ME"], ACT.Exp, scale=-1.0), hold=False)
                    for d in (0, 1):
                        b, L = sc[d], links[d]
                        ae.wait_ge(s_pe[d].sem, s_pe[d].at(it, "upg"))
                        ae.wait_ge(s_st[d].sem, s_st[d].at(it, "st", 1))
                        L("yg", a_.activation(b["Y"][:, 0:256], ps[4 * d][:, 0:256], ACT.Copy), hold=False)
                meet(ae, l * PHASES + 3)

                def mix(t):
                    link = linker(ae, o_act, t)
                    ae.wait_ge(o_dve.sem, o_dve.at(t, "hrm"))
                    link("hsd", a_.activation(HR3, HR2, ACT.Sqrt))
                    yield
                    ae.wait_ge(o_pe.sem, o_pe.at(t, "yt1"))
                    link("yt1", a_.activation(YT[:, 512:1024], ps[1][:, :], ACT.Copy))
                    yield
                    ae.wait_ge(o_dve.sem, o_dve.at(t, "mva"))
                    link("sda", a_.activation(oSD, oMV[:, 1:2], ACT.Sqrt, bias=eps))
                    yield
                    ae.wait_ge(o_dve.sem, o_dve.at(t, "mvb"))
                    link("sdb", a_.activation(oSD, oMV[:, 1:2], ACT.Sqrt, bias=eps))
                    yield

                def scores(t):
                    link = linker(ae, q_act, t)
                    ae.wait_ge(q_pe.sem, q_pe.at(t, "ut1"))
                    link("ut1", a_.activation(U2T[:, 512:1024], ps[1][:, :], ACT.Copy))
                    yield

                    def scored(b):
                        ae.wait_ge(q_pe.sem, q_pe.at(t, f"s{b}"))
                        link(f"sc{b}", a_.activation(SCO[:, 512 * b:512 * b + 512], ps[b][:, :], ACT.Copy))

                    scored(0)
                    scored(1)
                    ae.wait_ge(q_pe.sem, q_pe.at(t, "q7"))
                    link("qt1", a_.activation(QT[:, 512:1024], ps[3][:, :], ACT.Copy))
                    yield
                    scored(2)
                    scored(3)
                    yield
                    ae.wait_ge(q_dve.sem, q_dve.at(t, "sma"))
                    link("sme", a_.activation(IFR, JFR, ACT.Exp))

                def whole_round(t):
                    yield from mix(t)
                    yield from scores(t)

                for _ in whole_round(l * ROUNDS):
                    pass
                ae.sem_inc(passed, 1)
                with ae.Fori(0, TILES) as s:
                    it = l * TILES + s
                    link = linker(ae, e_act, it)
                    beside = whole_round(l * ROUNDS + 1 + s)

                    def gelu(g):
                        c = slice(GRP * g % 16, GRP * g % 16 + GRP)
                        ae.wait_ge(e_dve.sem, e_dve.at(it, f"dot{GRP * g + GRP - 1}"))
                        link(f"ge{g}", a_.activation(AG[:, c], DOT[:, c], ACT.Gelu))

                    def diag(g):
                        ae.wait_ge(e_dve.sem, e_dve.at(it, f"aw{g}"))
                        for n in range(GRP * g, GRP * g + GRP):
                            if n < DIAGS:
                                ae.wait_ge(e_pe.sem, e_pe.at(it, f"v{n + SLOTS - DIAGS}", 1))
                            else:
                                ae.wait_ge(e_pe.sem, e_pe.at(it, f"v{n - DIAGS}"))
                            link(f"dg{n}", a_.activation(DG[:, n % DIAGS * P:(n % DIAGS + 1) * P], ident, ACT.Copy,
                                                         scale=AW[:, n % 16:n % 16 + 1]), hold=n % 2 == 1)
                    gelu(0)
                    ae.wait_ge(e_st.sem, e_st.at(it, "st", 1))
                    ae.wait_ge(o_dve.sem, o_dve.at(l * ROUNDS + s, "u2c"))
                    link("ex", a_.activation(EX1, XO, ACT.Copy))
                    for g in range(1, SLOTS // GRP):
                        gelu(g)
                        diag(g - 1)
                        for _ in range(ACT_STEPS.get(GRP * g, 0)):
                            next(beside, None)
                    diag(SLOTS // GRP - 1)
                    ae.wait_ge(e_dve.sem, e_dve.at(it, "mv"))
                    link("sd", a_.activation(eSD, eMV[:, 1:2], ACT.Sqrt, bias=eps))
                meet(ae, l * PHASES + 4)

        @block.tensor
        def _(pe):
            give_credit(pe, pe_own)
            mm = nc.tensor.matmul

            pe.wait_ge(sem_silu, 1)
            pe.wait_ge(sem_ones, 2)
            pe.sem_inc(passed, 1)
            with pe.Fori(0, DEPTH) as l:
                pe.sem_inc(passed, 1)
                with pe.Fori(0, 3) as jj:
                    it = l * 3 + jj
                    mark = marker(m_pe)
                    for u in range(4):
                        pe.wait_ge(m_w[u].sem, m_w[u].at(it, "w"))
                        pe.wait_ge(m_dve.sem, m_dve.at(it, f"mod{u}", 1))
                        for k in range(KC):
                            i = mm(ps[u][0:2, :], CS2[:, 2 * k:2 * k + 2], WA[u][:, 512 * k:512 * k + 512],
                                   start=(k == 0), stop=(k == KC - 1))
                        mark(f"mod{u}", i)
            meet(pe, 0)

            def turn(bank, src, first):
                for c in range(4):
                    i = nc.tensor.transpose(bank[:, c * P:(c + 1) * P], src[:, (first + c) * P:(first + c + 1) * P], ident)
                return i

            pe.sem_inc(passed, 1)
            with pe.Fori(0, DEPTH) as l:
                def transposed(t):
                    mark = marker(n_pe)
                    pe.wait_ge(n_dve.sem, n_dve.at(t, "xsh"))
                    mark("tr0", turn(ps[0], U, 0))
                    mark("tr1", turn(ps[1], U, 4))

                transposed(l * ROUNDS)
                pe.sem_inc(passed, 1)
                with pe.Fori(0, TILES) as s:
                    it = l * TILES + s
                    mark = marker(p_pe)

                    def weights(q):
                        pe.wait_ge(p_w[q], (l + 1) * 16 * len(W_IN_PARTS[q]))
                    pe.wait_ge(p_dve.sem, p_dve.at(it, "ut1"))

                    def feature_major(bank, blocks):
                        for q, (c0, m) in enumerate(blocks):
                            for k in range(KC):
                                i = mm(bank[0:m, q * P:(q + 1) * P], win[:, k, c0:c0 + m], UT[:, k * P:(k + 1) * P],
                                       start=(k == 0), stop=(k == KC - 1))
                        return i

                    def token_major(out, c0, n):
                        for k in range(KC):
                            i = mm(out, UT[:, k * P:(k + 1) * P], win[:, k, c0:c0 + n], start=(k == 0), stop=(k == KC - 1))
                        return i

                    weights(0)
                    mark("A", feature_major(ps[2], [(O_GQ, P), (O_GK, P), (O_MQ, P), (O_MQ + P, P)]))
                    weights(1)
                    mark("B", feature_major(ps[3], [(O_MK, P), (O_MK + P, P), (O_SX, P), (O_SX + P, P)]))
                    pe.wait_ge(p_act.sem, p_act.at(it, "sigmo", 1))
                    mark("C", feature_major(ps[4], [(O_SX + 2 * P, P), (O_SX + 3 * P, P), (O_SB, P), (O_SB + P, P)]))
                    pe.wait_ge(p_dve.sem, p_dve.at(it, "dt", 1))
                    token_major(ps[5][:, 128:144], O_MI, 16)
                    token_major(ps[5][:, 144:160], O_SDT, 16)
                    mark("D", feature_major(ps[5], [(O_GA, 32)]))
                    weights(2)
                    mark("E1", token_major(ps[6][:, 0:256], O_GV, 256))
                    mark("E", token_major(ps[6][:, 256:512], O_MV, 256))
                    pe.wait_ge(p_dve.sem, p_dve.at(it, "gat"))
                    pe.wait_ge(p_par, (l + 1) * 96)
                    mark("gate", mm(ps[5][:, 160:416], GAT, WA2, start=True, stop=True))
                    token_major(ps[7][:, 0:256], O_GG, 256)
                    token_major(ps[7][:, 256:512], O_MO, 256)
                    transposed(l * ROUNDS + 1 + s)
                    weights(3)
                    pe.wait_ge(p_dve.sem, p_dve.at(it, "c4"))
                    mark("last", token_major(ps[4][:, :], O_SZ, 512))
                meet(pe, l * PHASES + 1)

                mark = marker(c_pe)
                for c in range(5):
                    pe.wait_ge(c_act.sem, c_act.at(l, f"silu{c}"))
                    if c >= 4:
                        pe.wait_ge(c_act.sem, c_act.at(l, f"alone{c - 4}"))
                    for q in range(4):
                        nc.tensor.transpose(ps[2 * (c % 4)][:, q * P:(q + 1) * P], CO[:, c, (2 + q) * P:(3 + q) * P], ident)
                    mark(f"t{c}", nc.tensor.transpose(ps[2 * (c % 4) + 1][:, 0:P], CO[:, c, 0:P], ident))
                meet(pe, l * PHASES + 2)

                pe.wait_ge(sem_tri, 64)
                pe.sem_inc(passed, 1)
                with pe.Fori(0, TILES) as s:
                    it = l * TILES + s
                    t = l * ROUNDS + s
                    marks = [marker(s_pe[d]) for d in (0, 1)]
                    i4 = ident[0:4, 0:4]
                    for d in (0, 1):
                        b, M = sc[d], marks[d]
                        la = b["TK"][:, 256 + VA:256 + VA + NDIR]
                        b0, b1, b2, b3 = ps[4 * d:4 * d + 4]
                        pe.wait_ge(s_la[d].sem, s_la[d].at(t, "la"))
                        pe.wait_ge(s_dve[d].sem, s_dve[d].at(it, "sng", 1))
                        pe.wait_ge(s_act[d].sem, s_act[d].at(it, "yg", 1))
                        mm(b0[:, 0:P], la[:, 0:P], TRI[d], start=True, stop=True)
                        mm(b0[:, 128:140], TRI[d], la[:, P:NDIR], start=True, stop=True)
                        mm(b0[:, 140:152], ones, la[:, P:NDIR], start=True, stop=True)
                        mm(b0[:, 152:153], la[:, 0:P], ones[:, 0:1], start=True, stop=True)
                        M("sum", mm(b0[0:4, 153:154], la[:, 128:132], ones[:, 0:1], start=True, stop=True))
                        for h in range(SH):
                            i = mm((b1, b2)[h // 4][:, h % 4 * P:(h % 4 + 1) * P],
                                   la[:, 132 + h:133 + h].broadcast_to([P, P]), TRI[d], start=True, stop=True)
                        M("cum", i)
                    for d in (0, 1):
                        b, M = sc[d], marks[d]
                        b0, b1, b2, b3 = ps[4 * d:4 * d + 4]
                        pe.wait_ge(s_qc[d].sem, s_qc[d].at(t, "qc"))
                        pe.wait_ge(s_dve[d].sem, s_dve[d].at(it, "g4"))
                        mm(b3[:, 0:256], b["FX"][:, 0:P], b["CTP"], start=True, stop=True)
                        M("g4r", mm(b0[0:4, 0:P], b["G4"], PERM[d], start=True, stop=True))
                    for d in (0, 1):
                        b, M = sc[d], marks[d]
                        b0, b1, b2, b3 = ps[4 * d:4 * d + 4]
                        pe.wait_ge(s_dve[d].sem, s_dve[d].at(it, "r4"))
                        mm(b0[:, 128:132], b["R4"], i4, start=True, stop=True)
                        mm(b0[:, 132:136], b["R4"][:, P - 1:P].broadcast_to([4, P]), i4, start=True, stop=True)
                        pe.wait_ge(s_ft[d].sem, s_ft[d].at(t, "ft"))
                        pe.wait_ge(s_act[d].sem, s_act[d].at(it, "ex1"))
                        nc.tensor.transpose(b2[:, 0:P], b["FT"][:, 4 * P:5 * P], ident)
                        M("km", nc.tensor.transpose(b2[:, P:2 * P], b["FT"][:, 5 * P:6 * P], ident))
                        for j in (0, 1):
                            i = mm(b3[:, 256 * j:256 * j + 256], b["FT"][:, (4 + j) * P:(5 + j) * P],
                                   b["QMP"][:, 256 * j:256 * j + 256], start=True, stop=True)
                        M("qk", i)
                    for d in (0, 1):
                        b, M = sc[d], marks[d]
                        b0, b1, b2, b3 = ps[4 * d:4 * d + 4]
                        pe.wait_ge(s_dve[d].sem, s_dve[d].at(it, "kdm"))
                        mm(b0[:, 136:140], PERM[d], b["GG8"][:, 0:4], start=True, stop=True)
                        M("kdt", nc.tensor.transpose(b2[:, 2 * P:3 * P], b["KD"], ident))
                    for d in (0, 1):
                        b, M = sc[d], marks[d]
                        b0, b1, b2, b3 = ps[4 * d:4 * d + 4]
                        pe.wait_ge(s_dve[d].sem, s_dve[d].at(it, "gt"))
                        for h in range(MH):
                            i = mm(b0[:, h * P:(h + 1) * P], b["GT"][:, h:h + 1].broadcast_to([P, P]), ident,
                                   start=True, stop=True)
                        M("gb", i)
                    for d in (0, 1):
                        b, M = sc[d], marks[d]
                        b0, b1, b2, b3 = ps[4 * d:4 * d + 4]
                        pe.wait_ge(s_dve[d].sem, s_dve[d].at(it, "w8"))
                        pe.wait_ge(s_pool[d].sem, s_pool[d].at(it, "xd"))
                        for h in range(SH):
                            mm(b1[:, h * HD:(h + 1) * HD], b["EX"][:, h * P:(h + 1) * P], b["XD"][:, h * HD:(h + 1) * HD],
                               start=True, stop=True)
                        pe.wait_ge(s_act[d].sem, s_act[d].at(it, "kmd"))
                        pe.wait_ge(s_ls[d].sem, s_ls[d].at(it, "ls"))
                        M("ssd", mm(b2[:, :], b["FX"][:, P:2 * P], b["ST"][:, S_SSD:S_ML], start=True, stop=True))
                    for d in (0, 1):
                        b, M = sc[d], marks[d]
                        b0, b1, b2, b3 = ps[4 * d:4 * d + 4]
                        pe.wait_ge(s_act[d].sem, s_act[d].at(it, "me3"))
                        for c in range(NB):
                            i = mm(b0[:, c * GH * BL:(c + 1) * GH * BL], b["KT"][:, c * P:(c + 1) * P],
                                   b["QP"][:, c * GH * BL:(c + 1) * GH * BL], start=True, stop=True)
                        M("att", i)
                        pe.wait_ge(s_pool[d].sem, s_pool[d].at(it, "xw"))
                        pe.wait_ge(s_dve[d].sem, s_dve[d].at(it, "qkm"))
                        M("ups", mm(b3[:, :], b["TX"][:, 512:640], b["XW"], start=True, stop=True))
                    for d in (0, 1):
                        b, M = sc[d], marks[d]
                        b0, b1, b2, b3 = ps[4 * d:4 * d + 4]
                        pe.wait_ge(s_dve[d].sem, s_dve[d].at(it, "ys1"))
                        pe.wait_ge(s_tv[d].sem, s_tv[d].at(t, "tv"))
                        va = b["TK"][:, 256:256 + VA]
                        for h in range(MH):
                            mm(b1[:, h * 65:h * 65 + 65], b["ME"][:, h * P:(h + 1) * P], va[:, h * 65:h * 65 + 65],
                               start=True, stop=True)
                        for j in (0, 1):
                            i = mm(b2[:, 130 * j:130 * j + 130], b["FT"][:, (2 + j) * P:(3 + j) * P],
                                   b["ST"][:, S_ML + 130 * j:S_ML + 130 * j + 130], start=True, stop=True)
                        M("mli", i)
                        pe.wait_ge(s_dve[d].sem, s_dve[d].at(it, "t1"))
                        mm(b0[:, 0:256], b["QH"], b["ST"][:, S_GLA:S_W], start=True, stop=False)
                        for h in range(GH):
                            mm(b0[:, h * HD:(h + 1) * HD], b["AT"][:, h * P:(h + 1) * P], b["TK"][:, h * HD:(h + 1) * HD],
                               start=False, stop=(h == GH - 1))
                        M("upg", mm(b0[:, 256:512], b["KMD"][:, 2 * P:3 * P], b["TK"][:, 0:256], start=True, stop=True))
                        pe.wait_ge(s_pool[d].sem, s_pool[d].at(it, "vw"))
                        for j in (0, 1):
                            i = mm(b3[:, 130 * j:130 * j + 130], b["KMD"][:, j * P:(j + 1) * P],
                                   b["VW"][:, 130 * j:130 * j + 130], start=True, stop=True)
                        M("upm", i)
                meet(pe, l * PHASES + 3)

                pe.wait_ge(e_w, (l + 1) * 32)
                pe.wait_ge(e_par, (l + 1) * 112)

                def mix(t):
                    mark = marker(o_pe)
                    pe.wait_ge(o_dve.sem, o_dve.at(t, "yn2"))
                    pe.wait_ge(q_act.sem, q_act.at(t, "sc3", 1))
                    mark("yt0", turn(ps[0], YF, 0))
                    mark("yt1", turn(ps[1], YF, 4))
                    yield
                    pe.wait_ge(o_dve.sem, o_dve.at(t, "yt0"))
                    pe.wait_ge(o_act.sem, o_act.at(t, "yt1"))
                    for h in (0, 1):
                        for k in range(KC):
                            i = mm(ps[2 + h][:, :], YT[:, k * P:(k + 1) * P], wo[:, k, 512 * h:512 * h + 512],
                                   start=(k == 0), stop=(k == KC - 1))
                            if k % 2 and (h, k) != (1, KC - 1):
                                yield
                    mark("out", i)
                    yield

                def scores(t):
                    mark = marker(q_pe)

                    def score(b):
                        for h in (2 * b, 2 * b + 1):
                            i = mm(ps[b][:, 256 * (h % 2):256 * (h % 2) + 256], QT[:, h * P:(h + 1) * P], KEYS,
                                   start=True, stop=True)
                        mark(f"s{b}", i)

                    pe.wait_ge(o_dve.sem, o_dve.at(t, "u2c"))
                    mark("ut0", turn(ps[0], SC2, 0))
                    mark("ut1", turn(ps[1], SC2, 4))
                    yield
                    pe.wait_ge(q_dve.sem, q_dve.at(t, "ut0"))
                    pe.wait_ge(q_act.sem, q_act.at(t, "ut1"))
                    for h in range(HEADS):
                        for k in range(KC):
                            i = mm(ps[2 + h // 4][:, h % 4 * P:(h % 4 + 1) * P], wq[:, k, h * P:(h + 1) * P],
                                   U2T[:, k * P:(k + 1) * P], start=(k == 0), stop=(k == KC - 1))
                        mark(f"q{h}", i)
                        if h == 5:
                            pe.wait_ge(q_dve.sem, q_dve.at(t, "qt0"))
                            score(0)
                            score(1)
                        yield
                    pe.wait_ge(q_act.sem, q_act.at(t, "qt1"))
                    score(2)
                    score(3)

                def whole_round(t):
                    yield from mix(t)
                    yield from scores(t)

                for _ in whole_round(l * ROUNDS):
                    pass
                pe.sem_inc(passed, 1)
                with pe.Fori(0, TILES) as s:
                    it = l * TILES + s
                    mark = marker(e_pe)
                    beside = whole_round(l * ROUNDS + 1 + s)
                    pe.wait_ge(e_dve.sem, e_dve.at(it, "r01", 1))
                    for n in range(SLOTS):
                        pe.wait_ge(e_act.sem, e_act.at(it, f"dg{n}"))
                        for h in (0, 1):
                            i = mm(ps[4 + h][:, :], DG[:, n % DIAGS * P:(n % DIAGS + 1) * P],
                                   ring[:, n % RING, D + 512 * h:D + 512 * h + 512], start=(n == 0), stop=(n == SLOTS - 1))
                        mark(f"v{n}", i)
                        if n in PE_STEPS:
                            next(beside, None)
                meet(pe, l * PHASES + 4)

        @block.gpsimd
        def _(ge):
            give_credit(ge, pool_own)
            g_ = nc.gpsimd

            meet(ge, 0)
            ge.sem_inc(passed, 1)
            with ge.Fori(0, DEPTH) as l:
                meet(ge, l * PHASES + 1)
                meet(ge, l * PHASES + 2)
                for d in (0, 1):
                    for t in ("CTP", "QMP", "QP"):
                        g_.memset(sc[d][t], 0.0).then_inc(s_pad, 1)
                apart(ge, s_pad, (l + 1) * 6)
                ge.sem_inc(passed, 1)
                with ge.Fori(0, TILES) as s:
                    it = l * TILES + s
                    t = l * ROUNDS + s
                    links = [linker(ge, s_pool[d], it, alone=True) for d in (0, 1)]
                    for d in (0, 1):
                        b, L = sc[d], links[d]
                        ge.wait_ge(s_la[d].sem, s_la[d].at(t, "la"))
                        ge.wait_ge(s_tx[d].sem, s_tx[d].at(t, "tx"))
                        ge.wait_ge(s_pe[d].sem, s_pe[d].at(it, "upm", 1))
                        L("xd", g_.tensor_tensor(grp(b["XD"], a=SH), grp(b["TX"][:, 0:512], a=SH),
                                                 b["TK"][:, 256 + VA + NDIR + 4:256 + VA + DB].unsqueeze(2)
                                                 .broadcast_to([P, SH, HD]), ALU.mult))
                    for d in (0, 1):
                        b, L = sc[d], links[d]
                        apart(ge, s_act[d].sem, s_act[d].at(it, "ea"))
                        L("xw", g_.tensor_tensor(grp(b["XW"], a=SH), grp(b["XD"], a=SH),
                                                 b["EA"][:, 21:29].unsqueeze(2).broadcast_to([P, SH, HD]), ALU.mult))
                    for d in (0, 1):
                        b, L = sc[d], links[d]
                        apart(ge, s_st[d].sem, s_st[d].at(it, "st", 1))
                        apart(ge, s_ls[d].sem, s_ls[d].at(it, "ls"))
                        sn, st = b["SN"], b["ST"]
                        L("sns", g_.tensor_tensor(grp(sn[:, 0:512], a=SH), grp(st[:, 0:512], a=SH),
                                                  b["EA"][:, 12:20].unsqueeze(2).broadcast_to([P, SH, HD]), ALU.mult))
                    for d in (0, 1):
                        b, L = sc[d], links[d]
                        sn, st = b["SN"], b["ST"]
                        apart(ge, s_tv[d].sem, s_tv[d].at(t, "tv"))
                        apart(ge, s_act[d].sem, s_act[d].at(it, "em"))
                        L("vw", g_.tensor_tensor(grp(b["VW"], a=MH), grp(b["TK"][:, 256:256 + VA], a=MH),
                                                 b["EM"][:, 8:12].unsqueeze(2).broadcast_to([P, MH, HD + 1]), ALU.mult))
                        L("snm", g_.tensor_tensor(grp(sn[:, S_ML:S_GLA], a=MH), grp(st[:, S_ML:S_GLA], a=MH),
                                                  b["EM"][:, 12:16].unsqueeze(2).broadcast_to([P, MH, HD + 1]), ALU.mult))
                    for d in (0, 1):
                        b, L = sc[d], links[d]
                        sn = b["SN"]
                        apart(ge, s_dve[d].sem, s_dve[d].at(it, "t1"))
                        L("sna1", g_.tensor_tensor(sn[:, 0:512], sn[:, 0:512], b["T1"], ALU.add))
                    for d in (0, 1):
                        b, L = sc[d], links[d]
                        sn = b["SN"]
                        apart(ge, s_dve[d].sem, s_dve[d].at(it, "t2"))
                        L("sna", g_.tensor_tensor(sn[:, S_ML:S_GLA], sn[:, S_ML:S_GLA], b["T2"], ALU.add))
                meet(ge, l * PHASES + 3)
                with ge.Fori(0, TILES) as s:
                    it = l * TILES + s
                    link = linker(ge, e_pool, it, alone=True)
                    half = SLOTS // 2
                    for u in (0, 1):
                        c = slice(u * half, (u + 1) * half)
                        if u == 0:
                            apart(ge, q_dve.sem, q_dve.at(l * ROUNDS + s, "ixb"))
                        apart(ge, e_dve.sem, e_dve.at(it, f"dot{(u + 1) * half - 1}", 1))
                        link(f"ix{u}", g_.tensor_copy(IDXC.bitcast(U32)[:, c], IDXN.bitcast(U32)[:, c]))
                        for n in range(u * half, (u + 1) * half):
                            if n < RING:
                                apart(ge, e_pe.sem, e_pe.at(it, f"v{n + SLOTS - RING}", 1))
                            else:
                                apart(ge, e_pe.sem, e_pe.at(it, f"v{n - RING}"))
                            g_.indirect_dma_start(ring[:, n % RING, :], None, io["experts"],
                                                  bass.IndirectOffsetOnAxis(ap=IDXC.bitcast(U32)[:, n:n + 1], axis=0)
                                                  ).then_inc(e_gat[n % RING].sem, 16)
                meet(ge, l * PHASES + 4)


W_IN_PARTS = (((O_GQ, O_GV), (O_MQ, O_MV)), ((O_MI, O_SZ), (O_SB, IN_W), (O_GG, O_MQ)),
              ((O_GV, O_GG), (O_MV, O_MI)), ((O_SZ, O_SB),))

SHAPES = {
    "ident": [P, P], "x_in": [NPOS, P, D], "pos_in": [NPOS, P, D], "c2t": [P, 2 * KC],
    "w_ada": [DEPTH, D, 6 * D], "b_ada": [DEPTH, 6 * D], "w_in": [DEPTH, D, IN_W],
    "gbias": [DEPTH, 2 * NDIR], "mlstm_bi": [DEPTH, 8], "ssd_a_log": [DEPTH, 16], "wa2": [DEPTH, 32, 256],
    "sgn": [2 * NDIR], "coef": [2 * NDIR], "conv_w": [DEPTH, P, 18], "conv_b": [DEPTH, P, 6],
    "tri": [2, P, P], "perm": [2, P, P], "gmask": [P, S_W], "w_out": [DEPTH, D, D], "peer_wq": [DEPTH, D, D],
    "keys": [DEPTH, P, 256], "gnorm_w": [DEPTH, D], "ln1_w": [DEPTH, D], "ln1_b": [DEPTH, D],
    "ln2_w": [DEPTH, D], "ln2_b": [DEPTH, D], "ssd_d": [DEPTH, SH], "iota": [TOPK], "lofs": [DEPTH, 1],
    "state0": [DEPTH, 2, 2, P, S_W], "m0": [DEPTH, 2, 2, MH], "zeros": [P, 6, P], "experts": [DEPTH * NE, 2 * D],
}


def program(nc, scratch="Internal"):
    io = {k: nc.dram_tensor("in_" + k, s, F32, kind="ExternalInput").ap() for k, s in SHAPES.items()}
    for k, s in (("xres", [NPOS, P, D]), ("state", [DEPTH, 2, 7, P, S_W]), ("mstate", [DEPTH, 2, 7, MH])):
        io[k] = nc.dram_tensor(k, s, F32, kind="ExternalOutput").ap()
    io["scratch"] = lambda name, shape, dt: nc.dram_tensor(name, shape, dt, kind=scratch).ap()
    build(nc, io)


def pos_rows():
    n = DEC_TILES * P
    f = np.float32
    r = np.repeat(np.arange(n // GRID_W, dtype=f), GRID_W)
    c = np.tile(np.arange(GRID_W, dtype=f), n // GRID_W)
    q = D // 4
    inv = f(1) / np.power(f(POS_BASE), np.arange(q, dtype=f) / f(q)).astype(f)
    ar, ac = r[:, None] * inv, c[:, None] * inv
    t = np.concatenate([np.sin(ar), np.cos(ar), np.sin(ac), np.cos(ac)], axis=-1).astype(f)
    out = np.zeros((NPOS, P, D), f)
    out[2:] = t.reshape(DEC_TILES, P, D)
    return out


def lay_out(i):
    f = np.float32
    a = {k: np.asarray(v) for k, v in i.items()}
    L = DEPTH
    x = np.zeros((NPOS, P, D), f)
    x[0] = a["x_prompt"][0]
    x[2:] = a["x_sample"][0].reshape(DEC_TILES, P, D)
    c2 = np.stack([a["c_ctx"], a["c"][0]])
    gb = np.concatenate([a["gla_ba"], a["mlstm_bf"], a["ssd_dt_bias"]], axis=2).reshape(L, 2 * NDIR)
    wa2 = np.zeros((L, 32, 256), f)
    keys = np.zeros((L, P, 256), f)
    for d in (0, 1):
        wa2[:, RANK * d:RANK * d + RANK, P * d:P * d + P] = a["gla_wa2"][:, d]
        keys[:, 64 * d:64 * d + 64, P * d:P * d + P] = a["peer_keys"][:, d].transpose(0, 2, 1)
    sgn = np.tile(np.concatenate([-np.ones(132, f), np.ones(8, f)]), 2)
    coef = np.tile(np.concatenate([np.full(128, -1.0 / 16.0, f), -np.ones(4, f), np.zeros(8, f)]), 2)
    up = np.triu(np.ones((P, P), f))
    eye = np.eye(P, dtype=f)
    st = np.zeros((L, 2, 2, P, S_W), f)
    mask = np.zeros((P, S_W), f)
    for h in range(SH):
        g = h // 4
        st[:, :, 1, HD * g:HD * g + HD, h * HD:(h + 1) * HD] = a["state_ssd"][0, :, :, h].transpose(0, 1, 3, 2)
        mask[HD * g:HD * g + HD, h * HD:(h + 1) * HD] = 1
    for h in range(MH):
        r, c = slice(HD * (h % 2), HD * (h % 2) + HD), S_ML + 65 * h
        st[:, :, 1, r, c:c + HD] = a["state_mlstm_c"][0, :, :, h].transpose(0, 1, 3, 2)
        st[:, :, 1, r, c + HD] = a["state_mlstm_n"][0, :, :, h]
        mask[r, c:c + 65] = 1
        r, c = slice(GDK * h, GDK * h + GDK), S_GLA + HD * h
        st[:, :, 1, r, c:c + HD] = a["state_gla"][0, :, :, h]
        mask[r, c:c + HD] = 1
    m0 = np.zeros((L, 2, 2, MH), f)
    m0[:, :, 1] = a["state_mlstm_m"][0]
    return {
        "ident": eye, "x_in": x, "pos_in": pos_rows(),
        "c2t": c2.reshape(2, KC, P).transpose(2, 1, 0).reshape(P, 2 * KC),
        "w_ada": a["w_ada"], "b_ada": a["b_ada"], "w_in": a["w_in"], "gbias": gb,
        "mlstm_bi": a["mlstm_bi"].reshape(L, 8), "ssd_a_log": a["ssd_a_log"].reshape(L, 16), "wa2": wa2,
        "sgn": sgn, "coef": coef,
        "conv_w": a["conv_w"].reshape(L, 3, 6, P).transpose(0, 3, 2, 1).reshape(L, P, 18),
        "conv_b": a["conv_b"].reshape(L, 6, P).transpose(0, 2, 1),
        "tri": np.stack([up, up.T]), "perm": np.stack([eye, eye[::-1]]), "gmask": mask,
        "w_out": a["w_out"], "peer_wq": a["peer_wq"], "keys": keys, "gnorm_w": a["gnorm_w"],
        "ln1_w": a["ln1_w"], "ln1_b": a["ln1_b"], "ln2_w": a["ln2_w"], "ln2_b": a["ln2_b"], "ssd_d": a["ssd_d"],
        "iota": np.arange(TOPK, dtype=f), "lofs": np.arange(L, dtype=f)[:, None] * f(NE),
        "state0": st, "m0": m0, "zeros": np.zeros((P, 6, P), f),
        "experts": np.concatenate([a["peer_u"], a["peer_v"]], axis=2).reshape(L * NE, 2 * D),
    }


def kernel(**inputs):
    import concourse.bacc as bacc
    from concourse.bass_utils import run_bass_kernel_spmd as run

    nc = bacc.Bacc("TRN2", target_bir_lowering=False, num_devices=1)
    program(nc)
    data = {"in_" + k: np.ascontiguousarray(v) for k, v in lay_out(inputs).items()}
    r = run(nc, [data], core_ids=[0]).results[0]
    x, m = r["xres"], r["mstate"]
    st = np.stack([r["state"][:, 0, 1], r["state"][:, 1, 0]], axis=1)
    gla = np.stack([st[:, :, GDK * h:GDK * h + GDK, S_GLA + HD * h:S_GLA + HD * h + HD] for h in range(GH)], axis=2)
    mc = np.stack([st[:, :, HD * (h % 2):HD * (h % 2) + HD, S_ML + 65 * h:S_ML + 65 * h + HD] for h in range(MH)], axis=2)
    mn = np.stack([st[:, :, HD * (h % 2):HD * (h % 2) + HD, S_ML + 65 * h + HD] for h in range(MH)], axis=2)
    ssd = np.stack([st[:, :, HD * (h // 4):HD * (h // 4) + HD, h * HD:h * HD + HD] for h in range(SH)], axis=2)
    mm = np.stack([m[:, 0, 1], m[:, 1, 0]], axis=1)
    return (x[0:1], x[2:].reshape(1, DEC_TILES * P, D), gla[None], mc.transpose(0, 1, 2, 4, 3)[None], mn[None],
            mm[None], ssd.transpose(0, 1, 2, 4, 3)[None])
```
